# Optimizing a Trainium2 kernel written in Bass

```python
import math
import jax, jax.numpy as jnp
from jax import lax
import numpy as np

D_MODEL = 1024
BATCH = 1
SEQ = 1024
DEPTH = 2

POOL_WINDOWS = (2, 4, 8, 16)
N_POOL_GROUPS = 4
POOL_GROUP = D_MODEL // N_POOL_GROUPS
HEAD_DIM = 64
N_HEADS = D_MODEL // HEAD_DIM
N_KV_HEADS = 4
GROUP_SIZE = N_HEADS // N_KV_HEADS
N_BRANCH = 3
CMP_LEN = 32
CMP_STRIDE = 16
CMP_HIDDEN = 4 * HEAD_DIM
SLC_LEN = 64
N_SEL = 4
WINDOW = 256
Q_BLOCK = 128
FORCED_SCORE = 1.0e4
N_BUCKETS = 32
MAX_DISTANCE = 128
D_FF = (7 * D_MODEL) // 2
N_EXPERTS = 8
TOP_K = 2
EPS = 1e-6
NEG = -1e30
TINY = 1e-30

kernel_name = "yoco_pool_nsa_moe_hybrid"

def rmsnorm(x, g):
    xf = x.astype(jnp.float32)
    y = xf * lax.rsqrt(jnp.mean(xf * xf, axis=-1, keepdims=True) + EPS)
    return (y * g.astype(jnp.float32)).astype(x.dtype)

def masked_softmax(s, mask):
    s = jnp.where(mask, s, NEG)
    m = jnp.max(s, axis=-1, keepdims=True)
    p = jnp.where(mask, jnp.exp(s - m), 0.0)
    return p / jnp.maximum(jnp.sum(p, axis=-1, keepdims=True), TINY)

def rel_bucket(dist):
    n = jnp.maximum(dist, 0)
    max_exact = N_BUCKETS // 2
    nf = jnp.maximum(n, 1).astype(jnp.float32)
    large = max_exact + (jnp.log(nf / max_exact) / math.log(MAX_DISTANCE / max_exact)
                         * (N_BUCKETS - max_exact)).astype(jnp.int32)
    large = jnp.minimum(large, N_BUCKETS - 1)
    return jnp.where(n < max_exact, n, large)

def pool_mixer(h, w_grp, scale):
    B, S, D = h.shape
    hg = h.reshape(B, S, N_POOL_GROUPS, POOL_GROUP)
    csum = jnp.cumsum(hg.astype(jnp.float32), axis=1)
    t = jnp.arange(S)
    pooled = []
    for gi, w in enumerate(POOL_WINDOWS):
        c = csum[:, :, gi]
        prev = jnp.pad(c, ((0, 0), (w, 0), (0, 0)))[:, :S]
        cnt = jnp.minimum(t + 1, w).astype(jnp.float32)[None, :, None]
        pooled.append((c - prev) / cnt)
    pooled = jnp.stack(pooled, axis=2)
    diff = (pooled - hg.astype(jnp.float32)).astype(h.dtype)
    y = jnp.einsum('bsgc,gcd->bsgd', diff, w_grp).reshape(B, S, D)
    return y * scale

def swiglu(h, wg, wu, wd):
    return (jax.nn.silu(h @ wg) * (h @ wu)) @ wd

def moe(h, router, wg, wu, wd):
    B, S, D = h.shape
    xf = h.reshape(-1, D)
    logits = jnp.einsum('nd,de->ne', xf, router, preferred_element_type=jnp.float32)
    top_val, top_idx = lax.top_k(logits, TOP_K)
    gate = jax.nn.softmax(top_val, axis=-1)
    flat_e = top_idx.reshape(-1)
    order = jnp.argsort(flat_e)
    tok = order // TOP_K
    sizes = jnp.bincount(flat_e, length=N_EXPERTS).astype(jnp.int32)
    xs = xf[tok]
    hid = jax.nn.silu(lax.ragged_dot(xs, wg, sizes)) * lax.ragged_dot(xs, wu, sizes)
    ys = lax.ragged_dot(hid, wd, sizes) * gate.reshape(-1)[order][:, None].astype(h.dtype)
    return jnp.zeros_like(xf).at[tok].add(ys).reshape(B, S, D)

def build_shared_kv(x, norm_kv, w_kv, g_k, cmp_pos, cmp_w1, cmp_w2):
    B, S, _ = x.shape
    y = rmsnorm(x, norm_kv)
    kv = (y @ w_kv).reshape(B, S, 2 * N_BRANCH, N_KV_HEADS, HEAD_DIM)
    k_c, v_c, k_s, v_s, k_w, v_w = [kv[:, :, i] for i in range(2 * N_BRANCH)]
    nc = (S - CMP_LEN) // CMP_STRIDE + 1
    idx = np.arange(nc)[:, None] * CMP_STRIDE + np.arange(CMP_LEN)[None, :]

    def compress(z, pos, w1, w2):
        blocks = z[:, idx] + pos[None, None, :, None, :]
        blocks = blocks.transpose(0, 1, 3, 2, 4).reshape(B, nc, N_KV_HEADS, CMP_LEN * HEAD_DIM)
        return jax.nn.silu(blocks @ w1) @ w2

    k_cmp = rmsnorm(compress(k_c, cmp_pos[0], cmp_w1[0], cmp_w2[0]), g_k[0])
    v_cmp = compress(v_c, cmp_pos[1], cmp_w1[1], cmp_w2[1])
    nsb = S // SLC_LEN

    def to_blocks(z):
        return (z.reshape(B, nsb, SLC_LEN, N_KV_HEADS, HEAD_DIM)
                 .transpose(0, 3, 1, 2, 4).reshape(B, N_KV_HEADS, nsb, SLC_LEN * HEAD_DIM))

    k_slc = to_blocks(rmsnorm(k_s, g_k[1]))
    v_slc = to_blocks(v_s)
    pad = ((0, 0), (WINDOW, 0), (0, 0), (0, 0))
    k_win = jnp.pad(rmsnorm(k_w, g_k[2]), pad)
    v_win = jnp.pad(v_w, pad)
    return (k_cmp, v_cmp, k_slc, v_slc, k_win, v_win)

def nsa_mixer(h, w_qg, g_q, w_o, rel_bias, k_cmp, v_cmp, k_slc, v_slc, k_win, v_win):
    B, S, _ = h.shape
    HD = N_HEADS * HEAD_DIM
    G, R, DH = N_KV_HEADS, GROUP_SIZE, HEAD_DIM
    qg = h @ w_qg
    q = rmsnorm(qg[..., :HD].reshape(B, S, G, R, DH), g_q) * (DH ** -0.5)
    gates = jax.nn.sigmoid(qg[..., HD:].astype(jnp.float32)).reshape(B, S, G, R, N_BRANCH).astype(h.dtype)
    nc = k_cmp.shape[1]
    nsb = S // SLC_LEN
    n_sel = min(N_SEL, nsb)
    cmp_start = np.arange(nc) * CMP_STRIDE
    cmp_end = jnp.asarray(cmp_start + CMP_LEN - 1, dtype=jnp.int32)
    slc_start = np.arange(nsb) * SLC_LEN
    overlap = np.clip(np.minimum(cmp_start[:, None] + CMP_LEN, slc_start[None, :] + SLC_LEN)
                      - np.maximum(cmp_start[:, None], slc_start[None, :]), 0, None) / CMP_LEN
    cmp_to_slc = jnp.asarray(overlap, dtype=jnp.float32)
    bias_tab = rel_bias.astype(jnp.float32).reshape(N_BUCKETS, G, R)
    bias_tab_g = bias_tab.transpose(1, 0, 2)
    g_idx = jnp.arange(G)
    jb = jnp.arange(nsb)

    def block(qb):
        t0 = qb * Q_BLOCK
        tq = t0 + jnp.arange(Q_BLOCK)
        qblk = lax.dynamic_slice_in_dim(q, t0, Q_BLOCK, axis=1)
        gblk = lax.dynamic_slice_in_dim(gates, t0, Q_BLOCK, axis=1)
        dc = tq[:, None] - cmp_end[None, :]
        s = jnp.einsum('bqgrd,bcgd->bgrqc', qblk, k_cmp, preferred_element_type=jnp.float32)
        s = s + bias_tab[rel_bucket(dc)].transpose(2, 3, 0, 1)
        p_cmp = masked_softmax(s, dc >= 0)
        o_cmp = jnp.einsum('bgrqc,bcgd->bqgrd', p_cmp.astype(v_cmp.dtype), v_cmp)
        imp = jnp.einsum('bgrqc,cj->bqgj', p_cmp, cmp_to_slc)
        blk_q = tq // SLC_LEN
        valid = jb[None, :] <= blk_q[:, None]
        forced = (jb[None, :] == 0) | (jb[None, :] == blk_q[:, None]) | (jb[None, :] == blk_q[:, None] - 1)
        score = jnp.where(forced[None, :, None, :], FORCED_SCORE,
                          jnp.where(valid[None, :, None, :], imp, NEG))
        _, sel = lax.top_k(score, n_sel)
        sel_t = sel.transpose(0, 2, 1, 3)
        flat = sel_t.reshape(B, G, Q_BLOCK * n_sel)[..., None]
        ks = jnp.take_along_axis(k_slc, flat, axis=2).reshape(B, G, Q_BLOCK, n_sel, SLC_LEN, DH)
        vs = jnp.take_along_axis(v_slc, flat, axis=2).reshape(B, G, Q_BLOCK, n_sel, SLC_LEN, DH)
        pos = sel_t[..., None] * SLC_LEN + jnp.arange(SLC_LEN)
        ds = tq[None, None, :, None, None] - pos
        bias_s = bias_tab_g[g_idx[None, :, None, None, None], rel_bucket(ds)]
        s = jnp.einsum('bqgrd,bgqnld->bgrqnl', qblk, ks, preferred_element_type=jnp.float32)
        s = (s + bias_s.transpose(0, 1, 5, 2, 3, 4)).reshape(B, G, R, Q_BLOCK, n_sel * SLC_LEN)
        mask_s = (ds >= 0).reshape(B, G, 1, Q_BLOCK, n_sel * SLC_LEN)
        p = masked_softmax(s, mask_s).reshape(B, G, R, Q_BLOCK, n_sel, SLC_LEN)
        o_slc = jnp.einsum('bgrqnl,bgqnld->bqgrd', p.astype(vs.dtype), vs)
        kw = lax.dynamic_slice_in_dim(k_win, t0, Q_BLOCK + WINDOW, axis=1)
        vw = lax.dynamic_slice_in_dim(v_win, t0, Q_BLOCK + WINDOW, axis=1)
        kpos = t0 - WINDOW + jnp.arange(Q_BLOCK + WINDOW)
        dw = tq[:, None] - kpos[None, :]
        mw = (dw >= 0) & (dw < WINDOW) & (kpos[None, :] >= 0)
        s = jnp.einsum('bqgrd,bkgd->bgrqk', qblk, kw, preferred_element_type=jnp.float32)
        s = s + bias_tab[rel_bucket(dw)].transpose(2, 3, 0, 1)
        p = masked_softmax(s, mw)
        o_win = jnp.einsum('bgrqk,bkgd->bqgrd', p.astype(vw.dtype), vw)
        return gblk[..., 0:1] * o_cmp + gblk[..., 1:2] * o_slc + gblk[..., 2:3] * o_win

    out = lax.map(block, jnp.arange(S // Q_BLOCK))
    out = out.transpose(1, 0, 2, 3, 4, 5).reshape(B, S, HD)
    return out @ w_o

def setup_inputs(seed: int = 0) -> dict:
    key = jax.random.key(seed)
    ks = iter(jax.random.split(key, 32))
    f32 = jnp.float32

    def nrm(shape, fan_in):
        return jax.random.normal(next(ks), shape, f32) * (fan_in ** -0.5)

    def gain(shape):
        return 1.0 + 0.05 * jax.random.normal(next(ks), shape, f32)

    n_a = DEPTH // 2
    n_b = DEPTH - n_a
    n_dense = (DEPTH + 1) // 2
    n_moe = DEPTH // 2
    HD = N_HEADS * HEAD_DIM
    return {
        "x": jax.random.normal(next(ks), (BATCH, SEQ, D_MODEL), f32),
        "rel_bias": 0.5 * jax.random.normal(next(ks), (N_BUCKETS, N_HEADS), f32),
        "norm_mix": gain((DEPTH, D_MODEL)),
        "norm_ffn": gain((DEPTH, D_MODEL)),
        "pool_w": nrm((n_a, N_POOL_GROUPS, POOL_GROUP, POOL_GROUP), POOL_GROUP),
        "pool_scale": gain((n_a, D_MODEL)),
        "norm_kv": gain((D_MODEL,)),
        "w_kv": nrm((D_MODEL, 2 * N_BRANCH * N_KV_HEADS * HEAD_DIM), D_MODEL),
        "g_k": gain((N_BRANCH, HEAD_DIM)),
        "cmp_pos": 0.1 * jax.random.normal(next(ks), (2, CMP_LEN, HEAD_DIM), f32),
        "cmp_w1": nrm((2, CMP_LEN * HEAD_DIM, CMP_HIDDEN), CMP_LEN * HEAD_DIM),
        "cmp_w2": nrm((2, CMP_HIDDEN, HEAD_DIM), CMP_HIDDEN),
        "w_qg": nrm((n_b, D_MODEL, HD + N_BRANCH * N_HEADS), D_MODEL),
        "g_q": gain((n_b, HEAD_DIM)),
        "w_o": nrm((n_b, HD, D_MODEL), HD),
        "ffn_wg": nrm((n_dense, D_MODEL, D_FF), D_MODEL),
        "ffn_wu": nrm((n_dense, D_MODEL, D_FF), D_MODEL),
        "ffn_wd": nrm((n_dense, D_FF, D_MODEL), D_FF),
        "router": nrm((n_moe, D_MODEL, N_EXPERTS), D_MODEL),
        "moe_wg": nrm((n_moe, N_EXPERTS, D_MODEL, D_FF), D_MODEL),
        "moe_wu": nrm((n_moe, N_EXPERTS, D_MODEL, D_FF), D_MODEL),
        "moe_wd": nrm((n_moe, N_EXPERTS, D_FF, D_MODEL), D_FF),
    }

def reference(x, rel_bias, norm_mix, norm_ffn, pool_w, pool_scale, norm_kv, w_kv, g_k,
              cmp_pos, cmp_w1, cmp_w2, w_qg, g_q, w_o, ffn_wg, ffn_wu, ffn_wd,
              router, moe_wg, moe_wu, moe_wd):
    n_a = DEPTH // 2
    shared = None
    for layer in range(DEPTH):
        h = rmsnorm(x, norm_mix[layer])
        if layer < n_a:
            x = x + pool_mixer(h, pool_w[layer], pool_scale[layer])
        else:
            j = layer - n_a
            x = x + nsa_mixer(h, w_qg[j], g_q[j], w_o[j], rel_bias, *shared)
        h = rmsnorm(x, norm_ffn[layer])
        i = layer // 2
        if layer % 2 == 0:
            x = x + swiglu(h, ffn_wg[i], ffn_wu[i], ffn_wd[i])
        else:
            x = x + moe(h, router[i], moe_wg[i], moe_wu[i], moe_wd[i])
        if layer == n_a - 1:
            shared = build_shared_kv(x, norm_kv, w_kv, g_k, cmp_pos, cmp_w1, cmp_w2)
    return x


_drawn_inputs = setup_inputs


def setup_inputs(seed=0):
    import zlib

    import numpy as np

    out = dict(_drawn_inputs(seed))
    spreads = {}
    factors = {'norm_kv': 2.702, 'g_k': 4.384, 'g_q': 4.023}
    for name, (base, spread) in spreads.items():
        noise = np.random.default_rng([zlib.crc32(name.encode()), seed]).standard_normal(out[name].shape)
        drawn = base * np.exp(spread * noise) if base else spread * noise
        out[name] = __import__('jax').numpy.asarray(drawn.astype(out[name].dtype))
    for name, factor in factors.items():
        out[name] = (out[name] * factor).astype(out[name].dtype)
    return out
```

```python
import concourse.bass as bass
from concourse import mybir
from contextlib import ExitStack, contextmanager

F32, F32R, I32, U32 = mybir.dt.float32, mybir.dt.float32r, mybir.dt.int32, mybir.dt.uint32
ALU, ACT, AX = mybir.AluOpType, mybir.ActivationFunctionType, mybir.AxisListType

SEQ, TILES, EPS = 1024, 8, 1e-6
N_GRP, GRP = 4, 256
N_EXP = 8
N_HEADS, N_KV, DH = 16, 4, 64
N_BUCKETS = 32
NEG, LOWEST = -1e30, -3.0e38
NEAR, CB = 384, 120
VEC = NEAR + 16 * 128
MAX_JOBS, JOB_COUNT_AT = 12, 56
ROUTE_AT, ROUTE_CONSTS = {}, 0
for _name, _len in (("down", N_EXP), ("starts", TILES), ("prior", 4 * N_EXP * N_EXP), ("record", MAX_JOBS + 1),
                    ("expert", 2 * N_EXP), ("skip", 2 * N_EXP)):
    ROUTE_AT[_name] = (ROUTE_CONSTS, _len)
    ROUTE_CONSTS += _len


@contextmanager
def phase_semaphores(nc):
    taken = []

    def new(name):
        taken.append(nc.alloc_semaphore(name))
        return taken[-1]
    yield new
    nc.clear_and_free_semaphores(taken)
    nc.all_engine_barrier()


P = 128
D = 1024
KT = D // P
FF = 3584
MT = FF // P
GROUP = 2
NG = MT // GROUP
CAP = 4
SLOT_TILES = 32
E_REC = 4


def swiglu_jobs(nc, name, wgu, wd, jobs, n_jobs, gather, y_rows, ident, widths):
    with ExitStack() as ctx:
        new_semaphore = ctx.enter_context(phase_semaphores(nc))
        def sb(n, shape, dt=F32):
            return ctx.enter_context(nc.sbuf_tensor(f"{name}_{n}", shape, dt))

        def sem(n):
            return new_semaphore(f"{name}_{n}")

        stage = sb("stage", [P, CAP, D])
        ids = sb("ids", [P, CAP], mybir.dt.uint32)
        gu_raw = [sb(f"gu_raw{s}", [P, 2 * D]) for s in range(2)]
        gu_hi = [sb(f"gu_hi{s}", [P, 2, KT, P], F32R) for s in range(2)]
        gu_lo = [sb(f"gu_lo{s}", [P, 2, KT, P], F32R) for s in range(2)]
        wd_raw = sb("wd_raw", [P, GROUP, D])
        wd_hi = [sb(f"wd_hi{s}", [P, GROUP, D], F32R) for s in range(2)]
        wd_lo = [sb(f"wd_lo{s}", [P, GROUP, D], F32R) for s in range(2)]
        act_gate = [sb(f"act_gate{s}", [P, CAP * P]) for s in range(2)]
        hid = [sb(f"hid{s}", [P, CAP * P]) for s in range(2)]
        hid_hi = [sb(f"hid_hi{s}", [P, GROUP, CAP * P], F32R) for s in range(2)]
        hid_lo = [sb(f"hid_lo{s}", [P, GROUP, CAP * P], F32R) for s in range(2)]
        ht_hi = sb("ht_hi", [P, KT, CAP * P], F32R)
        ht_lo = sb("ht_lo", [P, KT, CAP * P], F32R)
        yacc = sb("yacc", [P, CAP, D])
        ps = [ctx.enter_context(nc.psum_tensor(f"{name}_ps{b}", [P, 512], F32)) for b in range(8)]
        gate_ps, up_ps, y_ps = ps[0:4:2], ps[1:4:2], ps[4:8]

        s_gu_loaded = [sem(f"gu_loaded{s}") for s in range(2)]
        s_wd_loaded = sem("wd_loaded")
        s_gu_hi, s_gu_lo = sem("gu_hi_done"), sem("gu_lo_done")
        s_wd_hi, s_wd_lo = sem("wd_hi_done"), sem("wd_lo_done")
        s_gate, s_gu = sem("gate_done"), sem("gu_done")
        s_silu, s_hid, s_hhi, s_hlo = sem("silu_done"), sem("hid_done"), sem("hid_hi_done"), sem("hid_lo_done")
        s_yready, s_yadded = sem("y_ready"), sem("y_added")
        s_zeroed, s_stored, s_store_seen = sem("yacc_zeroed"), sem("y_stored"), sem("store_seen")
        s_ids, s_rows = sem("ids_loaded"), sem("rows_loaded")
        s_tr, s_tr_hi, s_tr_lo = sem("tr_done"), sem("tr_hi_done"), sem("tr_lo_done")

        block = ctx.enter_context(nc.Block())

        def job_count(eng):
            return n_jobs if isinstance(n_jobs, int) else eng.value_load(n_jobs, min_val=2, max_val=12)

        def field(eng, j, f, lo, hi):
            return eng.value_load(jobs[0:1, bass.ds(j * E_REC + f, 1)], min_val=lo, max_val=hi)

        def per_width(eng, j, body):
            if len(widths) == 1:
                body(widths[0])
                return
            tiles = field(eng, j, 2, 2, CAP)
            with eng.If(tiles == 2):
                body(2)
            with eng.Else():
                with eng.If(tiles == 3):
                    body(3)
                with eng.Else():
                    body(4)
                eng.nop()
            eng.nop()

        @block.sync
        def _(sp):
            with sp.Fori(0, job_count(sp)) as j:
                ws = field(sp, j, 0, 0, wd.shape[0] // FF - 1)
                with sp.Fori(0, NG // 2) as it:
                    for g in range(2):
                        for s in range(2):
                            n = it * 4 + (2 * g + s)
                            sp.wait_ge(s_gu_lo, j * MT + n + 1)
                            sp.dma_start(gu_raw[s][:, :], wgu[bass.ds((ws * MT + n) * P, P), :]).then_inc(
                                s_gu_loaded[s], 16)
                        q = it * 2 + g
                        sp.wait_ge(s_wd_lo, j * NG + q + 1)
                        src = wd[bass.ds((ws * NG + q) * GROUP * P, GROUP * P), :]
                        sp.dma_start(wd_raw[:, :, :], src.rearrange("(a p) d -> p a d", p=P)).then_inc(
                            s_wd_loaded, 16)

        @block.gpsimd
        def _(pool):
            pool.memset(yacc[:, :, :], 0.0).then_inc(s_zeroed, 1)

            def fetch(j):
                base = field(pool, j, 1, 0, y_rows.shape[1] - CAP)
                gather(pool, j, base, stage, ids, s_ids, s_rows)

            fetch(0)
            with pool.Fori(0, job_count(pool)) as j:
                pool.wait_ge(s_tr, j * KT + KT)
                fetch(j + 1)
                base = field(pool, j, 1, 0, y_rows.shape[1] - CAP)
                pool.wait_ge(s_yadded, j * 24 * NG + (24 + 24 * NG))

                def store(tiles):
                    pool.dma_start(y_rows[:, bass.ds(base, tiles), :], yacc[:, 0:tiles, :]).then_inc(s_stored, 16)
                per_width(pool, j, store)
                pool.wait_ge(s_stored, j * 16 + 16)
                pool.sem_inc(s_store_seen, 1)
                pool.memset(yacc[:, :, :], 0.0).then_inc(s_zeroed, 1)

        @block.scalar
        def _(act):
            def tr_hi(j1):
                for k in range(KT):
                    act.wait_ge(s_tr, j1 * KT + (k + 1))
                    act.copy(ht_hi[:, k, :], ps[k % 4][:, :]).then_inc(s_tr_hi, 1)

            tr_hi(0)
            with act.Fori(0, job_count(act)) as j:
                def job(tiles):
                    W = tiles * P

                    def silu(N, s):
                        act.wait_ge(s_gate, N + 1)
                        act.wait_ge(s_hid, N + 1)
                        act.activation(act_gate[s][:, 0:W], gate_ps[s][:, 0:W], ACT.Silu).then_inc(s_silu, 1)

                    def split(n, s):
                        N = j * MT + n
                        act.wait_ge(s_gu_loaded[s], j * (8 * MT) + (n - s) * 8 + 16)
                        act.wait_ge(s_gu, N + 1)
                        act.copy(gu_hi[s][:, :, :, :].rearrange("p a k c -> p (a k c)"), gu_raw[s][:, :]).then_inc(s_gu_hi, 1)

                    def hidhi(N, Q, s, b):
                        act.wait_ge(s_hid, N + 3)
                        act.wait_ge(s_yready, Q * 24 + 24)
                        act.copy(hid_hi[b][:, s, 0:W], hid[s][:, 0:W]).then_inc(s_hhi, 1)

                    def wdhi(q, b):
                        Q = j * NG + q
                        act.wait_ge(s_wd_loaded, Q * 16 + 16)
                        act.wait_ge(s_yready, Q * 24 + 24)
                        act.copy(wd_hi[b][:, :, :], wd_raw[:, :, :]).then_inc(s_wd_hi, 1)

                    def post_and_split(m, q, s, b, more=None):
                        silu(j * MT + m, s)
                        if more is not None:
                            split(more, s)
                        hidhi(j * MT + m, j * NG + q, s, b)

                    split(0, 0)
                    split(1, 1)
                    post_and_split(0, 0, 0, 0, 2)
                    wdhi(0, 0)
                    post_and_split(1, 0, 1, 0, 3)
                    with act.Fori(0, NG // 2 - 1) as it:
                        m = it * 4
                        post_and_split(m + 2, it * 2 + 1, 0, 1, m + 4)
                        wdhi(it * 2 + 1, 1)
                        post_and_split(m + 3, it * 2 + 1, 1, 1, m + 5)
                        post_and_split(m + 4, it * 2 + 2, 0, 0, m + 6)
                        wdhi(it * 2 + 2, 0)
                        post_and_split(m + 5, it * 2 + 2, 1, 0, m + 7)
                    post_and_split(MT - 2, NG - 1, 0, 1)
                    wdhi(NG - 1, 1)
                    post_and_split(MT - 1, NG - 1, 1, 1)
                per_width(act, j, job)
                tr_hi(j + 1)

        @block.vector
        def _(dve):
            dve.sem_inc(s_hid, 2)
            dve.sem_inc(s_yadded, 24)
            dve.sem_inc(s_gu_lo, 2)
            dve.sem_inc(s_wd_lo, 1)

            def tr_lo(j1):
                for k in range(KT):
                    dve.wait_ge(s_tr_hi, j1 * KT + (k + 1))
                    dve.tensor_tensor(ht_lo[:, k, :], ps[k % 4][:, :], ht_hi[:, k, :], ALU.subtract).then_inc(s_tr_lo, 1)

            tr_lo(0)
            with dve.Fori(0, job_count(dve)) as j:
                def job(tiles):
                    W = tiles * P
                    unit = 12 // tiles

                    def product(N, s):
                        dve.wait_ge(s_silu, N + 1)
                        dve.wait_ge(s_gu, N + 3)
                        dve.tensor_tensor(hid[s][:, 0:W], act_gate[s][:, 0:W], up_ps[s][:, 0:W], ALU.mult).then_inc(s_hid, 1)

                    def split(n, s):
                        dve.wait_ge(s_gu_hi, j * MT + n + 1)
                        dve.tensor_tensor(gu_lo[s][:, :, :, :].rearrange("p a k c -> p (a k c)"), gu_raw[s][:, :],
                                          gu_hi[s][:, :, :, :].rearrange("p a k c -> p (a k c)"),
                                          ALU.subtract).then_inc(s_gu_lo, 1)

                    def hidlo(N, s, b):
                        dve.wait_ge(s_hhi, N + 1)
                        dve.tensor_tensor(hid_lo[b][:, s, 0:W], hid[s][:, 0:W], hid_hi[b][:, s, 0:W], ALU.subtract).then_inc(s_hlo, 1)

                    def wdlo(q, b):
                        dve.wait_ge(s_wd_hi, j * NG + q + 1)
                        dve.tensor_tensor(wd_lo[b][:, :, :], wd_raw[:, :, :], wd_hi[b][:, :, :], ALU.subtract).then_inc(s_wd_lo, 1)

                    def add_y(q):
                        for u in range(2 * tiles):
                            t, h = u // 2, u % 2
                            dve.wait_ge(s_yready, (j * NG + q) * 24 + (48 + unit * (u + 1)))
                            dve.wait_ge(s_yadded, (j * NG + q) * 24 + unit * (u + 1))
                            dve.tensor_tensor(yacc[:, t, h * 512:(h + 1) * 512], yacc[:, t, h * 512:(h + 1) * 512],
                                              y_ps[u % 4][:, :], ALU.add).then_inc(s_yadded, unit)

                    def post_and_split(m, s, b, more=None):
                        product(j * MT + m, s)
                        if more is not None:
                            split(more, s)
                        hidlo(j * MT + m, s, b)

                    split(0, 0)
                    split(1, 1)
                    post_and_split(0, 0, 0, 2)
                    wdlo(0, 0)
                    dve.wait_ge(s_zeroed, j + 1)
                    post_and_split(1, 1, 0, 3)
                    with dve.Fori(0, NG // 2 - 1) as it:
                        m = it * 4
                        post_and_split(m + 2, 0, 1, m + 4)
                        wdlo(it * 2 + 1, 1)
                        add_y(it * 2)
                        post_and_split(m + 3, 1, 1, m + 5)
                        post_and_split(m + 4, 0, 0, m + 6)
                        wdlo(it * 2 + 2, 0)
                        add_y(it * 2 + 1)
                        post_and_split(m + 5, 1, 0, m + 7)
                    post_and_split(MT - 2, 0, 1)
                    wdlo(NG - 1, 1)
                    post_and_split(MT - 1, 1, 1)
                    add_y(NG - 2)
                    tr_lo(j + 1)
                    add_y(NG - 1)
                per_width(dve, j, job)

        @block.tensor
        def _(pe):
            pe.sem_inc(s_gu, 2)
            pe.sem_inc(s_yready, 48)

            def transpose_rows(j1):
                pe.wait_ge(s_rows, j1 * 16 * CAP + 16 * CAP)
                for k in range(KT):
                    if k >= 4:
                        pe.wait_ge(s_tr_lo, j1 * KT + (k - 3))
                    for t in range(CAP):
                        last = pe.transpose(ps[k % 4][:, t * P:(t + 1) * P], stage[:, t, k * P:(k + 1) * P], ident)
                    last.then_inc(s_tr, 1)

            transpose_rows(0)
            with pe.Fori(0, job_count(pe)) as j:
                def job(tiles):
                    W = tiles * P
                    unit = 12 // tiles

                    def gate_up(n, s):
                        N = j * MT + n
                        pe.wait_ge(s_gu_lo, N + 3)
                        pe.wait_ge(s_hid, N + 1)
                        for half, (out, done) in enumerate(((gate_ps[s], s_gate), (up_ps[s], s_gu))):
                            for k in range(KT):
                                pe.matmul(out[:, 0:W], gu_hi[s][:, half, k, :], ht_hi[:, k, 0:W], start=(k == 0), stop=False)
                                pe.matmul(out[:, 0:W], gu_hi[s][:, half, k, :], ht_lo[:, k, 0:W], start=False, stop=False)
                                last = pe.matmul(out[:, 0:W], gu_lo[s][:, half, k, :], ht_hi[:, k, 0:W],
                                                 start=False, stop=(k == KT - 1))
                            last.then_inc(done, 1)

                    def down(q, b):
                        Q = j * NG + q
                        pe.wait_ge(s_hlo, Q * 2 + 2)
                        pe.wait_ge(s_wd_lo, Q + 2)
                        for u in range(2 * tiles):
                            t, h = u // 2, u % 2
                            out = y_ps[u % 4][:, :]
                            pe.wait_ge(s_yadded, Q * 24 + (24 + unit * max(u - 3, 0)))
                            for a in range(GROUP):
                                rows = slice(t * P, (t + 1) * P)
                                cols = slice(h * 512, (h + 1) * 512)
                                pe.matmul(out, hid_hi[b][:, a, rows], wd_hi[b][:, a, cols], start=(a == 0), stop=False)
                                pe.matmul(out, hid_hi[b][:, a, rows], wd_lo[b][:, a, cols], start=False, stop=False)
                                last = pe.matmul(out, hid_lo[b][:, a, rows], wd_hi[b][:, a, cols],
                                                 start=False, stop=(a == GROUP - 1))
                            last.then_inc(s_yready, unit)

                    pe.wait_ge(s_tr_lo, j * KT + KT)
                    for n in range(4):
                        gate_up(n, n % 2)
                    with pe.Fori(0, NG // 2 - 1) as it:
                        m = it * 4
                        down(it * 2, 0)
                        gate_up(m + 4, 0)
                        gate_up(m + 5, 1)
                        down(it * 2 + 1, 1)
                        gate_up(m + 6, 0)
                        gate_up(m + 7, 1)
                    down(NG - 2, 0)
                    pe.wait_ge(s_hid, j * MT + MT + 2)
                    transpose_rows(j + 1)
                    down(NG - 1, 1)
                per_width(pe, j, job)


class Chain:

    def __init__(self, eng, sem, base):
        self.eng, self.sem, self.base, self.n = eng, sem, base, 0

    def step(self, instruction):
        self.n += 1
        instruction.then_inc(self.sem, 1)
        self.eng.wait_ge(self.sem, self.base + self.n)


def row_rstd(pool, chain, rstd, sums, width, minus_half):
    chain.step(pool.tensor_scalar(rstd, sums, 1.0 / width, EPS, ALU.mult, ALU.add))
    return pool.tensor_tensor(rstd, rstd, minus_half, ALU.pow)


def pairs(eng, tile):
    tile(0, 0)
    tile(1, 1)
    with eng.Fori(1, TILES // 2 - 1) as pair:
        tile(pair * 2, 0)
        tile(pair * 2 + 1, 1)
    tile(TILES - 2, 0)
    tile(TILES - 1, 1)


def begun(i, n):
    return not isinstance(i, int) or i >= n


def broadcast_rows(vector, n):
    return vector.to_broadcast([P, n])


def pool_mixer(nc, x, gain_mix, gain_ffn, pool_scale, pool_w, bands, x_mid, h_ffn):
    with ExitStack() as ctx:
        new_semaphore = ctx.enter_context(phase_semaphores(nc))
        def sb(n, shape, dt=F32):
            return ctx.enter_context(nc.sbuf_tensor(f"pool_{n}", shape, dt))

        def sem(n):
            return new_semaphore(f"pool_{n}")

        xt = [sb(f"xt{s}", [P, D]) for s in range(2)]
        xh = [sb(f"xh{s}", [P, D]) for s in range(2)]
        squares = sb("squares", [P, D])
        diff = [sb(f"diff{s}", [P, KT, P]) for s in range(2)]
        mid = [sb(f"mid{s}", [P, D]) for s in range(2)]
        hf = [sb(f"hf{s}", [P, D]) for s in range(2)]
        g_mix, g_ffn, g_scale = sb("g_mix", [P, D]), sb("g_ffn", [P, D]), sb("g_scale", [P, D])
        w = sb("w", [P, N_GRP, 2, GRP])
        band = sb("band", [P, 3, N_GRP, P])
        ss = sb("ss", [P, 4])
        rs = sb("rs", [P, 4])
        minus_half = sb("minus_half", [P, 1])
        d_ps = [ctx.enter_context(nc.psum_tensor(f"pool_d{s}", [P, KT, P], F32)) for s in range(2)]
        y_ps = [ctx.enter_context(nc.psum_tensor(f"pool_y{s}", [P, D], F32)) for s in range(2)]
        s_const, s_mid_out, s_hf_out = sem("const"), [sem(f"mid_out{s}") for s in range(2)], [sem(f"hf_out{s}") for s in range(2)]
        s_x = [sem(f"x{s}") for s in range(2)]
        s_rs, s_dve, s_pool, s_xh, s_d, s_diff, s_y, s_mid, s_hf, s_sq = (
            sem(n) for n in ("rs", "dve", "pool", "xh", "d", "diff", "y", "mid", "hf", "sq"))
        s_half, s_seen = sem("half"), sem("seen")
        block = ctx.enter_context(nc.Block())
        x_t = x.rearrange("(i p) d -> i p d", p=P)
        mid_t = x_mid.rearrange("(i p) d -> i p d", p=P)
        h_t = h_ffn.rearrange("(i p) d -> i p d", p=P)

        @block.sync
        def _(sp):
            sp.dma_start(g_mix[:, :], broadcast_rows(gain_mix, D)).then_inc(s_const, 16)
            sp.dma_start(g_ffn[:, :], broadcast_rows(gain_ffn, D)).then_inc(s_const, 16)
            sp.dma_start(g_scale[:, :], broadcast_rows(pool_scale, D)).then_inc(s_const, 16)
            sp.dma_start(w[:, :, :, :], pool_w.rearrange("g (k p) d -> p g k d", p=P)).then_inc(s_const, 16)
            sp.dma_start(band[:, :, :, :], bands).then_inc(s_const, 16)

            def tile(i, s):
                sp.wait_ge(s_mid, i + 1)
                sp.dma_start(mid_t[bass.ds(i, 1), :, :].rearrange("a p d -> p (a d)"), mid[s][:, :]).then_inc(s_mid_out[s], 16)
                sp.wait_ge(s_hf, i + 1)
                sp.dma_start(h_t[bass.ds(i, 1), :, :].rearrange("a p d -> p (a d)"), hf[s][:, :]).then_inc(s_hf_out[s], 16)
            pairs(sp, tile)
            for s in range(2):
                sp.wait_ge(s_mid_out[s], 16 * TILES // 2)
                sp.wait_ge(s_hf_out[s], 16 * TILES // 2)

        @block.gpsimd
        def _(pool):
            pool.memset(minus_half[:, :], -0.5).then_inc(s_half, 1)
            pool.wait_ge(s_half, 1)

            def tile(i, s):
                chain = Chain(pool, s_pool, i * 2)
                for half in range(2):
                    col = slice(2 * half + s, 2 * half + s + 1)
                    pool.wait_ge(s_sq, i * 2 + half + 1)
                    pool.sem_inc(s_seen, 1)
                    row_rstd(pool, chain, rs[:, col], ss[:, col], D, minus_half[:, :]).then_inc(s_rs, 1)
            pairs(pool, tile)

        @block.scalar
        def _(act):
            def load(i, s):
                act.dma_start(xt[s][:, :], x_t[bass.ds(i, 1), :, :].rearrange("a p d -> p (a d)")).then_inc(s_x[s], 16)
            load(0, 0)
            load(1, 1)

            def tile(i, s):
                act.wait_ge(s_x[s], (i - s) * 8 + 16)
                if begun(i, 1):
                    act.wait_ge(s_sq, i * 2)
                    act.wait_ge(s_rs, i * 2)
                act.activation(squares[:, :], xt[s][:, :], ACT.Square, accum_out=ss[:, s:s + 1]).then_inc(s_sq, 1)
                act.wait_ge(s_d, i + 1)
                if begun(i, 2):
                    act.wait_ge(s_y, i - 1)
                act.copy(diff[s][:, :, :], d_ps[s][:, :, :]).then_inc(s_diff, 1)
                act.wait_ge(s_mid, i + 1)
                if not isinstance(i, int) or i + 2 < TILES:
                    load(i + 2, s)
                act.wait_ge(s_sq, i * 2 + 1)
                act.activation(squares[:, :], mid[s][:, :], ACT.Square, accum_out=ss[:, 2 + s:3 + s]).then_inc(s_sq, 1)
            pairs(act, tile)

        @block.vector
        def _(dve):
            dve.wait_ge(s_const, 80)

            def tile(i, s):
                chain = Chain(dve, s_dve, i)
                dve.wait_ge(s_rs, i * 2 + 1)
                if begun(i, 2):
                    dve.wait_ge(s_d, i)
                dve.scalar_tensor_tensor(out=xh[s][:, :], in0=xt[s][:, :], scalar=rs[:, s:s + 1], in1=g_mix[:, :],
                                         op0=ALU.mult, op1=ALU.mult).then_inc(s_xh, 1)
                dve.wait_ge(s_y, i + 1)
                if begun(i, 2):
                    dve.wait_ge(s_mid_out[s], (i - s) * 8)
                    dve.wait_ge(s_hf_out[s], (i - s) * 8)
                chain.step(dve.tensor_tensor(mid[s][:, :], y_ps[s][:, :], g_scale[:, :], ALU.mult))
                dve.tensor_tensor(mid[s][:, :], mid[s][:, :], xt[s][:, :], ALU.add).then_inc(s_mid, 1)
                dve.wait_ge(s_rs, i * 2 + 2)
                dve.wait_ge(s_mid, i + 1)
                dve.scalar_tensor_tensor(out=hf[s][:, :], in0=mid[s][:, :], scalar=rs[:, 2 + s:3 + s], in1=g_ffn[:, :],
                                         op0=ALU.mult, op1=ALU.mult).then_inc(s_hf, 1)
            pairs(dve, tile)

        @block.tensor
        def _(pe):
            pe.wait_ge(s_const, 80)

            def tile(i, s):
                pe.wait_ge(s_xh, i + 1)
                if begun(i, 2):
                    pe.wait_ge(s_diff, i - 1)
                for c in range(KT):
                    g = c // 2
                    last = pe.matmul(d_ps[s][:, c, :], xh[s][:, c * P:(c + 1) * P], band[:, 1 if begun(i, 1) else 0, g, :],
                                     start=True, stop=not begun(i, 1))
                    if begun(i, 1):
                        last = pe.matmul(d_ps[s][:, c, :], xh[1 - s][:, c * P:(c + 1) * P], band[:, 2, g, :],
                                         start=False, stop=True)
                last.then_inc(s_d, 1)
                pe.wait_ge(s_diff, i + 1)
                if begun(i, 2):
                    pe.wait_ge(s_mid, i - 1)
                for g in range(N_GRP):
                    for k in range(2):
                        last = pe.matmul(y_ps[s][:, g * GRP:(g + 1) * GRP], diff[s][:, 2 * g + k, :], w[:, g, k, :],
                                         start=(k == 0), stop=(k == 1))
                last.then_inc(s_y, 1)
            pairs(pe, tile)


def add_norm(nc, name, a, b, gain, x_out, h_out, ident, xt_hi=None, xt_lo=None, router=None, logits=None):
    with ExitStack() as ctx:
        new_semaphore = ctx.enter_context(phase_semaphores(nc))
        def sb(n, shape, dt=F32):
            return ctx.enter_context(nc.sbuf_tensor(f"{name}_{n}", shape, dt))

        def sem(n):
            return new_semaphore(f"{name}_{n}")

        at = [sb(f"a{s}", [P, D]) for s in range(2)]
        bt = [sb(f"b{s}", [P, D]) for s in range(2)]
        xt = [sb(f"x{s}", [P, D]) for s in range(2)]
        ht = [sb(f"h{s}", [P, D]) for s in range(2)]
        squares = sb("squares", [P, D])
        ss, rs = sb("ss", [P, 2]), sb("rs", [P, 2])
        minus_half = sb("minus_half", [P, 1])
        t_ps = [ctx.enter_context(nc.psum_tensor(f"{name}_t{s}", [P, KT, P], F32)) for s in range(2)]
        if gain is not None:
            g = sb("g", [P, D])
        if router is not None:
            r = sb("r", [P, KT, N_EXP])
            hT = [sb(f"hT{s}", [P, KT, P]) for s in range(2)]
            l_ps = [ctx.enter_context(nc.psum_tensor(f"{name}_l{s}", [P, N_EXP], F32)) for s in range(2)]
        s_const, s_half, s_seen = sem("const"), sem("half"), sem("seen")
        s_in = [sem(f"in{s}") for s in range(2)]
        s_out = [sem(f"out{s}") for s in range(2)]
        s_x, s_sq, s_rs, s_pool, s_h, s_t, s_hi, s_lo, s_l = (
            sem(n) for n in ("sum", "sq", "rs", "pool", "h", "t", "hi", "lo", "l"))
        block = ctx.enter_context(nc.Block())
        n_const = (gain is not None) + (router is not None)

        def rows(dram, i):
            return dram[bass.ds(i * P, P), :]

        @block.sync
        def _(sp):
            if gain is not None:
                sp.dma_start(g[:, :], broadcast_rows(gain, D)).then_inc(s_const, 16)
            if router is not None:
                sp.dma_start(r[:, :, :], router.rearrange("(k p) e -> p k e", p=P)).then_inc(s_const, 16)

            def tile(i, s):
                sp.wait_ge(s_x, i + 1)
                sp.dma_start(rows(x_out, i), xt[s][:, :]).then_inc(s_out[s], 16)
                if h_out is not None:
                    sp.wait_ge(s_h, i + 1)
                    sp.dma_start(rows(h_out, i), ht[s][:, :]).then_inc(s_out[s], 16)
            pairs(sp, tile)
            for s in range(2):
                sp.wait_ge(s_out[s], (2 if h_out is not None else 1) * 16 * TILES // 2)

        @block.gpsimd
        def _(pool):
            pool.memset(minus_half[:, :], -0.5).then_inc(s_half, 1)
            pool.wait_ge(s_half, 1)

            def tile(i, s):
                pool.wait_ge(s_sq, i + 1)
                pool.sem_inc(s_seen, 1)
                chain = Chain(pool, s_pool, i)
                row_rstd(pool, chain, rs[:, s:s + 1], ss[:, s:s + 1], D, minus_half[:, :]).then_inc(s_rs, 1)
            pairs(pool, tile)

        @block.scalar
        def _(act):
            def load(i, s):
                act.dma_start(at[s][:, :], rows(a, i)).then_inc(s_in[s], 16)
                act.dma_start(bt[s][:, :], rows(b, i)).then_inc(s_in[s], 16)
            load(0, 0)
            load(1, 1)

            def tile(i, s):
                act.wait_ge(s_x, i + 1)
                if not isinstance(i, int) or i + 2 < TILES:
                    load(i + 2, s)
                if begun(i, 1):
                    act.wait_ge(s_sq, i)
                    act.wait_ge(s_rs, i)
                act.activation(squares[:, :], xt[s][:, :], ACT.Square, accum_out=ss[:, s:s + 1]).then_inc(s_sq, 1)
                act.wait_ge(s_t, i + 1)
                if router is None:
                    act.copy(xt_hi[:, :, bass.ds(i * P, P)], t_ps[s][:, :, :]).then_inc(s_hi, 1)
                else:
                    if begun(i, 2):
                        act.wait_ge(s_l, i - 1)
                    act.copy(hT[s][:, :, :], t_ps[s][:, :, :]).then_inc(s_hi, 1)
            pairs(act, tile)

        @block.vector
        def _(dve):
            if n_const:
                dve.wait_ge(s_const, 16 * n_const)

            def tile(i, s):
                dve.wait_ge(s_in[s], (i - s) * 16 + 32)
                if begun(i, 2):
                    dve.wait_ge(s_out[s], (i - s) * (16 if h_out is not None else 8))
                dve.tensor_tensor(xt[s][:, :], at[s][:, :], bt[s][:, :], ALU.add).then_inc(s_x, 1)
                dve.wait_ge(s_x, i + 1)
                dve.wait_ge(s_rs, i + 1)
                if begun(i, 2):
                    dve.wait_ge(s_t, i - 1)
                if gain is None:
                    dve.tensor_scalar(ht[s][:, :], xt[s][:, :], rs[:, s:s + 1], None, ALU.mult).then_inc(s_h, 1)
                else:
                    dve.scalar_tensor_tensor(out=ht[s][:, :], in0=xt[s][:, :], scalar=rs[:, s:s + 1], in1=g[:, :],
                                             op0=ALU.mult, op1=ALU.mult).then_inc(s_h, 1)
                if router is None:
                    dve.wait_ge(s_hi, i + 1)
                    dve.tensor_tensor(xt_lo[:, :, bass.ds(i * P, P)], t_ps[s][:, :, :], xt_hi[:, :, bass.ds(i * P, P)],
                                      ALU.subtract).then_inc(s_lo, 1)
                else:
                    dve.wait_ge(s_l, i + 1)
                    dve.tensor_copy(logits[:, bass.ds(i, 1), :], l_ps[s][:, :].rearrange("p (a e) -> p a e", a=1)).then_inc(s_lo, 1)
            pairs(dve, tile)

        @block.tensor
        def _(pe):
            if n_const:
                pe.wait_ge(s_const, 16 * n_const)

            def tile(i, s):
                pe.wait_ge(s_h, i + 1)
                if begun(i, 2):
                    pe.wait_ge(s_lo, i - 1)
                for k in range(KT):
                    last = pe.transpose(t_ps[s][:, k, :], ht[s][:, k * P:(k + 1) * P], ident)
                last.then_inc(s_t, 1)
                if router is not None:
                    pe.wait_ge(s_hi, i + 1)
                    for k in range(KT):
                        last = pe.matmul(l_ps[s][:, :], hT[s][:, k, :], r[:, k, :], start=(k == 0), stop=(k == KT - 1))
                    last.then_inc(s_l, 1)
            pairs(pe, tile)


def project(nc, name, xt_hi, xt_lo, w, w_gain, n_chunks, out):
    C = 512
    with ExitStack() as ctx:
        new_semaphore = ctx.enter_context(phase_semaphores(nc))
        def sb(n, shape, dt=F32):
            return ctx.enter_context(nc.sbuf_tensor(f"{name}_{n}", shape, dt))

        def sem(n):
            return new_semaphore(f"{name}_{n}")

        HK = KT // 2
        raw = [sb(f"raw{s}", [P, HK, C]) for s in range(2)]
        w_hi = [sb(f"hi{s}", [P, HK, C], F32R) for s in range(2)]
        w_lo = [sb(f"lo{s}", [P, HK, C], F32R) for s in range(2)]
        gains = sb("gains", [P, n_chunks, KT])
        ot = [sb(f"o{s}", [P, C]) for s in range(4)]
        ps = [ctx.enter_context(nc.psum_tensor(f"{name}_ps{b}", [P, C], F32)) for b in range(TILES)]
        s_raw = [sem(f"raw{s}") for s in range(2)]
        s_out = [sem(f"out{s}") for s in range(4)]
        s_gain, s_scaled, s_hi, s_lo, s_first_half, s_ready, s_copied = (
            sem(n) for n in ("gain", "scaled", "hi", "lo", "first_half", "ready", "copied"))
        block = ctx.enter_context(nc.Block())

        @block.sync
        def _(sp):
            if w_gain is not None:
                sp.dma_start(gains[:, :, :], w_gain).then_inc(s_gain, 16)
            with sp.Fori(0, n_chunks) as c:
                for half in range(2):
                    sp.wait_ge(s_lo, c * 2 + half + 1)
                    sp.dma_start(raw[half][:, :, :], w[bass.ds(c * P, P), half * HK * C:(half + 1) * HK * C]
                                 .rearrange("p (k n) -> p k n", k=HK)).then_inc(s_raw[half], 16)

        @block.gpsimd
        def _(pool):
            with pool.Fori(0, n_chunks) as c:
                for i in range(TILES):
                    pool.wait_ge(s_copied, c * TILES + (i + 1 + TILES))
                    pool.dma_start(out[i * P:(i + 1) * P, bass.ds(c * C, C)], ot[i % 4][:, :]).then_inc(s_out[i % 4], 16)
            for s in range(4):
                pool.wait_ge(s_out[s], 16 * 2 * n_chunks)

        @block.scalar
        def _(act):
            if w_gain is not None:
                act.wait_ge(s_gain, 16)
            with act.Fori(0, n_chunks) as c:
                for half in range(2):
                    act.wait_ge(s_raw[half], c * 16 + 16)
                    if half == 0:
                        act.wait_ge(s_first_half, c + 1)
                    else:
                        act.wait_ge(s_ready, c * TILES + 1)
                    if w_gain is not None:
                        for k in range(HK):
                            kk = half * HK + k
                            act.activation(raw[half][:, k, :], raw[half][:, k, :], ACT.Copy,
                                           scale=gains[:, bass.ds(c, 1), kk:kk + 1].rearrange("p a b -> p (a b)")
                                           ).then_inc(s_scaled, 1)
                        act.wait_ge(s_scaled, c * KT + (half + 1) * HK)
                    act.copy(w_hi[half][:, :, :], raw[half][:, :, :]).then_inc(s_hi, 1)

        @block.vector
        def _(dve):
            dve.sem_inc(s_lo, 2)
            dve.sem_inc(s_copied, TILES)

            def copy_out(c, i):
                dve.wait_ge(s_ready, c * TILES + (i + 2))
                if begun(c, 1) or i >= 4:
                    dve.wait_ge(s_out[i % 4], c * 32 + 16 * (i // 4))
                dve.tensor_copy(ot[i % 4][:, :], ps[i][:, :]).then_inc(s_copied, 1)

            def split(c, half):
                dve.wait_ge(s_hi, c * 2 + half + 1)
                dve.tensor_tensor(w_lo[half][:, :, :], raw[half][:, :, :], w_hi[half][:, :, :], ALU.subtract).then_inc(s_lo, 1)

            split(0, 0)
            split(0, 1)

            def split_and_copy_out(c):
                split(c, 0)
                for i in range(TILES):
                    if i == TILES // 2:
                        split(c, 1)
                    copy_out(c - 1, i)

            split_and_copy_out(1)
            if n_chunks > 2:
                with dve.Fori(2, n_chunks) as c:
                    split_and_copy_out(c)
            for i in range(TILES):
                copy_out(n_chunks - 1, i)

        @block.tensor
        def _(pe):
            pe.sem_inc(s_first_half, 1)
            pe.sem_inc(s_ready, 1)
            with pe.Fori(0, n_chunks) as c:
                for half in range(2):
                    pe.wait_ge(s_lo, c * 2 + half + 3)
                    for i in range(TILES):
                        if half == 0:
                            pe.wait_ge(s_copied, c * TILES + (i + 1))
                        for k in range(HK):
                            kk = half * HK + k
                            rows = slice(i * P, (i + 1) * P)
                            pe.matmul(ps[i][:, :], xt_hi[:, kk, rows], w_hi[half][:, k, :], start=(kk == 0), stop=False)
                            pe.matmul(ps[i][:, :], xt_hi[:, kk, rows], w_lo[half][:, k, :], start=False, stop=False)
                            last = pe.matmul(ps[i][:, :], xt_lo[:, kk, rows], w_hi[half][:, k, :],
                                             start=False, stop=(kk == KT - 1))
                        if half == 1:
                            last.then_inc(s_ready, 1)
                        if half == 0 and i == TILES - 1:
                            last.then_inc(s_first_half, 1)


def split_heads(nc, qkv, k_gain, ident, kt, qt_dram, gates):
    NH = N_HEADS + 2 * N_KV
    with ExitStack() as ctx:
        new_semaphore = ctx.enter_context(phase_semaphores(nc))
        def sb(n, shape, dt=F32):
            return ctx.enter_context(nc.sbuf_tensor(f"heads_{n}", shape, dt))

        def sem(n):
            return new_semaphore(f"heads_{n}")

        raw = [sb(f"raw{s}", [P, NH, DH]) for s in range(2)]
        squares = sb("squares", [P, NH, DH])
        ss = [sb(f"ss{s}", [P, NH]) for s in range(2)]
        minus_half = sb("minus_half", [P, NH])
        kg = sb("kg", [P, 2 * N_KV, DH])
        gate_raw = sb("gate_raw", [P, TILES, 3 * N_HEADS])
        qst = sb("qst", [P, N_HEADS, 2, DH], F32R)
        kst = sb("kst", [P, 2 * N_KV, 4, DH], F32R)
        qt = [sb(f"qt{s}", [P, N_HEADS // 2, P], F32R) for s in range(2)]
        q_ps = [ctx.enter_context(nc.psum_tensor(f"heads_q{s}", [P, 8, P], F32)) for s in range(2)]
        k_ps = [ctx.enter_context(nc.psum_tensor(f"heads_k{s}", [P, 8, P], F32)) for s in range(2)]
        s_const, s_half, s_seen = sem("const"), sem("half"), sem("seen")
        s_raw = [sem(f"raw{s}") for s in range(2)]
        s_qt_out = [sem(f"qt_out{s}") for s in range(2)]
        s_gate, s_gate_exp, s_chain, s_pool = sem("gate"), sem("gate_exp"), sem("chain"), sem("pool")
        s_sq, s_ss, s_rs, s_norm, s_hi, s_lo, s_tr, s_out = (
            sem(n) for n in ("sq", "ss", "rs", "norm", "hi", "lo", "tr", "out"))
        block = ctx.enter_context(nc.Block())
        chunks = ((0, 3 * 512, N_HEADS), (N_HEADS, 512, N_KV), (N_HEADS + N_KV, 1024, N_KV))

        @block.sync
        def _(sp):
            sp.dma_start(kg[:, :, :], k_gain.to_broadcast([P, 2 * N_KV * DH]).rearrange("p (h d) -> p h d", d=DH)).then_inc(s_const, 16)
            sp.dma_start(gate_raw[:, :, :], qkv[:, 5 * 512:5 * 512 + 3 * N_HEADS].rearrange("(i p) n -> p i n", p=P)).then_inc(s_gate, 16)

            def tile(i, s):
                if begun(i, 2):
                    sp.wait_ge(s_lo, i - 1)
                for h0, col, n in chunks:
                    sp.dma_start(raw[s][:, h0:h0 + n, :], qkv[bass.ds(i * P, P), col:col + n * DH]
                                 .rearrange("p (h d) -> p h d", d=DH)).then_inc(s_raw[s], 16)
            pairs(sp, tile)

        @block.gpsimd
        def _(pool):
            pool.memset(minus_half[:, :], -0.5).then_inc(s_half, 1)
            pool.wait_ge(s_half, 1)

            def tile(i, s):
                pool.wait_ge(s_ss, i + 1)
                pool.sem_inc(s_seen, 1)
                row_rstd(pool, Chain(pool, s_pool, i), ss[s][:, :], ss[s][:, :], DH, minus_half[:, :]).then_inc(s_rs, 1)
                for half in range(2):
                    pool.wait_ge(s_out, i * 3 + half + 1)
                    pool.dma_start(qt_dram[bass.ds(i * P, P), half * 8 * P:(half + 1) * 8 * P], qt[half][:, :, :].bitcast(F32)
                                   ).then_inc(s_qt_out[half], 16)
            pairs(pool, tile)
            for s in range(2):
                pool.wait_ge(s_qt_out[s], 16 * TILES)

        @block.scalar
        def _(act):
            act.wait_ge(s_gate, 16)
            act.activation(gate_raw[:, :, :], gate_raw[:, :, :], ACT.Exp, scale=-1.0).then_inc(s_gate_exp, 1)

            def tile(i, s):
                act.wait_ge(s_raw[s], (i - s) * 24 + 48)
                if begun(i, 1):
                    act.wait_ge(s_ss, i)
                act.activation(squares[:, :, :], raw[s][:, :, :], ACT.Square).then_inc(s_sq, 1)
                act.wait_ge(s_norm, i + 1)
                if begun(i, 1):
                    act.wait_ge(s_tr, i * 3)
                act.copy(qst[:, :, 0, :], raw[s][:, 0:N_HEADS, :]).then_inc(s_hi, 1)
                act.copy(kst[:, :, 0, :], raw[s][:, N_HEADS:NH, :]).then_inc(s_hi, 1)
                act.copy(kst[:, :, 1, :], raw[s][:, N_HEADS:NH, :]).then_inc(s_hi, 1)
                for half in range(2):
                    act.wait_ge(s_tr, i * 3 + half + 1)
                    if begun(i, 1):
                        act.wait_ge(s_qt_out[half], i * 16)
                    act.copy(qt[half][:, :, :], q_ps[half][:, :, :]).then_inc(s_out, 1)
                act.wait_ge(s_tr, i * 3 + 3)
                for half in range(2):
                    last = act.copy(kt[:, half * 4:half * 4 + 4, :, bass.ds(i * P, P)],
                                    k_ps[half][:, :, :].rearrange("p (h l) t -> p h l t", l=2))
                last.then_inc(s_out, 1)
            pairs(act, tile)

        @block.vector
        def _(dve):
            dve.wait_ge(s_gate_exp, 1)
            chain = Chain(dve, s_chain, 0)
            chain.step(dve.tensor_scalar(gate_raw[:, :, :], gate_raw[:, :, :], 1.0, None, ALU.add))
            chain.step(dve.reciprocal(gates[:, :, :], gate_raw[:, :, :]))
            dve.wait_ge(s_const, 16)

            def tile(i, s):
                dve.wait_ge(s_sq, i + 1)
                dve.tensor_reduce(ss[s][:, :], squares[:, :, :], AX.X, ALU.add).then_inc(s_ss, 1)
                dve.wait_ge(s_rs, i + 1)
                chain = Chain(dve, s_chain, i * 2 + 2)
                chain.step(dve.tensor_tensor(raw[s][:, :, :], raw[s][:, :, :],
                                             ss[s][:, :].rearrange("p (h a) -> p h a", a=1).to_broadcast([P, NH, DH]), ALU.mult))
                dve.tensor_tensor(raw[s][:, N_HEADS:NH, :], raw[s][:, N_HEADS:NH, :], kg[:, :, :], ALU.mult).then_inc(s_norm, 1)
                dve.wait_ge(s_hi, i * 3 + 3)
                dve.tensor_tensor(qst[:, :, 1, :], raw[s][:, 0:N_HEADS, :], qst[:, :, 0, :], ALU.subtract)
                dve.tensor_tensor(kst[:, :, 2, :], raw[s][:, N_HEADS:NH, :], kst[:, :, 0, :], ALU.subtract)
                chain.step(dve.tensor_tensor(kst[:, :, 3, :], raw[s][:, N_HEADS:NH, :], kst[:, :, 0, :], ALU.subtract))
                dve.sem_inc(s_lo, 1)
            pairs(dve, tile)

        @block.tensor
        def _(pe):
            def tile(i, s):
                pe.wait_ge(s_lo, i + 1)
                if begun(i, 1):
                    pe.wait_ge(s_out, i * 3)
                for half in range(2):
                    for h in range(8):
                        last = pe.transpose(q_ps[half][:, h, :], qst[:, half * 8 + h, :, :].rearrange("p a d -> p (a d)").bitcast(F32), ident)
                    last.then_inc(s_tr, 1)
                for half in range(2):
                    for h in range(4):
                        for hl in range(2):
                            last = pe.transpose(k_ps[half][:, h * 2 + hl, :],
                                                kst[:, half * 4 + h, hl * 2:hl * 2 + 2, :].rearrange("p a d -> p (a d)").bitcast(F32), ident)
                last.then_inc(s_tr, 1)
            pairs(pe, tile)


def compress_keys(nc, qkv, pos, w1, w2, kc_gain, ident, kct, vc):
    NBL = 64
    with ExitStack() as ctx:
        new_semaphore = ctx.enter_context(phase_semaphores(nc))
        def sb(n, shape, dt=F32):
            return ctx.enter_context(nc.sbuf_tensor(f"cmp_{n}", shape, dt))

        def sem(n):
            return new_semaphore(f"cmp_{n}")

        MP = SEQ // 2
        zrow = [sb(f"zrow{s}", [P, MP // P, N_KV, 2, DH]) for s in range(2)]
        zt = [sb(f"zt{s}", [P, N_KV, MP + 8]) for s in range(2)]
        posT = sb("posT", [P, 2, 16])
        w1s = [sb(f"w1s{s}", [P, 16, 2 * P]) for s in range(2)]
        w2s = sb("w2s", [P, 2, 2, DH])
        blk = [sb(f"blk{s}", [P, N_KV, NBL]) for s in range(2)]
        hidT = [sb(f"hidT{s}", [P, 2, N_KV, NBL]) for s in range(2)]
        kc = sb("kc", [NBL, N_KV, DH])
        sq = sb("sq", [NBL, N_KV, DH])
        ss = sb("ss", [NBL, N_KV])
        minus_half = sb("minus_half", [NBL, N_KV])
        kg = sb("kg", [NBL, DH])
        kst = sb("kst", [NBL, N_KV, 2, DH])
        t_ps = [ctx.enter_context(nc.psum_tensor(f"cmp_t{s}", [P, MP], F32)) for s in range(4)]
        h_ps = [ctx.enter_context(nc.psum_tensor(f"cmp_h{s}", [P, N_KV, NBL], F32)) for s in range(2)]
        o_ps = [ctx.enter_context(nc.psum_tensor(f"cmp_o{s}", [NBL, N_KV, DH], F32)) for s in range(2)]
        s_const, s_z, s_half, s_zero = sem("const"), sem("z"), sem("half"), sem("zero")
        s_tr, s_zt, s_blk, s_h, s_hid, s_o, s_fin = (sem(n) for n in ("tr", "zt", "blk", "h", "hid", "o", "fin"))
        s_chain, s_pool, s_ss, s_rs, s_norm, s_st, s_ktr = (
            sem(n) for n in ("chain", "pool", "ss", "rs", "norm", "st", "ktr"))
        s_h_step = sem("h_step")
        block = ctx.enter_context(nc.Block())

        @block.sync
        def _(sp):
            for z in range(2):
                src = qkv[:, z * 256:(z + 1) * 256].rearrange("(m p l) (g d) -> p m g l d", p=P, l=2, d=DH)
                for m in range(MP // P):
                    for g in range(N_KV):
                        sp.dma_start(zrow[z][:, m, g, :, :], src[:, m, g, :, :]).then_inc(s_z, 16)
            sp.dma_start(posT[:, :, :], pos).then_inc(s_const, 16)
            for z in range(2):
                sp.dma_start(w1s[z][:, :, :], w1[z].rearrange("(l p) n -> p l n", p=P)).then_inc(s_const, 16)
                sp.dma_start(w2s[:, z, :, :], w2[z].rearrange("(k p) n -> p k n", p=P)).then_inc(s_const, 16)
            sp.dma_start(kg[:, :], kc_gain.to_broadcast([NBL, DH])).then_inc(s_const, 16)

        @block.gpsimd
        def _(pool):
            for z in range(2):
                pool.memset(zt[z][:, :, MP:MP + 8], 0.0).then_inc(s_zero, 1)
            pool.memset(minus_half[:, :], -0.5).then_inc(s_half, 1)
            pool.wait_ge(s_half, 1)
            pool.wait_ge(s_ss, 1)
            row_rstd(pool, Chain(pool, s_pool, 0), ss[:, :], ss[:, :], DH, minus_half[:, :]).then_inc(s_rs, 1)

        @block.scalar
        def _(act):
            for z in range(2):
                for g in range(N_KV):
                    act.wait_ge(s_tr, z * N_KV + g + 1)
                    act.copy(zt[z][:, g, 0:MP], t_ps[g][:, :]).then_inc(s_zt, 1)
            for z in range(2):
                for n in range(2):
                    act.wait_ge(s_h, z * 2 + n + 1)
                    act.activation(hidT[z][:, n, :, :], h_ps[n][:, :, :], ACT.Silu).then_inc(s_hid, 1)
            act.wait_ge(s_norm, 1)
            for a in range(2):
                act.copy(kst[:, :, a, :], kc[:, :, :]).then_inc(s_st, 1)
            act.wait_ge(s_ktr, 1)
            for g in range(N_KV):
                for copy in range(2):
                    act.copy(kct[:, g, copy * NBL:(copy + 1) * NBL], t_ps[g][:, 0:NBL]).then_inc(s_fin, 1)
            act.wait_ge(s_fin, 2 * N_KV)

        @block.vector
        def _(dve):
            dve.wait_ge(s_const, 16 * 6)
            dve.wait_ge(s_zero, 2)
            dve.wait_ge(s_zt, 2 * N_KV)
            for z in range(2):
                for l in range(16):
                    n = z * 16 + l
                    if n >= 2:
                        dve.wait_ge(s_h_step, n - 1)
                    dve.tensor_scalar(blk[l % 2][:, :, :], zt[z][:, :, l:l + 8 * (NBL - 1) + 1:8], posT[:, z, l:l + 1], None,
                                      ALU.add).then_inc(s_blk, 1)
            chain = Chain(dve, s_chain, 0)
            dve.wait_ge(s_o, 1)
            chain.step(dve.tensor_copy(kc[:, :, :], o_ps[0][:, :, :]))
            dve.wait_ge(s_o, 2)
            chain.step(dve.tensor_copy(vc[:, :, :], o_ps[1][:, :, :]))
            chain.step(dve.tensor_tensor(sq[:, :, :], kc[:, :, :], kc[:, :, :], ALU.mult))
            dve.tensor_reduce(ss[:, :], sq[:, :, :], AX.X, ALU.add).then_inc(s_ss, 1)
            dve.wait_ge(s_rs, 1)
            chain.step(dve.tensor_tensor(kc[:, :, :], kc[:, :, :],
                                         ss[:, :].rearrange("p (h a) -> p h a", a=1).to_broadcast([NBL, N_KV, DH]), ALU.mult))
            dve.tensor_tensor(kc[:, :, :], kc[:, :, :],
                              kg[:, :].rearrange("p (a d) -> p a d", a=1).to_broadcast([NBL, N_KV, DH]), ALU.mult).then_inc(s_norm, 1)

        @block.tensor
        def _(pe):
            pe.wait_ge(s_z, 16 * 2 * (MP // P) * N_KV)
            for z in range(2):
                for g in range(N_KV):
                    if z == 1:
                        pe.wait_ge(s_zt, g + 1)
                    for m in range(MP // P):
                        last = pe.transpose(t_ps[g][:, m * P:(m + 1) * P], zrow[z][:, m, g, :, :].rearrange("p l d -> p (l d)"), ident)
                    last.then_inc(s_tr, 1)
            for z in range(2):
                for l in range(16):
                    pe.wait_ge(s_blk, z * 16 + l + 1)
                    if z == 1 and l == 0:
                        pe.wait_ge(s_hid, 2)
                    for n in range(2):
                        last = pe.matmul(h_ps[n][:, :, :], w1s[z][:, l, n * P:(n + 1) * P], blk[l % 2][:, :, :],
                                         start=(l == 0), stop=(l == 15))
                        if l == 15:
                            last.then_inc(s_h, 1)
                    if l < 15:
                        last.then_inc(s_h_step, 1)
                    else:
                        pe.wait_ge(s_h, z * 2 + 2)
                        pe.sem_inc(s_h_step, 1)
            for z in range(2):
                pe.wait_ge(s_hid, z * 2 + 2)
                for g in range(N_KV):
                    for n in range(2):
                        last = pe.matmul(o_ps[z][:, g, :], hidT[z][:, n, g, :], w2s[:, z, n, :], start=(n == 0), stop=(n == 1))
                last.then_inc(s_o, 1)
            pe.wait_ge(s_st, 2)
            for g in range(N_KV):
                last = pe.transpose(t_ps[g][:, 0:NBL], kst[:, g, :, :].rearrange("p a d -> p (a d)"), ident[0:NBL, 0:NBL])
            last.then_inc(s_ktr, 1)


def bias_tables(nc, rel_bias, onehot, win_mask, vec_dram, win, cmpb):
    NB1 = N_BUCKETS + 1
    with ExitStack() as ctx:
        new_semaphore = ctx.enter_context(phase_semaphores(nc))
        tab = ctx.enter_context(nc.sbuf_tensor("bias_tab", [NB1, N_HEADS], F32))
        hot = ctx.enter_context(nc.sbuf_tensor("bias_hot", [NB1, VEC], F32))
        vec = ctx.enter_context(nc.sbuf_tensor("bias_vec", [N_HEADS, VEC], F32))
        ps = [ctx.enter_context(nc.psum_tensor(f"bias_ps{b}", [N_HEADS, 512], F32)) for b in range(5)]
        s_in, s_neg, s_mm, s_copy, s_vec, s_out = (
            new_semaphore(f"bias_{n}") for n in ("in", "neg", "mm", "copy", "vec", "out"))
        block = ctx.enter_context(nc.Block())
        spans = [(a, min(a + 512, VEC)) for a in range(0, VEC, 512)]

        @block.sync
        def _(sp):
            sp.dma_start(tab[0:N_BUCKETS, :], rel_bias).then_inc(s_in, 16)
            sp.dma_start(hot[:, :], onehot).then_inc(s_in, 16)
            sp.dma_start(win[:, :, 0:P], win_mask.rearrange("p (a n) -> p a n", a=1).to_broadcast([P, N_HEADS, P])).then_inc(s_out, 16)
            sp.wait_ge(s_copy, len(spans))
            sp.dma_start(vec_dram, vec[:, :]).then_inc(s_vec, 16)
            sp.wait_ge(s_vec, 16)
            for q in range(P):
                sp.dma_start(win[q:q + 1, :, P:3 * P], vec_dram[:, 127 - q:127 - q + 2 * P].rearrange("(a h) n -> a h n", a=1)
                             ).then_inc(s_out, 16)
            phases = vec_dram[:, NEAR:VEC].rearrange("h (r m) -> r h m", r=16)
            for a in range(8):
                sp.dma_start(cmpb[16 * a:16 * a + 16, :, :], phases[:, :, 7 - a:7 - a + CB]).then_inc(s_out, 16)
            sp.wait_ge(s_out, 16 * (P + 9))

        @block.vector
        def _(dve):
            dve.memset(tab[N_BUCKETS:NB1, :], NEG).then_inc(s_neg, 1)
            for n, (a, b) in enumerate(spans):
                dve.wait_ge(s_mm, n + 1)
                dve.tensor_copy(vec[:, a:b], ps[n][:, 0:b - a]).then_inc(s_copy, 1)

        @block.tensor
        def _(pe):
            pe.wait_ge(s_in, 32)
            pe.wait_ge(s_neg, 1)
            for n, (a, b) in enumerate(spans):
                pe.matmul(ps[n][:, 0:b - a], tab[:, :], hot[:, a:b], start=True, stop=True).then_inc(s_mm, 1)


def attend(nc, qkv, qt_dram, kt, kct, vc, gates, win, cmpb, sel_const, row_valid, ident, ot_dram):
    with ExitStack() as ctx:
        new_semaphore = ctx.enter_context(phase_semaphores(nc))
        def sb(n, shape, dt=F32):
            return ctx.enter_context(nc.sbuf_tensor(f"att_{n}", shape, dt))

        def sem(n):
            return new_semaphore(f"att_{n}")

        R = N_HEADS // N_KV
        NBL, NSB = 64, 16
        vs, vw = sb("vs", [P, TILES, N_KV * DH]), sb("vw", [P, TILES, N_KV * DH])
        qt = [sb(f"qt{s}", [P, N_HEADS, P], F32R) for s in range(2)]
        p_slc = [sb(f"p_slc{s}", [P, R, SEQ]) for s in range(2)]
        p_win = [sb(f"p_win{s}", [P, R, 3 * P]) for s in range(2)]
        p_cmp = [sb(f"p_cmp{s}", [P, N_HEADS, NBL]) for s in range(2)]
        shares = sb("shares", [P, N_HEADS, NBL])
        near = [sb(f"near{s}", [P, 2 * P]) for s in range(2)]
        pt = [sb(f"pt{s}", [P, R, P]) for s in range(4)]
        ot = [sb(f"ot{s}", [P, 2, P]) for s in range(2)]
        mx, neg_max, sums, scale = sb("mx", [P, 8, 2]), sb("neg_max", [P, 8]), sb("sums", [P, 8]), sb("scale", [P, 8])
        c_mx, c_rs = sb("c_mx", [P, N_HEADS]), sb("c_rs", [P, N_HEADS])
        c_scale = [sb(f"c_scale{s}", [P, N_HEADS]) for s in range(2)]
        group_p = sb("group_p", [P, N_KV, NBL])
        imp, pick, top = sb("imp", [P, N_KV, NSB]), sb("pick", [P, N_KV, NSB]), sb("top", [P, N_KV])
        sel = [sb(f"sel{s}", [P, N_KV, NSB]) for s in range(2)]
        consts = sb("consts", [P, 2 * TILES + 1, NSB])
        valid = sb("valid", [P, 1])
        s_ps = [ctx.enter_context(nc.psum_tensor(f"att_s{s}", [P, SEQ], F32)) for s in range(2)]
        t_ps = [ctx.enter_context(nc.psum_tensor(f"att_t{s}", [P, R, P], F32)) for s in range(2)]
        o_ps = [ctx.enter_context(nc.psum_tensor(f"att_o{s}", [P, 512], F32)) for s in range(2)]
        s_const, s_qt = sem("const"), [sem(f"qt{s}") for s in range(2)]
        s_scores, s_sread, s_negmax, s_exp, s_scale, s_scaled = (
            sem(n) for n in ("scores", "sread", "negmax", "exp", "scale", "scaled"))
        s_cready, s_cexp, s_cscale, s_cscaled, s_sel, s_near = (
            sem(n) for n in ("cready", "cexp", "cscale", "cscaled", "sel", "near"))
        s_tr, s_pt_act, s_pt_dve, s_pv, s_oevac = (sem(n) for n in ("tr", "pt_act", "pt_dve", "pv", "oevac"))
        s_chain, s_ot_out = sem("chain"), [sem(f"ot_out{s}") for s in range(2)]
        block = ctx.enter_context(nc.Block())

        def cmp_step(i, g):
            return 36 * i + g

        def unit_step(u, b):
            return 36 * (u // 4) + 4 + 8 * (u % 4) + b

        def key_tiles(u):
            i = u // 4
            w0 = max(0, i - 2)
            return ([("cmp", 0, 0)] + [("win", (t - i + 2) * P, t) for t in range(w0, i + 1)]
                    + [("slc", t * P, t) for t in range(i + 1)])

        first_pt = [0]
        for u in range(4 * TILES):
            first_pt.append(first_pt[-1] + len(key_tiles(u)))

        def part(u, b):
            n = len(key_tiles(u))
            return range(first_pt[u] + n * b // 8, first_pt[u] + n * (b + 1) // 8)

        @block.sync
        def _(sp):
            sp.dma_start(vs[:, :, :], qkv[:, 768:1024].rearrange("(i p) n -> p i n", p=P)).then_inc(s_const, 16)
            sp.dma_start(vw[:, :, :], qkv[:, 1280:1536].rearrange("(i p) n -> p i n", p=P)).then_inc(s_const, 16)
            sp.dma_start(consts[:, :, :], sel_const).then_inc(s_const, 16)
            sp.dma_start(valid[:, :], row_valid).then_inc(s_const, 16)

            def load_q(i):
                sp.dma_start(qt[i % 2][:, :, :].bitcast(F32), qt_dram[i * P:(i + 1) * P, :].rearrange("p (h t) -> p h t", t=P)
                             ).then_inc(s_qt[i % 2], 16)
            load_q(0)
            load_q(1)
            for u in range(4 * TILES):
                i, g = divmod(u, 4)
                if g == 0 and 1 <= i < TILES - 1:
                    sp.wait_ge(s_scores, 36 * i)
                    load_q(i + 1)
                sp.wait_ge(s_oevac, u + 1)
                sp.dma_start(ot_dram[:, 2 * g:2 * g + 2, i * P:(i + 1) * P], ot[u % 2][:, :, :]).then_inc(s_ot_out[u % 2], 16)
            for s in range(2):
                sp.wait_ge(s_ot_out[s], 16 * 2 * TILES)

        @block.gpsimd
        def _(pool):
            def scale_cmp(i):
                pool.wait_ge(s_cscale, i + 1)
                pool.tensor_tensor(p_cmp[i % 2][:, :, :], p_cmp[i % 2][:, :, :],
                                   c_scale[i % 2][:, :].rearrange("p (h a) -> p h a", a=1).to_broadcast([P, N_HEADS, NBL]),
                                   ALU.mult).then_inc(s_cscaled, 1)

            def near_bias(u, r):
                i, g = divmod(u, 4)
                n = (u - 8) * R + r
                pool.wait_ge(s_sel, i - 1)
                if n >= 2:
                    v, q = divmod(n - 2, R)
                    pool.wait_ge(s_sread, unit_step(v + 8, 2 * q) + 1)
                pool.tensor_tensor(near[n % 2][:, :].rearrange("p (b c) -> p b c", c=DH),
                                   win[:, 4 * g + r, P:3 * P].rearrange("p (b c) -> p b c", c=DH),
                                   sel[i % 2][:, g, 2 * i - 2:2 * i + 2].rearrange("p (b a) -> p b a", a=1).to_broadcast([P, 4, DH]),
                                   ALU.add).then_inc(s_near, 1)

            def scale_p(k):
                u, b = divmod(k, 8)
                i = u // 4
                if b % 2 == 0:
                    p = p_slc[u % 2][:, b // 2, 0:(i + 1) * P]
                else:
                    p = p_win[u % 2][:, b // 2, max(0, 2 - i) * P:3 * P]
                pool.wait_ge(s_scale, k + 1)
                pool.tensor_scalar(p, p, scale[:, k % 8:k % 8 + 1], None, ALU.mult).then_inc(s_scaled, 1)

            for i in range(TILES):
                for g in range(N_KV):
                    u = 4 * i + g
                    for b in range(8):
                        if i >= 2 and b % 2 == 0:
                            near_bias(u, b // 2)
                        if u or b:
                            scale_p(8 * u + b - 1)
                        if g == 0 and b == 0:
                            scale_cmp(i)
            scale_p(8 * 4 * TILES - 1)

        @block.scalar
        def _(act):
            def copy_pt(m):
                act.wait_ge(s_tr, m + 1)
                if m >= 4:
                    act.wait_ge(s_pv, m - 3)
                rows = NBL if m in first_pt else P
                act.copy(pt[m % 4][0:rows, :, :], t_ps[m % 2][0:rows, :, :]).then_inc(s_pt_act, 1)

            def copy_out(u):
                act.wait_ge(s_pv, first_pt[u + 1])
                if u >= 2:
                    act.wait_ge(s_ot_out[u % 2], 16 * (u // 2))
                act.copy(ot[u % 2][:, :, :], o_ps[u % 2][:, 0:2 * P].rearrange("p (a q) -> p a q", a=2)).then_inc(s_oevac, 1)

            def values_part(u, b):
                for m in part(u, b):
                    if m == first_pt[u] + 1 and u >= 1:
                        copy_out(u - 1)
                    if m % 2 == 0:
                        copy_pt(m)

            for i in range(TILES):
                act.wait_ge(s_cready, i + 1)
                act.activation(p_cmp[i % 2][:, :, :], p_cmp[i % 2][:, :, :], ACT.Exp).then_inc(s_cexp, 1)
                for g in range(N_KV):
                    u = 4 * i + g
                    for b in range(8):
                        k = 8 * u + b
                        if b % 2 == 0:
                            p = p_slc[u % 2][:, b // 2, 0:(i + 1) * P]
                        else:
                            p = p_win[u % 2][:, b // 2, max(0, 2 - i) * P:3 * P]
                        act.wait_ge(s_negmax, k + 1)
                        act.activation(p, p, ACT.Exp, bias=neg_max[:, k % 8:k % 8 + 1],
                                       accum_out=sums[:, k % 8:k % 8 + 1]).then_inc(s_exp, 1)
                        if u:
                            values_part(u - 1, b)
            for b in range(8):
                values_part(4 * TILES - 1, b)
            copy_out(4 * TILES - 1)

        @block.vector
        def _(dve):
            dve.wait_ge(s_const, 64)
            chain = Chain(dve, s_chain, 0)

            def bc(ap, n):
                return ap.rearrange("p (h a) -> p h a", a=1).to_broadcast([P, ap.shape[1], n])

            def copy_pt(m):
                dve.wait_ge(s_tr, m + 1)
                if m >= 4:
                    dve.wait_ge(s_pv, m - 3)
                rows = NBL if m in first_pt else P
                dve.tensor_copy(pt[m % 4][0:rows, :, :], t_ps[m % 2][0:rows, :, :]).then_inc(s_pt_dve, 1)

            def finish(k):
                u, b = divmod(k, 8)
                i, g = divmod(u, 4)
                dve.wait_ge(s_exp, k + 1)
                if k >= 8:
                    dve.wait_ge(s_scaled, k - 7)
                c = slice(k % 8, k % 8 + 1)
                chain.step(dve.reciprocal(sums[:, c], sums[:, c]))
                at = (4 * g + b // 2) * 3 + 1 + b % 2
                dve.tensor_tensor(scale[:, c], sums[:, c], gates[:, i, at:at + 1], ALU.mult).then_inc(s_scale, 1)

            def compressed(i):
                pc = p_cmp[i % 2]
                for g in range(N_KV):
                    n = cmp_step(i, g)
                    dve.wait_ge(s_scores, n + 1)
                    if i >= 2 and g == 0:
                        dve.wait_ge(s_tr, first_pt[4 * (i - 1)])
                    hs = slice(4 * g, 4 * g + 4)
                    dve.tensor_tensor(pc[:, hs, :], s_ps[n % 2][:, 0:4 * P].rearrange("p (r c) -> p r c", c=P)[:, :, 0:NBL],
                                      cmpb[:, hs, 56 - 8 * i:56 - 8 * i + NBL], ALU.add).then_inc(s_sread, 1)
                dve.wait_ge(s_sread, cmp_step(i, 3) + 1)
                chain.step(dve.tensor_reduce(c_mx[:, :], pc[:, :, :], AX.X, ALU.max))
                dve.tensor_tensor(pc[:, :, :], pc[:, :, :], bc(c_mx[:, :], NBL), ALU.subtract).then_inc(s_cready, 1)
                if i:
                    finish(8 * 4 * i - 1)
                dve.wait_ge(s_cexp, i + 1)
                chain.step(dve.tensor_reduce(c_rs[:, :], pc[:, :, :], AX.X, ALU.add))
                chain.step(dve.reciprocal(c_rs[:, :], c_rs[:, :]))
                if i == 0:
                    chain.step(dve.tensor_scalar(c_rs[:, :], c_rs[:, :], valid[:, 0:1], None, ALU.mult))
                if i >= 2:
                    chain.step(dve.tensor_tensor(shares[:, :, :], pc[:, :, :], bc(c_rs[:, :], NBL), ALU.mult))
                    dve.wait_ge(s_cscaled, i - 1)
                dve.tensor_tensor(c_scale[i % 2][:, :], c_rs[:, :],
                                  gates[:, i, :].rearrange("p (h b) -> p h b", b=3)[:, :, 0], ALU.mult).then_inc(s_cscale, 1)
                if i >= 2:
                    select_blocks(i)

            def select_blocks(i):
                chain.step(dve.tensor_reduce(group_p[:, :, :], shares[:, :, :].rearrange("p (g r) c -> p g c r", r=R), AX.X, ALU.add))
                fours = group_p[:, :, :].rearrange("p g (j c) -> p g j c", c=4)
                chain.step(dve.tensor_reduce(imp[:, :, :], fours[:, :, :, 0:3], AX.X, ALU.add))
                chain.step(dve.scalar_tensor_tensor(out=imp[:, :, :], in0=fours[:, :, :, 3], scalar=0.5, in1=imp[:, :, :],
                                                    op0=ALU.mult, op1=ALU.add))
                chain.step(dve.scalar_tensor_tensor(out=imp[:, :, 1:NSB], in0=fours[:, :, 0:NSB - 1, 3], scalar=0.5,
                                                    in1=imp[:, :, 1:NSB], op0=ALU.mult, op1=ALU.add))

                def per_group(row):
                    return consts[:, row:row + 1, :].to_broadcast([P, N_KV, NSB])

                chain.step(dve.tensor_tensor(imp[:, :, :], imp[:, :, :], per_group(i), ALU.add))
                chain.step(dve.tensor_reduce(top[:, :], imp[:, :, :], AX.X, ALU.max))
                chain.step(dve.tensor_tensor(pick[:, :, :], imp[:, :, :], bc(top[:, :], NSB), ALU.is_equal))
                chain.step(dve.tensor_tensor(pick[:, :, :], pick[:, :, :], per_group(2 * TILES), ALU.mult))
                chain.step(dve.tensor_reduce(top[:, :], pick[:, :, :], AX.X, ALU.max))
                chain.step(dve.tensor_tensor(pick[:, :, :], pick[:, :, :], bc(top[:, :], NSB), ALU.is_equal))
                chain.step(dve.tensor_tensor(pick[:, :, :], pick[:, :, :], per_group(TILES + i), ALU.add))
                dve.tensor_scalar(sel[i % 2][:, :, :], pick[:, :, :], 1.0, -NEG, ALU.subtract, ALU.mult).then_inc(s_sel, 1)
                dve.wait_ge(s_sel, i - 1)

            def add_bias(u, b):
                i, g = divmod(u, 4)
                r, k, n = b // 2, 8 * u + b, unit_step(u, b)
                c = k % 8
                ps = s_ps[n % 2]
                dve.wait_ge(s_scores, n + 1)
                if u >= 2 and b == 0:
                    dve.wait_ge(s_tr, first_pt[u - 1])
                h = 4 * g + r
                if b % 2 or i < 2:
                    if b % 2:
                        lo = max(0, 2 - i) * P
                        out, keys = p_win[u % 2][:, r, lo:3 * P], 3 * P - lo
                    else:
                        keys = (i + 1) * P
                        out = p_slc[u % 2][:, r, 0:keys]
                    dve.tensor_tensor_reduce(out, ps[:, 0:keys], win[:, h, 3 * P - keys:3 * P], 1.0, LOWEST,
                                             ALU.add, ALU.max, mx[:, c, 0:1]).then_inc(s_sread, 1)
                    dve.wait_ge(s_sread, n + 1)
                    dve.tensor_scalar(neg_max[:, c:c + 1], mx[:, c, 0:1], -1.0, None, ALU.mult).then_inc(s_negmax, 1)
                else:
                    far = (i - 1) * P
                    out = p_slc[u % 2][:, r, :]
                    chain.step(dve.tensor_tensor_reduce(
                        out[:, 0:far].rearrange("p (b c) -> p b c", c=DH), ps[:, 0:far].rearrange("p (b c) -> p b c", c=DH),
                        bc(sel[i % 2][:, g, 0:2 * i - 2], DH), 1.0, LOWEST, ALU.add, ALU.max, mx[:, c, 0:1]))
                    m = (u - 8) * R + r
                    dve.wait_ge(s_near, m + 1)
                    dve.tensor_tensor_reduce(out[:, far:far + 2 * P], ps[:, far:far + 2 * P], near[m % 2][:, :], 1.0, LOWEST,
                                             ALU.add, ALU.max, mx[:, c, 1:2]).then_inc(s_sread, 1)
                    dve.wait_ge(s_sread, n + 1)
                    dve.tensor_scalar(neg_max[:, c:c + 1], mx[:, c, 0:1], mx[:, c, 1:2], -1.0, ALU.max, ALU.mult
                                      ).then_inc(s_negmax, 1)

            for i in range(TILES):
                compressed(i)
                for g in range(N_KV):
                    u = 4 * i + g
                    for b in range(8):
                        add_bias(u, b)
                        if b or g:
                            finish(8 * u + b - 1)
                        if u:
                            for m in part(u - 1, b):
                                if m % 2:
                                    copy_pt(m)
            finish(8 * 4 * TILES - 1)
            for b in range(8):
                for m in part(4 * TILES - 1, b):
                    if m % 2:
                        copy_pt(m)

        @block.tensor
        def _(pe):
            pe.wait_ge(s_const, 64)

            def free_scores(n):
                if n >= 2:
                    pe.wait_ge(s_sread, n - 1)

            def cmp_scores(i, g):
                n = cmp_step(i, g)
                free_scores(n)
                for r in range(R):
                    last = pe.matmul(s_ps[n % 2][:, r * P:(r + 1) * P], qt[i % 2][:, 4 * g + r, :].bitcast(F32), kct[:, g, :],
                                     start=True, stop=True)
                last.then_inc(s_scores, 1)

            def scores(u, b):
                i, g = divmod(u, 4)
                n = unit_step(u, b)
                free_scores(n)
                q = qt[i % 2][:, 4 * g + b // 2, :]
                t0 = max(0, i - 2) * P if b % 2 else 0
                for c0 in range(t0, (i + 1) * P, 512):
                    c1 = min(c0 + 512, (i + 1) * P)
                    for hl in range(2):
                        last = pe.matmul(s_ps[n % 2][:, c0 - t0:c1 - t0], q, kt[:, 4 * (b % 2) + g, hl, c0:c1],
                                         start=(hl == 0), stop=(hl == 1))
                last.then_inc(s_scores, 1)

            def of(m):
                u = max(x for x in range(4 * TILES) if first_pt[x] <= m)
                return u, key_tiles(u)[m - first_pt[u]]

            def transpose_p(m):
                u, (branch, col, t) = of(m)
                i, g = divmod(u, 4)
                if branch == "cmp":
                    pe.wait_ge(s_cscaled, i + 1)
                    pe.wait_ge(s_scaled, 8 * u + 8)
                if m >= 2:
                    pe.wait_ge(s_pt_dve if m % 2 else s_pt_act, m // 2)
                for r in range(R):
                    if branch == "cmp":
                        last = pe.transpose(t_ps[m % 2][0:NBL, r, :], p_cmp[i % 2][:, 4 * g + r, :], ident)
                    else:
                        p = (p_win if branch == "win" else p_slc)[u % 2]
                        last = pe.transpose(t_ps[m % 2][:, r, :], p[:, r, col:col + P], ident)
                last.then_inc(s_tr, 1)

            def values(m):
                u, (branch, col, t) = of(m)
                g = u % 4
                pe.wait_ge(s_pt_dve if m % 2 else s_pt_act, m // 2 + 1)
                start, stop = m == first_pt[u], m + 1 == first_pt[u + 1]
                if start and u >= 2:
                    pe.wait_ge(s_oevac, u - 1)
                rows = NBL if branch == "cmp" else P
                v = vc[:, g, :] if branch == "cmp" else (vw if branch == "win" else vs)[:, t, g * DH:(g + 1) * DH]
                for parity in range(2):
                    last = pe.matmul(o_ps[u % 2][parity * DH:(parity + 1) * DH, 0:2 * P].rearrange("p (a q) -> p a q", a=2), v,
                                     pt[m % 4][0:rows, parity:R:2, :], start=start, stop=stop)
                last.then_inc(s_pv, 1)

            def values_part(u, b):
                for m in part(u, b):
                    transpose_p(m)
                    if m:
                        values(m - 1)

            for i in range(TILES):
                pe.wait_ge(s_qt[i % 2], 16 * (i // 2 + 1))
                for g in range(N_KV):
                    cmp_scores(i, g)
                for g in range(N_KV):
                    u = 4 * i + g
                    for b in range(8):
                        scores(u, b)
                        if u:
                            values_part(u - 1, b)
            for b in range(8):
                values_part(4 * TILES - 1, b)
            values(first_pt[-1] - 1)


def split_rows(nc, src, xt_hi, xt_lo):
    with ExitStack() as ctx:
        new_semaphore = ctx.enter_context(phase_semaphores(nc))
        raw = [ctx.enter_context(nc.sbuf_tensor(f"split_raw{s}", [P, SEQ], F32)) for s in range(2)]
        s_in = [new_semaphore(f"split_in{s}") for s in range(2)]
        s_hi, s_lo = (new_semaphore(f"split_{n}") for n in ("hi", "lo"))
        block = ctx.enter_context(nc.Block())

        @block.sync
        def _(sp):
            for k in range(KT):
                if k >= 2:
                    sp.wait_ge(s_lo, k - 1)
                sp.dma_start(raw[k % 2][:, :], src[:, k, :]).then_inc(s_in[k % 2], 16)

        @block.scalar
        def _(act):
            for k in range(KT):
                act.wait_ge(s_in[k % 2], 16 * (k // 2 + 1))
                act.copy(xt_hi[:, k, :], raw[k % 2][:, :]).then_inc(s_hi, 1)

        @block.vector
        def _(dve):
            for k in range(KT):
                dve.wait_ge(s_hi, k + 1)
                dve.tensor_tensor(xt_lo[:, k, :], raw[k % 2][:, :], xt_hi[:, k, :], ALU.subtract).then_inc(s_lo, 1)


def route(nc, logits, consts, before, token_ids, slots, weights, jobs, slot_tokens):
    E2 = 2 * N_EXP
    NR = MAX_JOBS + 1
    with ExitStack() as ctx:
        new_semaphore = ctx.enter_context(phase_semaphores(nc))
        def sb(n, shape, dt=F32):
            return ctx.enter_context(nc.sbuf_tensor(f"route_{n}", shape, dt))

        def sem(n):
            return new_semaphore(f"route_{n}")

        te = [P, TILES, N_EXP]
        con = sb("con", [P, ROUTE_CONSTS])
        lower, ones = sb("lower", [P, P]), sb("ones", [P, P])
        ids, zero = sb("ids", [P, TILES], I32), sb("zero", [P, SLOT_TILES], I32)
        rest, hit, tmp = sb("rest", te), sb("hit", te), sb("tmp", te)
        first, second, both = sb("first", te), sb("second", te), sb("both", te)
        top = [sb(f"top{s}", [P, TILES]) for s in range(2)]
        low, ratio = sb("low", [P, TILES]), sb("ratio", [P, TILES])
        ahead = sb("ahead", te)
        counts = sb("counts", te)
        total = sb("total", [P, N_EXP])
        cube = sb("cube", [P, N_EXP, N_EXP])
        tiles, base, odd = sb("tiles", [P, N_EXP]), sb("base", [P, N_EXP]), sb("odd", [P, N_EXP])
        slot_f = sb("slot_f", [P, 2, TILES])
        have, left, field = sb("have", [P, N_EXP, 2]), sb("left", [P, N_EXP, 2]), sb("field", [P, 3, N_EXP, 2])
        order, square = sb("order", [P, E2]), sb("square", [P, E2, E2])
        at, pick = sb("at", [P, NR, E2]), sb("pick", [P, NR, E2])
        records = sb("records", [P, 64])
        c_ps = ctx.enter_context(nc.psum_tensor("route_c", te, F32))
        r_ps = ctx.enter_context(nc.psum_tensor("route_r", te, F32))
        s_in, s_one, s_both, s_mm, s_chain, s_low, s_exp, s_slots, s_zero, s_zeroed, s_scatter, s_jobs = (
            sem(n) for n in ("in", "one", "both", "mm", "chain", "low", "exp", "slots", "zero", "zeroed", "scatter", "jobs"))
        block = ctx.enter_context(nc.Block())

        def const(name):
            a, n = ROUTE_AT[name]
            return con[:, a:a + n]

        @block.sync
        def _(sp):
            sp.dma_start(con[:, :], consts).then_inc(s_in, 16)
            sp.dma_start(lower[:, :], before).then_inc(s_in, 16)
            sp.dma_start(ids[:, :], token_ids).then_inc(s_in, 16)
            sp.wait_ge(s_zero, 1)
            sp.dma_start(slot_tokens.rearrange("(p s) a -> p (s a)", p=P), zero[:, :]).then_inc(s_zeroed, 16)

        @block.gpsimd
        def _(pool):
            pool.memset(zero[:, :], 0).then_inc(s_zero, 1)
            pool.memset(ones[:, :], 1.0).then_inc(s_one, 1)
            pool.wait_ge(s_zeroed, 16)
            pool.wait_ge(s_in, 48)
            pool.wait_ge(s_slots, 1)
            for i in range(TILES):
                for choice in range(2):
                    pool.indirect_dma_start(out=slot_tokens, out_offset=bass.IndirectOffsetOnAxis(ap=slots[:, choice, i:i + 1], axis=0),
                                            in_=ids[:, i:i + 1], in_offset=None).then_inc(s_scatter, 16)
            pool.wait_ge(s_scatter, 16 * 2 * TILES)

        @block.scalar
        def _(act):
            act.wait_ge(s_low, 1)
            act.activation(ratio[:, :], low[:, :], ACT.Exp).then_inc(s_exp, 1)

        @block.tensor
        def _(pe):
            pe.wait_ge(s_in, 48)
            pe.wait_ge(s_one, 1)
            pe.wait_ge(s_both, 1)
            pe.matmul(c_ps[:, :, :], ones[:, :], both[:, :, :], start=True, stop=True).then_inc(s_mm, 1)
            pe.matmul(r_ps[:, :, :], lower[:, :], both[:, :, :], start=True, stop=True).then_inc(s_mm, 1)

        @block.vector
        def _(dve):
            chain = Chain(dve, s_chain, 0)

            def do(out, a, b, op):
                chain.step(dve.tensor_tensor(out, a, b, op))

            def last(ap, n):
                return ap.rearrange("p (m a) -> p m a", a=1).to_broadcast([P, ap.shape[1], n])

            def mid(ap, n):
                return ap.rearrange("p (a m) -> p a m", a=1).to_broadcast([P, n, ap.shape[1]])

            def reduce(out, a, op=ALU.add):
                chain.step(dve.tensor_reduce(out, a, AX.X, op))

            def best(out, values, top):
                reduce(top, values, ALU.max)
                do(hit[:, :, :], values, last(top, N_EXP), ALU.is_equal)
                do(hit[:, :, :], hit[:, :, :], mid(const("down"), TILES), ALU.mult)
                reduce(low[:, :], hit[:, :, :], ALU.max)
                do(out, hit[:, :, :], last(low[:, :], N_EXP), ALU.is_equal)

            dve.wait_ge(s_in, 48)
            best(first[:, :, :], logits[:, :, :], top[0][:, :])
            chain.step(dve.scalar_tensor_tensor(out=rest[:, :, :], in0=first[:, :, :], scalar=LOWEST, in1=logits[:, :, :],
                                                op0=ALU.mult, op1=ALU.add))
            best(second[:, :, :], rest[:, :, :], top[1][:, :])
            dve.tensor_tensor(both[:, :, :], first[:, :, :], second[:, :, :], ALU.add).then_inc(s_both, 1)
            dve.tensor_tensor(low[:, :], top[1][:, :], top[0][:, :], ALU.subtract).then_inc(s_low, 1)
            dve.wait_ge(s_exp, 1)
            chain.step(dve.tensor_scalar(low[:, :], ratio[:, :], 1.0, None, ALU.add))
            chain.step(dve.reciprocal(weights[:, 0, :], low[:, :]))
            do(weights[:, 1, :], weights[:, 0, :], ratio[:, :], ALU.mult)

            dve.wait_ge(s_mm, 2)
            chain.step(dve.tensor_copy(counts[:, :, :], c_ps[:, :, :]))
            chain.step(dve.memset(ahead[:, 0, :], 0.0))
            for i in range(1, TILES):
                do(ahead[:, i, :], ahead[:, i - 1, :], counts[:, i - 1, :], ALU.add)
            do(total[:, :], ahead[:, TILES - 1, :], counts[:, TILES - 1, :], ALU.add)
            do(ahead[:, :, :], r_ps[:, :, :], ahead[:, :, :], ALU.add)

            do(cube[:, :, :], last(total[:, :], TILES), mid(const("starts"), N_EXP), ALU.is_gt)
            reduce(tiles[:, :], cube[:, :, :])
            chain.step(dve.tensor_scalar(odd[:, :], tiles[:, :], 1.0, None, ALU.is_equal))
            chain.step(dve.scalar_tensor_tensor(out=odd[:, :], in0=tiles[:, :], scalar=CAP + 1.0, in1=odd[:, :],
                                                op0=ALU.is_equal, op1=ALU.add))
            do(tiles[:, :], tiles[:, :], odd[:, :], ALU.add)
            prior = const("prior").rearrange("p (a b) -> p a b", b=E2)
            do(cube[:, :, :], mid(tiles[:, :], N_EXP), prior[:, 0:N_EXP, 0:N_EXP], ALU.mult)
            reduce(base[:, :], cube[:, :, :])

            chain.step(dve.scalar_tensor_tensor(out=ahead[:, :, :], in0=mid(base[:, :], TILES), scalar=float(P), in1=ahead[:, :, :],
                                                op0=ALU.mult, op1=ALU.add))
            for choice, hot in enumerate((first, second)):
                do(tmp[:, :, :], hot[:, :, :], ahead[:, :, :], ALU.mult)
                reduce(slot_f[:, choice, :], tmp[:, :, :])
            dve.tensor_copy(slots[:, :, :], slot_f[:, :, :]).then_inc(s_slots, 1)

            do(left[:, :, :], last(tiles[:, :], 2), const("skip").rearrange("p (e c) -> p e c", c=2), ALU.subtract)
            chain.step(dve.tensor_scalar(have[:, :, :], left[:, :, :], 0.0, None, ALU.is_gt))
            do(square[:, :, :], mid(have[:, :, :].rearrange("p e c -> p (e c)"), E2), prior, ALU.mult)
            reduce(order[:, :], square[:, :, :])
            do(at[:, :, :], mid(order[:, :], NR), last(const("record"), E2), ALU.is_equal)
            do(at[:, :, :], at[:, :, :], mid(have[:, :, :].rearrange("p e c -> p (e c)"), NR), ALU.mult)
            chain.step(dve.tensor_copy(field[:, 0, :, :], const("expert").rearrange("p (e c) -> p e c", c=2)))
            do(field[:, 1, :, :], last(base[:, :], 2), const("skip").rearrange("p (e c) -> p e c", c=2), ALU.add)
            chain.step(dve.tensor_scalar(field[:, 2, :, :], left[:, :, :], float(CAP), None, ALU.min))
            chain.step(dve.memset(records[:, :], 0.0))
            for f in range(3):
                do(pick[:, :, :], at[:, :, :], mid(field[:, f, :, :].rearrange("p e c -> p (e c)"), NR), ALU.mult)
                reduce(records[:, f:f + E_REC * (NR - 1) + 1:E_REC], pick[:, :, :])
            reduce(records[:, JOB_COUNT_AT:JOB_COUNT_AT + 1], have[:, :, :].rearrange("p e c -> p (e c)"))
            dve.tensor_copy(jobs[0:1, :], records[0:1, :]).then_inc(s_jobs, 1)


def combine(nc, x, y, slots, weights, out):
    with ExitStack() as ctx:
        new_semaphore = ctx.enter_context(phase_semaphores(nc))
        S = 3
        xt, y1, y2 = ([ctx.enter_context(nc.sbuf_tensor(f"comb_{n}{s}", [P, D], F32)) for s in range(S)] for n in ("x", "y1", "y2"))
        s_x = [new_semaphore(f"comb_x{s}") for s in range(S)]
        s_y = [new_semaphore(f"comb_y{s}") for s in range(S)]
        s_out = [new_semaphore(f"comb_out{s}") for s in range(S)]
        s_sum = new_semaphore("comb_sum")
        block = ctx.enter_context(nc.Block())

        @block.sync
        def _(sp):
            for i in range(TILES):
                s = i % S
                if i >= S:
                    sp.wait_ge(s_out[s], 16 * (i // S))
                sp.dma_start(xt[s][:, :], x[i * P:(i + 1) * P, :]).then_inc(s_x[s], 16)

        @block.gpsimd
        def _(pool):
            for i in range(TILES):
                s = i % S
                if i >= S:
                    pool.wait_ge(s_sum, 2 * (i - S) + 2)
                for choice, yt in enumerate((y1, y2)):
                    pool.indirect_dma_start(out=yt[s][:, :], out_offset=None, in_=y,
                                            in_offset=bass.IndirectOffsetOnAxis(ap=slots[:, choice, i:i + 1], axis=0)
                                            ).then_inc(s_y[s], 16)

        @block.vector
        def _(dve):
            for i in range(TILES):
                s = i % S
                dve.wait_ge(s_x[s], 16 * (i // S + 1))
                dve.wait_ge(s_y[s], 32 * (i // S + 1))
                for choice, yt in enumerate((y1, y2)):
                    dve.scalar_tensor_tensor(out=xt[s][:, :], in0=yt[s][:, :], scalar=weights[:, choice, i:i + 1], in1=xt[s][:, :],
                                             op0=ALU.mult, op1=ALU.add).then_inc(s_sum, 1)
                    dve.wait_ge(s_sum, 2 * i + choice + 1)

        @block.scalar
        def _(act):
            for i in range(TILES):
                s = i % S
                act.wait_ge(s_sum, 2 * i + 2)
                act.dma_start(out[i * P:(i + 1) * P, :], xt[s][:, :]).then_inc(s_out[s], 16)
            for s in range(S):
                act.wait_ge(s_out[s], 16 * len(range(s, TILES, S)))


def trunk(nc, x, onehot, rel_bias, gain_mix0, gain_ffn0, gain_ffn1, pool_w, pool_scale, chunk_gains, w_kvq, k_gains,
          cmp_pos, cmp_w1, cmp_w2, w_o, ffn_wgu, ffn_wd, router, moe_wgu, moe_wd, bands, identity, win_mask,
          sel_const, row_valid, route_const, before, token_ids, ffn_jobs, out):
    def dram(name, shape, dt=F32):
        return nc.dram_tensor(name, shape, dt, kind="Internal").ap()

    x_mid, h_ffn, y_ffn, x1 = (dram(n, [SEQ, D]) for n in ("x_mid", "h_ffn", "y_ffn", "x1"))
    qkv = dram("qkv", [SEQ, 6 * 512])
    qt_dram = dram("qt", [SEQ, N_HEADS * P])
    bias_vec = dram("bias_vec_rows", [N_HEADS, VEC])
    ot_dram = dram("ot_rows", [P, KT, SEQ])
    att_out, x2, h_moe = (dram(n, [SEQ, D]) for n in ("att_out", "x2", "h_moe"))
    slot_tokens = dram("slot_tokens", [SLOT_TILES * P, 1], I32)
    y_moe = dram("y_moe", [SLOT_TILES * P, D])

    with ExitStack() as whole:
        def sb(stack, name, shape, dt=F32):
            return stack.enter_context(nc.sbuf_tensor(name, shape, dt))

        ident_t = sb(whole, "ident", [P, P])
        ident = ident_t[:, :]
        dense_jobs = sb(whole, "dense_jobs", [1, 64], I32)
        zeros = sb(whole, "zeros", [P, D // 4])
        s_zeros, s_y_zeroed = nc.alloc_semaphore("zeros"), nc.alloc_semaphore("y_zeroed")
        k_gain_dram = dram("k_gain_dram", [1, (2 * N_KV + 1) * DH])
        with ExitStack() as first:
            gk, gq = (sb(first, n, [1, (2 * N_KV + 1) * DH]) for n in ("gk", "gq"))
            s_ident, s_gains, s_product = (nc.alloc_semaphore(n) for n in ("ident_loaded", "gains_loaded", "gains_product"))
            with nc.Block() as block:
                @block.sync
                def _(sp):
                    sp.dma_start(gk[:, :], k_gains[0:1, :]).then_inc(s_gains, 16)
                    sp.dma_start(gq[:, :], k_gains[1:2, :]).then_inc(s_gains, 16)
                    sp.dma_start(ident, identity).then_inc(s_ident, 16)
                    sp.dma_start(dense_jobs[:, :], ffn_jobs).then_inc(s_ident, 16)
                    sp.wait_ge(s_product, 1)
                    sp.dma_start(k_gain_dram, gk[:, :]).then_inc(s_ident, 16)
                    sp.wait_ge(s_ident, 48)

                @block.gpsimd
                def _(pool):
                    pool.memset(zeros[:, :], 0.0).then_inc(s_zeros, 1)

                @block.scalar
                def _(act):
                    act.wait_ge(s_zeros, 1)
                    act.dma_start(y_moe.rearrange("(p s) (a d) -> p (s a) d", p=P, a=4),
                                  zeros[:, :].rearrange("p (a d) -> p a d", a=1).to_broadcast([P, 4 * SLOT_TILES, D // 4])
                                  ).then_inc(s_y_zeroed, 16)

                @block.vector
                def _(dve):
                    dve.wait_ge(s_gains, 32)
                    dve.scalar_tensor_tensor(out=gk[:, :], in0=gk[:, :], scalar=DH ** -0.5, in1=gq[:, :],
                                             op0=ALU.mult, op1=ALU.mult).then_inc(s_product, 1)

        pool_mixer(nc, x, gain_mix0, gain_ffn0, pool_scale, pool_w, bands, x_mid, h_ffn)

        def dense_rows(pool, j, base, stage, ids, s_ids, s_rows):
            for t in range(CAP):
                pool.dma_start(stage[:, t, :], h_ffn[bass.ds((base + t) * P, P), :]).then_inc(s_rows, 16)
        swiglu_jobs(nc, "ffn", ffn_wgu, ffn_wd, dense_jobs, SEQ // (CAP * P), dense_rows,
                    y_ffn.rearrange("(s p) d -> p s d", p=P), ident, (CAP,))

        with ExitStack() as att:
            with ExitStack() as proj:
                xt_hi, xt_lo = (sb(proj, f"xt_{n}", [P, KT, SEQ], F32R) for n in ("hi", "lo"))
                add_norm(nc, "kvn", x_mid, y_ffn, None, x1, None, ident, xt_hi, xt_lo)
                project(nc, "kvq", xt_hi, xt_lo, w_kvq, chunk_gains, 6, qkv)
            kt = sb(att, "kt", [P, 2 * N_KV, 2, SEQ], F32R)
            gates = sb(att, "gates", [P, TILES, 3 * N_HEADS])
            kct = sb(att, "kct", [P, N_KV, P])
            vc = sb(att, "vc", [P // 2, N_KV, DH])
            win = sb(att, "win", [P, N_HEADS, 3 * P])
            cmpb = sb(att, "cmpb", [P, N_HEADS, CB])
            split_heads(nc, qkv, k_gain_dram[:, 0:2 * N_KV * DH], ident, kt, qt_dram, gates)
            compress_keys(nc, qkv, cmp_pos, cmp_w1, cmp_w2, k_gain_dram[:, 2 * N_KV * DH:(2 * N_KV + 1) * DH], ident, kct, vc)
            bias_tables(nc, rel_bias, onehot, win_mask, bias_vec, win, cmpb)
            attend(nc, qkv, qt_dram, kt, kct, vc, gates, win, cmpb, sel_const, row_valid, ident, ot_dram)

        with ExitStack() as proj:
            xt_hi, xt_lo = (sb(proj, f"ot_{n}", [P, KT, SEQ], F32R) for n in ("hi", "lo"))
            split_rows(nc, ot_dram, xt_hi, xt_lo)
            project(nc, "wo", xt_hi, xt_lo, w_o, None, 2, att_out)

        logits = sb(whole, "logits", [P, TILES, N_EXP])
        slots = sb(whole, "slots", [P, 2, TILES], U32)
        weights = sb(whole, "weights", [P, 2, TILES])
        jobs = sb(whole, "jobs", [1, 64], I32)
        add_norm(nc, "moen", x1, att_out, gain_ffn1, x2, h_moe, ident, router=router, logits=logits)
        route(nc, logits, route_const, before, token_ids, slots, weights, jobs, slot_tokens)

        def expert_rows(pool, j, base, stage, ids, s_ids, s_rows):
            with nc.allow_non_contiguous_dma(reason="one token number a partition and tile"):
                pool.dma_start(ids[:, :], slot_tokens.rearrange("(s p) a -> p (s a)", p=P)[:, bass.ds(base, CAP)].bitcast(U32)
                               ).then_inc(s_ids, 16)
            pool.wait_ge(s_ids, j * 16 + 16)
            pool.sem_inc(s_ids_seen, 1)
            for t in range(CAP):
                pool.indirect_dma_start(out=stage[:, t, :], out_offset=None, in_=h_moe,
                                        in_offset=bass.IndirectOffsetOnAxis(ap=ids[:, t:t + 1], axis=0)).then_inc(s_rows, 16)
        s_ids_seen = nc.alloc_semaphore("ids_seen")
        with nc.Block() as block:
            @block.sync
            def _(sp):
                sp.wait_ge(s_y_zeroed, 16)
        swiglu_jobs(nc, "moe", moe_wgu, moe_wd, jobs, jobs[0:1, JOB_COUNT_AT:JOB_COUNT_AT + 1], expert_rows,
                    y_moe.rearrange("(s p) d -> p s d", p=P), ident, (2, 3, CAP))
        combine(nc, x2, y_moe, slots, weights, out)


_INS = ["x", "onehot", "rel_bias", "gain_mix0", "gain_ffn0", "gain_ffn1", "pool_w", "pool_scale", "chunk_gains", "w_kvq",
        "k_gains", "cmp_pos", "cmp_w1", "cmp_w2", "w_o", "ffn_wgu", "ffn_wd", "router", "moe_wgu", "moe_wd", "bands",
        "identity", "win_mask", "sel_const", "row_valid", "route_const", "before", "token_ids", "ffn_jobs"]


def rel_bucket(dist):
    import math
    import numpy as np
    n = np.maximum(dist, 0)
    exact = N_BUCKETS // 2
    nf = np.maximum(n, 1).astype(np.float32)
    large = exact + (np.log(nf / np.float32(exact)) / np.float32(math.log(128 / exact)) * np.float32(N_BUCKETS - exact)).astype(np.int32)
    return np.where(n < exact, n, np.minimum(large, N_BUCKETS - 1))


def shape_constants():
    import numpy as np
    f = np.float32
    hot = np.zeros((N_BUCKETS + 1, VEC), f)

    def put(first, dist):
        last = N_BUCKETS - 1
        for c, (d, b) in enumerate(zip(dist, rel_bucket(dist))):
            if d < 0:
                hot[N_BUCKETS, first + c] = 1
            elif b != last:
                hot[b, first + c], hot[last, first + c] = 1, -1
    put(0, 255 - np.arange(3 * P - 1))
    for r in range(16):
        put(NEAR + r * P, r - 16 * (np.arange(P - 1) - 63) - 31)
    s, t = np.arange(P)[:, None], np.arange(P)[None, :]
    bands = np.zeros((P, 3, N_GRP, P), f)
    for g, w in enumerate((2, 4, 8, 16)):
        inside = (t - s >= 0) & (t - s < w)
        bands[:, 0, g] = inside / np.minimum(t + 1, w).astype(f) - (s == t)
        bands[:, 1, g] = inside / f(w) - (s == t)
        bands[:, 2, g] = (t + P - s < w) / f(w)
    nsb = SEQ // 64
    sel = np.zeros((P, 2 * TILES + 1, nsb), f)
    blk = np.arange(nsb)[None, :]
    for i in range(TILES):
        own = 2 * i + np.arange(P)[:, None] // 64
        sel[:, i] = np.where((blk >= 1) & (blk <= own - 2), 0, -8)
        sel[:, TILES + i] = (blk == 0) | (blk == own) | (blk == own - 1)
    sel[:, 2 * TILES] = nsb - np.arange(nsb)
    e2 = 2 * N_EXP
    route = {
        "down": N_EXP - np.arange(N_EXP), "starts": P * np.arange(TILES),
        "prior": (np.arange(e2)[None, :] < np.arange(e2)[:, None]).ravel(),
        "record": np.arange(MAX_JOBS + 1), "expert": np.repeat(np.arange(N_EXP), 2), "skip": np.tile([0, CAP], N_EXP),
    }
    rc = np.zeros((P, ROUTE_CONSTS), f)
    for name, (a, n) in ROUTE_AT.items():
        rc[:, a:a + n] = route[name]
    jobs = np.zeros((1, 64), np.int32)
    for j in range(SEQ // (CAP * P)):
        jobs[0, E_REC * j:E_REC * j + 3] = (0, j * CAP, CAP)
    return {
        "onehot": hot, "bands": bands, "identity": np.eye(P, dtype=f), "win_mask": np.where(t > s, 0, NEG).astype(f),
        "sel_const": sel, "row_valid": (np.arange(P) >= 31).astype(f).reshape(P, 1), "route_const": rc,
        "before": (s < t).astype(f), "token_ids": (np.arange(TILES)[None, :] * P + np.arange(P)[:, None]).astype(np.int32),
        "ffn_jobs": jobs,
    }


def kernel(x, rel_bias, norm_mix, norm_ffn, pool_w, pool_scale, norm_kv, w_kv, g_k, cmp_pos, cmp_w1, cmp_w2, w_qg, g_q,
           w_o, ffn_wg, ffn_wu, ffn_wd, router, moe_wg, moe_wu, moe_wd):
    import numpy as np
    import concourse.bacc as bacc
    from concourse.bass_utils import run_bass_kernel_spmd

    def chunked(w):
        n = w.shape[1] // 512
        return w.reshape(KT, P, n, 512).transpose(2, 1, 0, 3).reshape(n * P, KT * 512)

    def gate_up(wg, wu):
        w = np.stack([wg, wu], 1).reshape(-1, 2, KT, P, MT, P)
        return w.transpose(0, 4, 3, 1, 2, 5).reshape(-1, 2 * D)

    a = {k: np.asarray(v) for k, v in dict(
        x=x, rel_bias=rel_bias, norm_mix=norm_mix, norm_ffn=norm_ffn, pool_w=pool_w, pool_scale=pool_scale, norm_kv=norm_kv,
        w_kv=w_kv, g_k=g_k, cmp_pos=cmp_pos, cmp_w1=cmp_w1, cmp_w2=cmp_w2, w_qg=w_qg, g_q=g_q, w_o=w_o, ffn_wg=ffn_wg,
        ffn_wu=ffn_wu, ffn_wd=ffn_wd, router=router, moe_wg=moe_wg, moe_wu=moe_wu, moe_wd=moe_wd).items()}
    w_all = np.concatenate([a["w_kv"], a["w_qg"][0], np.zeros((D, 6 * 512 - 1536 - 1072), np.float32)], 1)
    gains = np.stack([a["norm_kv"]] * 3 + [a["norm_mix"][1]] * 3)
    arrays = {
        "x": a["x"].reshape(SEQ, D), "rel_bias": a["rel_bias"], "gain_mix0": a["norm_mix"][0:1], "gain_ffn0": a["norm_ffn"][0:1],
        "gain_ffn1": a["norm_ffn"][1:2], "pool_w": a["pool_w"][0], "pool_scale": a["pool_scale"][0:1],
        "chunk_gains": gains.reshape(6, KT, P).transpose(2, 0, 1), "w_kvq": chunked(w_all),
        "k_gains": np.stack([np.concatenate([a["g_k"][1]] * N_KV + [a["g_k"][2]] * N_KV + [a["g_k"][0]]),
                             np.concatenate([a["g_q"][0]] * (2 * N_KV + 1))]),
        "cmp_pos": a["cmp_pos"].reshape(2, 16, P).transpose(2, 0, 1), "cmp_w1": a["cmp_w1"], "cmp_w2": a["cmp_w2"],
        "w_o": chunked(a["w_o"][0]), "ffn_wgu": gate_up(a["ffn_wg"], a["ffn_wu"]), "ffn_wd": a["ffn_wd"].reshape(-1, D),
        "router": a["router"][0], "moe_wgu": gate_up(a["moe_wg"][0], a["moe_wu"][0]), "moe_wd": a["moe_wd"].reshape(-1, D),
        **shape_constants(),
    }
    nc = bacc.Bacc("TRN2", target_bir_lowering=False, num_devices=1)
    ins, args = {}, []
    for name in _INS:
        v = np.ascontiguousarray(arrays[name])
        ins[f"in_{name}"] = v
        args.append(nc.dram_tensor(f"in_{name}", v.shape, mybir.dt.from_np(v.dtype), kind="ExternalInput").ap())
    out = nc.dram_tensor("out_x", [SEQ, D], F32, kind="ExternalOutput").ap()
    trunk(nc, *args, out)
    r = run_bass_kernel_spmd(nc, [ins], core_ids=[0])
    return r.results[0]["out_x"].reshape(1, SEQ, D)
```

```python
import concourse.bass as bass
from concourse import mybir
from contextlib import ExitStack, contextmanager

F32, F32R, I32, U32 = mybir.dt.float32, mybir.dt.float32r, mybir.dt.int32, mybir.dt.uint32
ALU, ACT, AX = mybir.AluOpType, mybir.ActivationFunctionType, mybir.AxisListType

SEQ, TILES, EPS = 1024, 8, 1e-6
N_GRP, GRP = 4, 256
N_EXP = 8
N_HEADS, N_KV, DH = 16, 4, 64
N_BUCKETS = 32
NEG, LOWEST = -1e30, -3.0e38
NEAR, CB = 384, 120
VEC = NEAR + 16 * 128
MAX_JOBS, JOB_COUNT_AT = 12, 56
ROUTE_AT, ROUTE_CONSTS = {}, 0
for _name, _len in (("down", N_EXP), ("starts", TILES), ("prior", 4 * N_EXP * N_EXP), ("record", MAX_JOBS + 1),
                    ("expert", 2 * N_EXP), ("skip", 2 * N_EXP)):
    ROUTE_AT[_name] = (ROUTE_CONSTS, _len)
    ROUTE_CONSTS += _len


@contextmanager
def phase_semaphores(nc):
    taken = []

    def new(name):
        taken.append(nc.alloc_semaphore(name))
        return taken[-1]
    yield new
    nc.clear_and_free_semaphores(taken)
    nc.all_engine_barrier()


P = 128
D = 1024
KT = D // P
FF = 3584
MT = FF // P
GROUP = 2
NG = MT // GROUP
CAP = 4
SLOT_TILES = 32
E_REC = 4


def swiglu_jobs(nc, name, wgu, wd, jobs, n_jobs, gather, y_rows, ident, widths):
    with ExitStack() as ctx:
        new_semaphore = ctx.enter_context(phase_semaphores(nc))

        def sb(n, shape, dt=F32):
            return ctx.enter_context(nc.sbuf_tensor(f"{name}_{n}", shape, dt))

        def sem(n):
            return new_semaphore(f"{name}_{n}")

        stage = sb("stage", [P, CAP, D])
        ids = sb("ids", [P, CAP], mybir.dt.uint32)
        gu_raw = [sb(f"gu_raw{s}", [P, 2 * D]) for s in range(2)]
        gu_hi = [sb(f"gu_hi{s}", [P, 2, KT, P], F32R) for s in range(2)]
        gu_lo = [sb(f"gu_lo{s}", [P, 2, KT, P], F32R) for s in range(2)]
        wd_raw = sb("wd_raw", [P, GROUP, D])
        wd_hi = [sb(f"wd_hi{s}", [P, GROUP, D], F32R) for s in range(2)]
        wd_lo = [sb(f"wd_lo{s}", [P, GROUP, D], F32R) for s in range(2)]
        act_gate = [sb(f"act_gate{s}", [P, CAP * P]) for s in range(2)]
        hid = [sb(f"hid{s}", [P, CAP * P]) for s in range(2)]
        hid_hi = [sb(f"hid_hi{s}", [P, GROUP, CAP * P], F32R) for s in range(2)]
        hid_lo = [sb(f"hid_lo{s}", [P, GROUP, CAP * P], F32R) for s in range(2)]
        ht_hi = sb("ht_hi", [P, KT, CAP * P], F32R)
        ht_lo = sb("ht_lo", [P, KT, CAP * P], F32R)
        yacc = sb("yacc", [P, CAP, D])
        ps = [ctx.enter_context(nc.psum_tensor(f"{name}_ps{b}", [P, 512], F32)) for b in range(8)]
        gate_ps, up_ps, y_ps = ps[0:4:2], ps[1:4:2], ps[4:8]

        s_gu_loaded = [sem(f"gu_loaded{s}") for s in range(2)]
        s_wd_loaded = sem("wd_loaded")
        s_gu_hi, s_gu_lo = sem("gu_hi_done"), sem("gu_lo_done")
        s_wd_hi, s_wd_lo = sem("wd_hi_done"), sem("wd_lo_done")
        s_gate, s_gu = sem("gate_done"), sem("gu_done")
        s_silu, s_hid, s_hhi, s_hlo = sem("silu_done"), sem("hid_done"), sem("hid_hi_done"), sem("hid_lo_done")
        s_yready, s_yadded = sem("y_ready"), sem("y_added")
        s_zeroed, s_stored, s_store_seen = sem("yacc_zeroed"), sem("y_stored"), sem("store_seen")
        s_ids, s_rows = sem("ids_loaded"), sem("rows_loaded")
        s_tr, s_tr_hi, s_tr_lo = sem("tr_done"), sem("tr_hi_done"), sem("tr_lo_done")

        block = ctx.enter_context(nc.Block())

        def job_count(eng):
            return n_jobs if isinstance(n_jobs, int) else eng.value_load(n_jobs, min_val=2, max_val=12)

        def field(eng, j, f, lo, hi):
            return eng.value_load(jobs[0:1, bass.ds(j * E_REC + f, 1)], min_val=lo, max_val=hi)

        def per_width(eng, j, body):
            if len(widths) == 1:
                body(widths[0])
                return
            tiles = field(eng, j, 2, 2, CAP)
            with eng.If(tiles == 2):
                body(2)
            with eng.Else():
                with eng.If(tiles == 3):
                    body(3)
                with eng.Else():
                    body(4)
                eng.nop()
            eng.nop()

        @block.sync
        def _(sp):
            with sp.Fori(0, job_count(sp)) as j:
                ws = field(sp, j, 0, 0, wd.shape[0] // FF - 1)
                with sp.Fori(0, NG // 2) as it:
                    for g in range(2):
                        for s in range(2):
                            n = it * 4 + (2 * g + s)
                            sp.wait_ge(s_gu_lo, j * MT + n + 1)
                            sp.dma_start(gu_raw[s][:, :], wgu[bass.ds((ws * MT + n) * P, P), :]).then_inc(
                                s_gu_loaded[s], 16)
                        q = it * 2 + g
                        sp.wait_ge(s_wd_lo, j * NG + q + 1)
                        src = wd[bass.ds((ws * NG + q) * GROUP * P, GROUP * P), :]
                        sp.dma_start(wd_raw[:, :, :], src.rearrange("(a p) d -> p a d", p=P)).then_inc(
                            s_wd_loaded, 16)

        @block.gpsimd
        def _(pool):
            pool.memset(yacc[:, :, :], 0.0).then_inc(s_zeroed, 1)

            def fetch(j):
                base = field(pool, j, 1, 0, y_rows.shape[1] - CAP)
                gather(pool, j, base, stage, ids, s_ids, s_rows)

            fetch(0)
            with pool.Fori(0, job_count(pool)) as j:
                pool.wait_ge(s_tr, j * KT + KT)
                fetch(j + 1)
                base = field(pool, j, 1, 0, y_rows.shape[1] - CAP)
                pool.wait_ge(s_yadded, j * 24 * NG + (24 + 24 * NG))

                def store(tiles):
                    pool.dma_start(y_rows[:, bass.ds(base, tiles), :], yacc[:, 0:tiles, :]).then_inc(s_stored, 16)
                per_width(pool, j, store)
                pool.wait_ge(s_stored, j * 16 + 16)
                pool.sem_inc(s_store_seen, 1)
                pool.memset(yacc[:, :, :], 0.0).then_inc(s_zeroed, 1)

        @block.scalar
        def _(act):
            def tr_hi(j1):
                for k in range(KT):
                    act.wait_ge(s_tr, j1 * KT + (k + 1))
                    act.copy(ht_hi[:, k, :], ps[k % 4][:, :]).then_inc(s_tr_hi, 1)

            tr_hi(0)
            with act.Fori(0, job_count(act)) as j:
                def job(tiles):
                    W = tiles * P

                    def silu(N, s):
                        act.wait_ge(s_gate, N + 1)
                        act.wait_ge(s_hid, N + 1)
                        act.activation(act_gate[s][:, 0:W], gate_ps[s][:, 0:W], ACT.Silu).then_inc(s_silu, 1)

                    def split(n, s):
                        N = j * MT + n
                        act.wait_ge(s_gu_loaded[s], j * (8 * MT) + (n - s) * 8 + 16)
                        act.wait_ge(s_gu, N + 1)
                        act.copy(gu_hi[s][:, :, :, :].rearrange("p a k c -> p (a k c)"), gu_raw[s][:, :]).then_inc(s_gu_hi, 1)

                    def hidhi(N, Q, s, b):
                        act.wait_ge(s_hid, N + 3)
                        act.wait_ge(s_yready, Q * 24 + 24)
                        act.copy(hid_hi[b][:, s, 0:W], hid[s][:, 0:W]).then_inc(s_hhi, 1)

                    def wdhi(q, b):
                        Q = j * NG + q
                        act.wait_ge(s_wd_loaded, Q * 16 + 16)
                        act.wait_ge(s_yready, Q * 24 + 24)
                        act.copy(wd_hi[b][:, :, :], wd_raw[:, :, :]).then_inc(s_wd_hi, 1)

                    def post_and_split(m, q, s, b, more=None):
                        silu(j * MT + m, s)
                        if more is not None:
                            split(more, s)
                        hidhi(j * MT + m, j * NG + q, s, b)

                    split(0, 0)
                    split(1, 1)
                    post_and_split(0, 0, 0, 0, 2)
                    wdhi(0, 0)
                    post_and_split(1, 0, 1, 0, 3)
                    with act.Fori(0, NG // 2 - 1) as it:
                        m = it * 4
                        post_and_split(m + 2, it * 2 + 1, 0, 1, m + 4)
                        wdhi(it * 2 + 1, 1)
                        post_and_split(m + 3, it * 2 + 1, 1, 1, m + 5)
                        post_and_split(m + 4, it * 2 + 2, 0, 0, m + 6)
                        wdhi(it * 2 + 2, 0)
                        post_and_split(m + 5, it * 2 + 2, 1, 0, m + 7)
                    post_and_split(MT - 2, NG - 1, 0, 1)
                    wdhi(NG - 1, 1)
                    post_and_split(MT - 1, NG - 1, 1, 1)
                per_width(act, j, job)
                tr_hi(j + 1)

        @block.vector
        def _(dve):
            dve.sem_inc(s_hid, 2)
            dve.sem_inc(s_yadded, 24)
            dve.sem_inc(s_gu_lo, 2)
            dve.sem_inc(s_wd_lo, 1)

            def tr_lo(j1):
                for k in range(KT):
                    dve.wait_ge(s_tr_hi, j1 * KT + (k + 1))
                    dve.tensor_tensor(ht_lo[:, k, :], ps[k % 4][:, :], ht_hi[:, k, :], ALU.subtract).then_inc(s_tr_lo, 1)

            tr_lo(0)
            with dve.Fori(0, job_count(dve)) as j:
                def job(tiles):
                    W = tiles * P
                    unit = 12 // tiles

                    def product(N, s):
                        dve.wait_ge(s_silu, N + 1)
                        dve.wait_ge(s_gu, N + 3)
                        dve.tensor_tensor(hid[s][:, 0:W], act_gate[s][:, 0:W], up_ps[s][:, 0:W], ALU.mult).then_inc(s_hid, 1)

                    def split(n, s):
                        dve.wait_ge(s_gu_hi, j * MT + n + 1)
                        dve.tensor_tensor(gu_lo[s][:, :, :, :].rearrange("p a k c -> p (a k c)"), gu_raw[s][:, :],
                                          gu_hi[s][:, :, :, :].rearrange("p a k c -> p (a k c)"),
                                          ALU.subtract).then_inc(s_gu_lo, 1)

                    def hidlo(N, s, b):
                        dve.wait_ge(s_hhi, N + 1)
                        dve.tensor_tensor(hid_lo[b][:, s, 0:W], hid[s][:, 0:W], hid_hi[b][:, s, 0:W], ALU.subtract).then_inc(s_hlo, 1)

                    def wdlo(q, b):
                        dve.wait_ge(s_wd_hi, j * NG + q + 1)
                        dve.tensor_tensor(wd_lo[b][:, :, :], wd_raw[:, :, :], wd_hi[b][:, :, :], ALU.subtract).then_inc(s_wd_lo, 1)

                    def add_y(q):
                        for u in range(2 * tiles):
                            t, h = u // 2, u % 2
                            dve.wait_ge(s_yready, (j * NG + q) * 24 + (48 + unit * (u + 1)))
                            dve.wait_ge(s_yadded, (j * NG + q) * 24 + unit * (u + 1))
                            dve.tensor_tensor(yacc[:, t, h * 512:(h + 1) * 512], yacc[:, t, h * 512:(h + 1) * 512],
                                              y_ps[u % 4][:, :], ALU.add).then_inc(s_yadded, unit)

                    def post_and_split(m, s, b, more=None):
                        product(j * MT + m, s)
                        if more is not None:
                            split(more, s)
                        hidlo(j * MT + m, s, b)

                    split(0, 0)
                    split(1, 1)
                    post_and_split(0, 0, 0, 2)
                    wdlo(0, 0)
                    dve.wait_ge(s_zeroed, j + 1)
                    post_and_split(1, 1, 0, 3)
                    with dve.Fori(0, NG // 2 - 1) as it:
                        m = it * 4
                        post_and_split(m + 2, 0, 1, m + 4)
                        wdlo(it * 2 + 1, 1)
                        add_y(it * 2)
                        post_and_split(m + 3, 1, 1, m + 5)
                        post_and_split(m + 4, 0, 0, m + 6)
                        wdlo(it * 2 + 2, 0)
                        add_y(it * 2 + 1)
                        post_and_split(m + 5, 1, 0, m + 7)
                    post_and_split(MT - 2, 0, 1)
                    wdlo(NG - 1, 1)
                    post_and_split(MT - 1, 1, 1)
                    add_y(NG - 2)
                    tr_lo(j + 1)
                    add_y(NG - 1)
                per_width(dve, j, job)

        @block.tensor
        def _(pe):
            pe.sem_inc(s_gu, 2)
            pe.sem_inc(s_yready, 48)

            def transpose_rows(j1):
                pe.wait_ge(s_rows, j1 * 16 * CAP + 16 * CAP)
                for k in range(KT):
                    if k >= 4:
                        pe.wait_ge(s_tr_lo, j1 * KT + (k - 3))
                    for t in range(CAP):
                        last = pe.transpose(ps[k % 4][:, t * P:(t + 1) * P], stage[:, t, k * P:(k + 1) * P], ident)
                    last.then_inc(s_tr, 1)

            transpose_rows(0)
            with pe.Fori(0, job_count(pe)) as j:
                def job(tiles):
                    W = tiles * P
                    unit = 12 // tiles

                    def gate_up(n, s):
                        N = j * MT + n
                        pe.wait_ge(s_gu_lo, N + 3)
                        pe.wait_ge(s_hid, N + 1)
                        for half, (out, done) in enumerate(((gate_ps[s], s_gate), (up_ps[s], s_gu))):
                            for k in range(KT):
                                pe.matmul(out[:, 0:W], gu_hi[s][:, half, k, :], ht_hi[:, k, 0:W], start=(k == 0), stop=False)
                                pe.matmul(out[:, 0:W], gu_hi[s][:, half, k, :], ht_lo[:, k, 0:W], start=False, stop=False)
                                last = pe.matmul(out[:, 0:W], gu_lo[s][:, half, k, :], ht_hi[:, k, 0:W],
                                                 start=False, stop=(k == KT - 1))
                            last.then_inc(done, 1)

                    def down(q, b):
                        Q = j * NG + q
                        pe.wait_ge(s_hlo, Q * 2 + 2)
                        pe.wait_ge(s_wd_lo, Q + 2)
                        for u in range(2 * tiles):
                            t, h = u // 2, u % 2
                            out = y_ps[u % 4][:, :]
                            pe.wait_ge(s_yadded, Q * 24 + (24 + unit * max(u - 3, 0)))
                            for a in range(GROUP):
                                rows = slice(t * P, (t + 1) * P)
                                cols = slice(h * 512, (h + 1) * 512)
                                pe.matmul(out, hid_hi[b][:, a, rows], wd_hi[b][:, a, cols], start=(a == 0), stop=False)
                                pe.matmul(out, hid_hi[b][:, a, rows], wd_lo[b][:, a, cols], start=False, stop=False)
                                last = pe.matmul(out, hid_lo[b][:, a, rows], wd_hi[b][:, a, cols],
                                                 start=False, stop=(a == GROUP - 1))
                            last.then_inc(s_yready, unit)

                    pe.wait_ge(s_tr_lo, j * KT + KT)
                    for n in range(4):
                        gate_up(n, n % 2)
                    with pe.Fori(0, NG // 2 - 1) as it:
                        m = it * 4
                        down(it * 2, 0)
                        gate_up(m + 4, 0)
                        gate_up(m + 5, 1)
                        down(it * 2 + 1, 1)
                        gate_up(m + 6, 0)
                        gate_up(m + 7, 1)
                    down(NG - 2, 0)
                    pe.wait_ge(s_hid, j * MT + MT + 2)
                    transpose_rows(j + 1)
                    down(NG - 1, 1)
                per_width(pe, j, job)


class Chain:

    def __init__(self, eng, sem, base):
        self.eng, self.sem, self.base, self.n = eng, sem, base, 0

    def step(self, instruction):
        self.n += 1
        instruction.then_inc(self.sem, 1)
        self.eng.wait_ge(self.sem, self.base + self.n)


def row_rstd(pool, chain, rstd, sums, width, minus_half):
    chain.step(pool.tensor_scalar(rstd, sums, 1.0 / width, EPS, ALU.mult, ALU.add))
    return pool.tensor_tensor(rstd, rstd, minus_half, ALU.pow)


def pairs(eng, tile):
    tile(0, 0)
    tile(1, 1)
    with eng.Fori(1, TILES // 2 - 1) as pair:
        tile(pair * 2, 0)
        tile(pair * 2 + 1, 1)
    tile(TILES - 2, 0)
    tile(TILES - 1, 1)


def begun(i, n):
    return not isinstance(i, int) or i >= n


def broadcast_rows(vector, n):
    return vector.to_broadcast([P, n])


def pool_mixer(nc, x, gain_mix, gain_ffn, pool_scale, pool_w, bands, x_mid, h_ffn):
    with ExitStack() as ctx:
        new_semaphore = ctx.enter_context(phase_semaphores(nc))

        def sb(n, shape, dt=F32):
            return ctx.enter_context(nc.sbuf_tensor(f"pool_{n}", shape, dt))

        def sem(n):
            return new_semaphore(f"pool_{n}")

        xt = [sb(f"xt{s}", [P, D]) for s in range(2)]
        xh = [sb(f"xh{s}", [P, D]) for s in range(2)]
        squares = sb("squares", [P, D])
        diff = [sb(f"diff{s}", [P, KT, P]) for s in range(2)]
        mid = [sb(f"mid{s}", [P, D]) for s in range(2)]
        hf = [sb(f"hf{s}", [P, D]) for s in range(2)]
        g_mix, g_ffn, g_scale = sb("g_mix", [P, D]), sb("g_ffn", [P, D]), sb("g_scale", [P, D])
        w = sb("w", [P, N_GRP, 2, GRP])
        band = sb("band", [P, 3, N_GRP, P])
        ss = sb("ss", [P, 4])
        rs = sb("rs", [P, 4])
        minus_half = sb("minus_half", [P, 1])
        d_ps = [ctx.enter_context(nc.psum_tensor(f"pool_d{s}", [P, KT, P], F32)) for s in range(2)]
        y_ps = [ctx.enter_context(nc.psum_tensor(f"pool_y{s}", [P, D], F32)) for s in range(2)]
        s_const, s_mid_out, s_hf_out = sem("const"), [sem(f"mid_out{s}") for s in range(2)], [sem(f"hf_out{s}") for s in range(2)]
        s_x = [sem(f"x{s}") for s in range(2)]
        s_dve, s_pool, s_xh, s_d, s_diff, s_y, s_mid, s_hf = (
            sem(n) for n in ("dve", "pool", "xh", "d", "diff", "y", "mid", "hf"))
        (s_sq_x, s_sq_mid), (s_rs_x, s_rs_mid) = ([sem(f"{n}_{which}") for which in ("x", "mid")] for n in ("sq", "rs"))
        s_half, s_seen = sem("half"), sem("seen")
        block = ctx.enter_context(nc.Block())
        x_t = x.rearrange("(i p) d -> i p d", p=P)
        mid_t = x_mid.rearrange("(i p) d -> i p d", p=P)
        h_t = h_ffn.rearrange("(i p) d -> i p d", p=P)

        @block.sync
        def _(sp):
            sp.dma_start(g_mix[:, :], broadcast_rows(gain_mix, D)).then_inc(s_const, 16)
            sp.dma_start(g_ffn[:, :], broadcast_rows(gain_ffn, D)).then_inc(s_const, 16)
            sp.dma_start(g_scale[:, :], broadcast_rows(pool_scale, D)).then_inc(s_const, 16)
            sp.dma_start(w[:, :, :, :], pool_w.rearrange("g (k p) d -> p g k d", p=P)).then_inc(s_const, 16)
            sp.dma_start(band[:, :, :, :], bands).then_inc(s_const, 16)

            def tile(i, s):
                sp.wait_ge(s_mid, i + 1)
                sp.dma_start(mid_t[bass.ds(i, 1), :, :].rearrange("a p d -> p (a d)"), mid[s][:, :]).then_inc(s_mid_out[s], 16)
                if begun(i, 1):
                    store_h(i - 1, 1 - s)

            def store_h(i, s):
                sp.wait_ge(s_hf, i + 1)
                sp.dma_start(h_t[bass.ds(i, 1), :, :].rearrange("a p d -> p (a d)"), hf[s][:, :]).then_inc(s_hf_out[s], 16)
            pairs(sp, tile)
            store_h(TILES - 1, 1)
            for s in range(2):
                sp.wait_ge(s_mid_out[s], 16 * TILES // 2)
                sp.wait_ge(s_hf_out[s], 16 * TILES // 2)

        @block.gpsimd
        def _(pool):
            pool.memset(minus_half[:, :], -0.5).then_inc(s_half, 1)
            pool.wait_ge(s_half, 1)

            def rstd(i, col, sums_made, done, base):
                pool.wait_ge(sums_made, i + 1)
                pool.sem_inc(s_seen, 1)
                row_rstd(pool, Chain(pool, s_pool, base), rs[:, col:col + 1], ss[:, col:col + 1], D, minus_half[:, :]).then_inc(done, 1)

            rstd(0, 0, s_sq_x, s_rs_x, 0)

            def tile(i, s):
                more = not isinstance(i, int) or i + 1 < TILES
                if more:
                    rstd(i + 1, 1 - s, s_sq_x, s_rs_x, i * 2 + 1)
                rstd(i, 2 + s, s_sq_mid, s_rs_mid, i * 2 + (2 if more else 1))
            pairs(pool, tile)

        @block.scalar
        def _(act):
            def load(i, s):
                act.dma_start(xt[s][:, :], x_t[bass.ds(i, 1), :, :].rearrange("a p d -> p (a d)")).then_inc(s_x[s], 16)
            load(0, 0)
            load(1, 1)

            def square_x(i, s):
                act.wait_ge(s_x[s], (i - s) * 8 + 16)
                if begun(i, 1):
                    act.wait_ge(s_sq_x, i)
                if begun(i, 2):
                    act.wait_ge(s_sq_mid, i - 1)
                    act.wait_ge(s_rs_x, i - 1)
                act.activation(squares[:, :], xt[s][:, :], ACT.Square, accum_out=ss[:, s:s + 1]).then_inc(s_sq_x, 1)
            square_x(0, 0)

            def tile(i, s):
                act.wait_ge(s_d, i + 1)
                if begun(i, 2):
                    act.wait_ge(s_y, i - 1)
                act.copy(diff[s][:, :, :], d_ps[s][:, :, :]).then_inc(s_diff, 1)
                more = not isinstance(i, int) or i + 1 < TILES
                if more:
                    square_x(i + 1, 1 - s)
                act.wait_ge(s_mid, i + 1)
                if not isinstance(i, int) or i + 2 < TILES:
                    load(i + 2, s)
                act.wait_ge(s_sq_x, i + (2 if more else 1))
                if begun(i, 1):
                    act.wait_ge(s_sq_mid, i)
                if begun(i, 2):
                    act.wait_ge(s_rs_mid, i - 1)
                act.activation(squares[:, :], mid[s][:, :], ACT.Square, accum_out=ss[:, 2 + s:3 + s]).then_inc(s_sq_mid, 1)
            pairs(act, tile)

        @block.vector
        def _(dve):
            dve.wait_ge(s_const, 80)

            def normed_x(i, s):
                dve.wait_ge(s_rs_x, i + 1)
                if begun(i, 2):
                    dve.wait_ge(s_d, i)
                dve.scalar_tensor_tensor(out=xh[s][:, :], in0=xt[s][:, :], scalar=rs[:, s:s + 1], in1=g_mix[:, :],
                                         op0=ALU.mult, op1=ALU.mult).then_inc(s_xh, 1)

            def normed_mid(i, s):
                dve.wait_ge(s_rs_mid, i + 1)
                if begun(i, 2):
                    dve.wait_ge(s_hf_out[s], (i - s) * 8)
                dve.scalar_tensor_tensor(out=hf[s][:, :], in0=mid[s][:, :], scalar=rs[:, 2 + s:3 + s], in1=g_ffn[:, :],
                                         op0=ALU.mult, op1=ALU.mult).then_inc(s_hf, 1)
            normed_x(0, 0)

            def tile(i, s):
                if not isinstance(i, int) or i + 1 < TILES:
                    normed_x(i + 1, 1 - s)
                if begun(i, 1):
                    normed_mid(i - 1, 1 - s)
                dve.wait_ge(s_y, i + 1)
                if begun(i, 2):
                    dve.wait_ge(s_hf, i - 1)
                    dve.wait_ge(s_mid_out[s], (i - s) * 8)
                Chain(dve, s_dve, i).step(dve.tensor_tensor(mid[s][:, :], y_ps[s][:, :], g_scale[:, :], ALU.mult))
                dve.tensor_tensor(mid[s][:, :], mid[s][:, :], xt[s][:, :], ALU.add).then_inc(s_mid, 1)
            pairs(dve, tile)
            normed_mid(TILES - 1, 1)

        @block.tensor
        def _(pe):
            pe.wait_ge(s_const, 80)

            def tile(i, s):
                pe.wait_ge(s_xh, i + 1)
                if begun(i, 2):
                    pe.wait_ge(s_diff, i - 1)
                for c in range(KT):
                    g = c // 2
                    last = pe.matmul(d_ps[s][:, c, :], xh[s][:, c * P:(c + 1) * P], band[:, 1 if begun(i, 1) else 0, g, :],
                                     start=True, stop=not begun(i, 1))
                    if begun(i, 1):
                        last = pe.matmul(d_ps[s][:, c, :], xh[1 - s][:, c * P:(c + 1) * P], band[:, 2, g, :],
                                         start=False, stop=True)
                last.then_inc(s_d, 1)
                pe.wait_ge(s_diff, i + 1)
                if begun(i, 2):
                    pe.wait_ge(s_mid, i - 1)
                for g in range(N_GRP):
                    for k in range(2):
                        last = pe.matmul(y_ps[s][:, g * GRP:(g + 1) * GRP], diff[s][:, 2 * g + k, :], w[:, g, k, :],
                                         start=(k == 0), stop=(k == 1))
                last.then_inc(s_y, 1)
            pairs(pe, tile)


def add_norm(nc, name, a, b, gain, x_out, h_out, ident, xt_hi=None, xt_lo=None, router=None, logits=None):
    with ExitStack() as ctx:
        new_semaphore = ctx.enter_context(phase_semaphores(nc))

        def sb(n, shape, dt=F32):
            return ctx.enter_context(nc.sbuf_tensor(f"{name}_{n}", shape, dt))

        def sem(n):
            return new_semaphore(f"{name}_{n}")

        at = [sb(f"a{s}", [P, D]) for s in range(2)]
        bt = [sb(f"b{s}", [P, D]) for s in range(2)]
        xt = [sb(f"x{s}", [P, D]) for s in range(2)]
        ht = [sb(f"h{s}", [P, D]) for s in range(2)]
        squares = sb("squares", [P, D])
        ss, rs = sb("ss", [P, 2]), sb("rs", [P, 2])
        minus_half = sb("minus_half", [P, 1])
        t_ps = [ctx.enter_context(nc.psum_tensor(f"{name}_t{s}", [P, KT, P], F32)) for s in range(2)]
        if gain is not None:
            g = sb("g", [P, D])
        if router is not None:
            r = sb("r", [P, KT, N_EXP])
            hT = [sb(f"hT{s}", [P, KT, P]) for s in range(2)]
            l_ps = [ctx.enter_context(nc.psum_tensor(f"{name}_l{s}", [P, N_EXP], F32)) for s in range(2)]
        s_const, s_half, s_seen = sem("const"), sem("half"), sem("seen")
        s_in = [sem(f"in{s}") for s in range(2)]
        s_out = [sem(f"out{s}") for s in range(2)]
        s_h_out = [sem(f"h_out{s}") for s in range(2)]
        s_x, s_sq, s_rs, s_pool, s_h, s_t, s_hi, s_lo, s_l = (
            sem(n) for n in ("sum", "sq", "rs", "pool", "h", "t", "hi", "lo", "l"))
        block = ctx.enter_context(nc.Block())
        n_const = (gain is not None) + (router is not None)

        def rows(dram, i):
            return dram[bass.ds(i * P, P), :]

        @block.sync
        def _(sp):
            if gain is not None:
                sp.dma_start(g[:, :], broadcast_rows(gain, D)).then_inc(s_const, 16)
            if router is not None:
                sp.dma_start(r[:, :, :], router.rearrange("(k p) e -> p k e", p=P)).then_inc(s_const, 16)

            def store_x(i, s):
                sp.wait_ge(s_x, i + 1)
                sp.dma_start(rows(x_out, i), xt[s][:, :]).then_inc(s_out[s], 16)
            store_x(0, 0)

            def tile(i, s):
                if not isinstance(i, int) or i + 1 < TILES:
                    store_x(i + 1, 1 - s)
                if h_out is not None:
                    sp.wait_ge(s_h, i + 1)
                    sp.dma_start(rows(h_out, i), ht[s][:, :]).then_inc(s_h_out[s], 16)
            pairs(sp, tile)
            for s in range(2):
                sp.wait_ge(s_out[s], 16 * TILES // 2)
                if h_out is not None:
                    sp.wait_ge(s_h_out[s], 16 * TILES // 2)

        @block.gpsimd
        def _(pool):
            pool.memset(minus_half[:, :], -0.5).then_inc(s_half, 1)
            pool.wait_ge(s_half, 1)

            def tile(i, s):
                pool.wait_ge(s_sq, i + 1)
                pool.sem_inc(s_seen, 1)
                chain = Chain(pool, s_pool, i)
                row_rstd(pool, chain, rs[:, s:s + 1], ss[:, s:s + 1], D, minus_half[:, :]).then_inc(s_rs, 1)
            pairs(pool, tile)

        @block.scalar
        def _(act):
            def load(i, s):
                act.dma_start(at[s][:, :], rows(a, i)).then_inc(s_in[s], 16)
                act.dma_start(bt[s][:, :], rows(b, i)).then_inc(s_in[s], 16)
            load(0, 0)
            load(1, 1)

            def square(i, s):
                act.wait_ge(s_x, i + 1)
                if begun(i, 1):
                    act.wait_ge(s_sq, i)
                    act.wait_ge(s_rs, i)
                act.activation(squares[:, :], xt[s][:, :], ACT.Square, accum_out=ss[:, s:s + 1]).then_inc(s_sq, 1)
            square(0, 0)

            def tile(i, s):
                if not isinstance(i, int) or i + 2 < TILES:
                    act.wait_ge(s_x, i + 1)
                    load(i + 2, s)
                if not isinstance(i, int) or i + 1 < TILES:
                    square(i + 1, 1 - s)
                act.wait_ge(s_t, i + 1)
                if router is None:
                    act.copy(xt_hi[:, :, bass.ds(i * P, P)], t_ps[s][:, :, :]).then_inc(s_hi, 1)
                else:
                    if begun(i, 2):
                        act.wait_ge(s_l, i - 1)
                    act.copy(hT[s][:, :, :], t_ps[s][:, :, :]).then_inc(s_hi, 1)
            pairs(act, tile)

        @block.vector
        def _(dve):
            if n_const:
                dve.wait_ge(s_const, 16 * n_const)

            def add(i, s):
                dve.wait_ge(s_in[s], (i - s) * 16 + 32)
                if begun(i, 2):
                    dve.wait_ge(s_h, i - 1)
                    dve.wait_ge(s_out[s], (i - s) * 8)
                dve.tensor_tensor(xt[s][:, :], at[s][:, :], bt[s][:, :], ALU.add).then_inc(s_x, 1)
            add(0, 0)

            def tile(i, s):
                if not isinstance(i, int) or i + 1 < TILES:
                    add(i + 1, 1 - s)
                dve.wait_ge(s_rs, i + 1)
                if begun(i, 2):
                    dve.wait_ge(s_t, i - 1)
                    if h_out is not None:
                        dve.wait_ge(s_h_out[s], (i - s) * 8)
                if gain is None:
                    dve.tensor_scalar(ht[s][:, :], xt[s][:, :], rs[:, s:s + 1], None, ALU.mult).then_inc(s_h, 1)
                else:
                    dve.scalar_tensor_tensor(out=ht[s][:, :], in0=xt[s][:, :], scalar=rs[:, s:s + 1], in1=g[:, :],
                                             op0=ALU.mult, op1=ALU.mult).then_inc(s_h, 1)
                if begun(i, 1):
                    finish(i - 1, 1 - s)

            def finish(i, s):
                if router is None:
                    dve.wait_ge(s_hi, i + 1)
                    dve.tensor_tensor(xt_lo[:, :, bass.ds(i * P, P)], t_ps[s][:, :, :], xt_hi[:, :, bass.ds(i * P, P)],
                                      ALU.subtract).then_inc(s_lo, 1)
                else:
                    dve.wait_ge(s_l, i + 1)
                    dve.tensor_copy(logits[:, bass.ds(i, 1), :], l_ps[s][:, :].rearrange("p (a e) -> p a e", a=1)).then_inc(s_lo, 1)
            pairs(dve, tile)
            finish(TILES - 1, 1)

        @block.tensor
        def _(pe):
            if n_const:
                pe.wait_ge(s_const, 16 * n_const)

            def tile(i, s):
                pe.wait_ge(s_h, i + 1)
                if begun(i, 2):
                    pe.wait_ge(s_lo, i - 1)
                for k in range(KT):
                    last = pe.transpose(t_ps[s][:, k, :], ht[s][:, k * P:(k + 1) * P], ident)
                last.then_inc(s_t, 1)
                if router is not None and begun(i, 1):
                    route_logits(i - 1, 1 - s)

            def route_logits(i, s):
                pe.wait_ge(s_hi, i + 1)
                for k in range(KT):
                    last = pe.matmul(l_ps[s][:, :], hT[s][:, k, :], r[:, k, :], start=(k == 0), stop=(k == KT - 1))
                last.then_inc(s_l, 1)
            pairs(pe, tile)
            if router is not None:
                route_logits(TILES - 1, 1)


def project(nc, name, xt_hi, xt_lo, w, w_gain, n_chunks, out, last_cols=512, side_loads=None):
    C = 512
    with ExitStack() as ctx:
        new_semaphore = ctx.enter_context(phase_semaphores(nc))

        def sb(n, shape, dt=F32):
            return ctx.enter_context(nc.sbuf_tensor(f"{name}_{n}", shape, dt))

        def sem(n):
            return new_semaphore(f"{name}_{n}")

        HK = KT // 2
        raw = [sb(f"raw{s}", [P, HK, C]) for s in range(2)]
        w_hi = [sb(f"hi{s}", [P, HK, C], F32R) for s in range(2)]
        w_lo = [sb(f"lo{s}", [P, HK, C], F32R) for s in range(2)]
        gains = sb("gains", [P, n_chunks, KT])
        ot = [sb(f"o{s}", [P, C]) for s in range(4)]
        ps = [ctx.enter_context(nc.psum_tensor(f"{name}_ps{b}", [P, C], F32)) for b in range(TILES)]
        s_raw = [sem(f"raw{s}") for s in range(2)]
        s_out = [sem(f"out{s}") for s in range(4)]
        s_gain, s_scaled, s_hi, s_lo, s_first_half, s_ready, s_copied, s_side = (
            sem(n) for n in ("gain", "scaled", "hi", "lo", "first_half", "ready", "copied", "side"))
        block = ctx.enter_context(nc.Block())

        @block.sync
        def _(sp):
            if w_gain is not None:
                sp.dma_start(gains[:, :, :], w_gain).then_inc(s_gain, 16)
            side = 0
            for c in range(n_chunks):
                for half in range(2):
                    sp.wait_ge(s_lo, c * 2 + half + 1)
                    sp.dma_start(raw[half][:, :, :], w[c * P:(c + 1) * P, half * HK * C:(half + 1) * HK * C]
                                 .rearrange("p (k n) -> p k n", k=HK)).then_inc(s_raw[half], 16)
                if side_loads:
                    side += side_loads(sp, c, s_side)
            if side:
                sp.wait_ge(s_side, 16 * side)

        @block.gpsimd
        def _(pool):
            def store(c, cols):
                for i in range(TILES):
                    pool.wait_ge(s_copied, c * TILES + (i + 1 + TILES))
                    pool.dma_start(out[i * P:(i + 1) * P, bass.ds(c * C, cols)], ot[i % 4][:, 0:cols]).then_inc(s_out[i % 4], 16)
            with pool.Fori(0, n_chunks - 1) as c:
                store(c, C)
            store(n_chunks - 1, last_cols)
            for s in range(4):
                pool.wait_ge(s_out[s], 16 * 2 * n_chunks)

        @block.scalar
        def _(act):
            if w_gain is not None:
                act.wait_ge(s_gain, 16)
            with act.Fori(0, n_chunks) as c:
                for half in range(2):
                    act.wait_ge(s_raw[half], c * 16 + 16)
                    if half == 0:
                        act.wait_ge(s_first_half, c + 1)
                    else:
                        act.wait_ge(s_ready, c * TILES + 1)
                    if w_gain is not None:
                        for k in range(HK):
                            kk = half * HK + k
                            act.activation(raw[half][:, k, :], raw[half][:, k, :], ACT.Copy,
                                           scale=gains[:, bass.ds(c, 1), kk:kk + 1].rearrange("p a b -> p (a b)")
                                           ).then_inc(s_scaled, 1)
                        act.wait_ge(s_scaled, c * KT + (half + 1) * HK)
                    act.copy(w_hi[half][:, :, :], raw[half][:, :, :]).then_inc(s_hi, 1)

        @block.vector
        def _(dve):
            dve.sem_inc(s_lo, 2)
            dve.sem_inc(s_copied, TILES)

            def copy_out(c, i, cols=C):
                dve.wait_ge(s_ready, c * TILES + (i + 2))
                if begun(c, 1) or i >= 4:
                    dve.wait_ge(s_out[i % 4], c * 32 + 16 * (i // 4))
                dve.tensor_copy(ot[i % 4][:, 0:cols], ps[i][:, 0:cols]).then_inc(s_copied, 1)

            def split(c, half):
                dve.wait_ge(s_hi, c * 2 + half + 1)
                dve.tensor_tensor(w_lo[half][:, :, :], raw[half][:, :, :], w_hi[half][:, :, :], ALU.subtract).then_inc(s_lo, 1)

            split(0, 0)
            split(0, 1)

            def split_and_copy_out(c):
                split(c, 0)
                for i in range(TILES):
                    if i == TILES // 2:
                        split(c, 1)
                    copy_out(c - 1, i)

            split_and_copy_out(1)
            if n_chunks > 2:
                with dve.Fori(2, n_chunks) as c:
                    split_and_copy_out(c)
            for i in range(TILES):
                copy_out(n_chunks - 1, i, last_cols)

        @block.tensor
        def _(pe):
            pe.sem_inc(s_first_half, 1)
            pe.sem_inc(s_ready, 1)

            def chunk(c, cols):
                for half in range(2):
                    pe.wait_ge(s_lo, c * 2 + half + 3)
                    for i in range(TILES):
                        if half == 0:
                            pe.wait_ge(s_copied, c * TILES + (i + 1))
                        for k in range(HK):
                            kk = half * HK + k
                            rows = slice(i * P, (i + 1) * P)
                            pe.matmul(ps[i][:, 0:cols], xt_hi[:, kk, rows], w_hi[half][:, k, 0:cols], start=(kk == 0), stop=False)
                            pe.matmul(ps[i][:, 0:cols], xt_hi[:, kk, rows], w_lo[half][:, k, 0:cols], start=False, stop=False)
                            last = pe.matmul(ps[i][:, 0:cols], xt_lo[:, kk, rows], w_hi[half][:, k, 0:cols],
                                             start=False, stop=(kk == KT - 1))
                        if half == 1:
                            last.then_inc(s_ready, 1)
                        if half == 0 and i == TILES - 1:
                            last.then_inc(s_first_half, 1)
            with pe.Fori(0, n_chunks - 1) as c:
                chunk(c, C)
            chunk(n_chunks - 1, last_cols)


def split_heads(nc, qkv, k_gain, ident, kt, qt_dram, gates):
    NH = N_HEADS + 2 * N_KV
    with ExitStack() as ctx:
        new_semaphore = ctx.enter_context(phase_semaphores(nc))

        def sb(n, shape, dt=F32):
            return ctx.enter_context(nc.sbuf_tensor(f"heads_{n}", shape, dt))

        def sem(n):
            return new_semaphore(f"heads_{n}")

        raw = [sb(f"raw{s}", [P, NH, DH]) for s in range(2)]
        squares = sb("squares", [P, NH, DH])
        ss = [sb(f"ss{s}", [P, NH]) for s in range(2)]
        minus_half = sb("minus_half", [P, NH])
        kg = sb("kg", [P, 2 * N_KV, DH])
        gate_raw = sb("gate_raw", [P, TILES, 3 * N_HEADS])
        qst = [sb(f"qst{s}", [P, N_HEADS, 2, DH], F32R) for s in range(2)]
        kst = [sb(f"kst{s}", [P, 2 * N_KV, 4, DH], F32R) for s in range(2)]
        qt = [sb(f"qt{s}", [P, N_HEADS // 2, P], F32R) for s in range(2)]
        q_ps = [ctx.enter_context(nc.psum_tensor(f"heads_q{s}", [P, 8, P], F32)) for s in range(2)]
        k_ps = [ctx.enter_context(nc.psum_tensor(f"heads_k{s}", [P, 8, P], F32)) for s in range(2)]
        s_const, s_half, s_seen = sem("const"), sem("half"), sem("seen")
        s_raw = [sem(f"raw{s}") for s in range(2)]
        s_qt_out = [sem(f"qt_out{s}") for s in range(2)]
        s_gate, s_gate_exp, s_chain, s_pool = sem("gate"), sem("gate_exp"), sem("chain"), sem("pool")
        s_sq, s_ss, s_rs, s_norm, s_hi, s_lo, s_tr, s_out = (
            sem(n) for n in ("sq", "ss", "rs", "norm", "hi", "lo", "tr", "out"))
        block = ctx.enter_context(nc.Block())
        chunks = ((0, 3 * 512, N_HEADS), (N_HEADS, 512, N_KV), (N_HEADS + N_KV, 1024, N_KV))

        @block.sync
        def _(sp):
            sp.dma_start(kg[:, :, :], k_gain.to_broadcast([P, 2 * N_KV * DH]).rearrange("p (h d) -> p h d", d=DH)).then_inc(s_const, 16)
            sp.dma_start(gate_raw[:, :, :], qkv[:, 5 * 512:5 * 512 + 3 * N_HEADS].rearrange("(i p) n -> p i n", p=P)).then_inc(s_gate, 16)

            def tile(i, s):
                if begun(i, 2):
                    sp.wait_ge(s_lo, i - 1)
                for h0, col, n in chunks:
                    sp.dma_start(raw[s][:, h0:h0 + n, :], qkv[bass.ds(i * P, P), col:col + n * DH]
                                 .rearrange("p (h d) -> p h d", d=DH)).then_inc(s_raw[s], 16)
            pairs(sp, tile)

        @block.gpsimd
        def _(pool):
            pool.memset(minus_half[:, :], -0.5).then_inc(s_half, 1)
            pool.wait_ge(s_half, 1)

            def rstd(i, s):
                pool.wait_ge(s_ss, i + 1)
                pool.sem_inc(s_seen, 1)
                row_rstd(pool, Chain(pool, s_pool, i), ss[s][:, :], ss[s][:, :], DH, minus_half[:, :]).then_inc(s_rs, 1)

            def store(i):
                for half in range(2):
                    pool.wait_ge(s_out, i * 3 + half + 1)
                    pool.dma_start(qt_dram[bass.ds(i * P, P), half * 8 * P:(half + 1) * 8 * P], qt[half][:, :, :].bitcast(F32)
                                   ).then_inc(s_qt_out[half], 16)

            def tile(i, s):
                if not isinstance(i, int) or i + 1 < TILES:
                    rstd(i + 1, 1 - s)
                if begun(i, 1):
                    store(i - 1)
            rstd(0, 0)
            pairs(pool, tile)
            store(TILES - 1)
            for s in range(2):
                pool.wait_ge(s_qt_out[s], 16 * TILES)

        @block.scalar
        def _(act):
            act.wait_ge(s_gate, 16)
            act.activation(gate_raw[:, :, :], gate_raw[:, :, :], ACT.Exp, scale=-1.0).then_inc(s_gate_exp, 1)

            def square(i, s):
                act.wait_ge(s_raw[s], (i - s) * 24 + 48)
                if begun(i, 1):
                    act.wait_ge(s_ss, i)
                act.activation(squares[:, :, :], raw[s][:, :, :], ACT.Square).then_inc(s_sq, 1)

            def store(i, s):
                for half in range(2):
                    act.wait_ge(s_tr, i * 3 + half + 1)
                    if begun(i, 1):
                        act.wait_ge(s_qt_out[half], i * 16)
                    act.copy(qt[half][:, :, :], q_ps[half][:, :, :]).then_inc(s_out, 1)
                act.wait_ge(s_tr, i * 3 + 3)
                for half in range(2):
                    last = act.copy(kt[:, half * 4:half * 4 + 4, :, bass.ds(i * P, P)],
                                    k_ps[half][:, :, :].rearrange("p (h l) t -> p h l t", l=2))
                last.then_inc(s_out, 1)

            square(0, 0)

            def tile(i, s):
                if not isinstance(i, int) or i + 1 < TILES:
                    square(i + 1, 1 - s)
                act.wait_ge(s_norm, i + 1)
                if begun(i, 2):
                    act.wait_ge(s_tr, i * 3 - 3)
                act.copy(qst[s][:, :, 0, :], raw[s][:, 0:N_HEADS, :]).then_inc(s_hi, 1)
                act.copy(kst[s][:, :, 0, :], raw[s][:, N_HEADS:NH, :]).then_inc(s_hi, 1)
                act.copy(kst[s][:, :, 1, :], raw[s][:, N_HEADS:NH, :]).then_inc(s_hi, 1)
                if begun(i, 1):
                    store(i - 1, 1 - s)
            pairs(act, tile)
            store(TILES - 1, 1)

        @block.vector
        def _(dve):
            dve.wait_ge(s_gate_exp, 1)
            chain = Chain(dve, s_chain, 0)
            chain.step(dve.tensor_scalar(gate_raw[:, :, :], gate_raw[:, :, :], 1.0, None, ALU.add))
            chain.step(dve.reciprocal(gates[:, :, :], gate_raw[:, :, :]))
            dve.wait_ge(s_const, 16)

            def sums(i, s):
                dve.wait_ge(s_sq, i + 1)
                dve.tensor_reduce(ss[s][:, :], squares[:, :, :], AX.X, ALU.add).then_inc(s_ss, 1)
            sums(0, 0)

            def tile(i, s):
                dve.wait_ge(s_rs, i + 1)
                chain = Chain(dve, s_chain, i * 2 + 2)
                chain.step(dve.tensor_tensor(raw[s][:, :, :], raw[s][:, :, :],
                                             ss[s][:, :].rearrange("p (h a) -> p h a", a=1).to_broadcast([P, NH, DH]), ALU.mult))
                dve.tensor_tensor(raw[s][:, N_HEADS:NH, :], raw[s][:, N_HEADS:NH, :], kg[:, :, :], ALU.mult).then_inc(s_norm, 1)
                if not isinstance(i, int) or i + 1 < TILES:
                    sums(i + 1, 1 - s)
                dve.wait_ge(s_hi, i * 3 + 3)
                dve.tensor_tensor(qst[s][:, :, 1, :], raw[s][:, 0:N_HEADS, :], qst[s][:, :, 0, :], ALU.subtract)
                dve.tensor_tensor(kst[s][:, :, 2, :], raw[s][:, N_HEADS:NH, :], kst[s][:, :, 0, :], ALU.subtract)
                chain.step(dve.tensor_tensor(kst[s][:, :, 3, :], raw[s][:, N_HEADS:NH, :], kst[s][:, :, 0, :], ALU.subtract))
                dve.sem_inc(s_lo, 1)
            pairs(dve, tile)

        @block.tensor
        def _(pe):
            def tile(i, s):
                pe.wait_ge(s_lo, i + 1)
                if begun(i, 1):
                    pe.wait_ge(s_out, i * 3)
                for half in range(2):
                    for h in range(8):
                        last = pe.transpose(q_ps[half][:, h, :], qst[s][:, half * 8 + h, :, :].rearrange("p a d -> p (a d)").bitcast(F32), ident)
                    last.then_inc(s_tr, 1)
                for half in range(2):
                    for h in range(4):
                        for hl in range(2):
                            last = pe.transpose(k_ps[half][:, h * 2 + hl, :],
                                                kst[s][:, half * 4 + h, hl * 2:hl * 2 + 2, :].rearrange("p a d -> p (a d)").bitcast(F32), ident)
                last.then_inc(s_tr, 1)
            pairs(pe, tile)


def compress_keys(nc, qkv, pos, w1, w2, kc_gain, ident, kct, vc):
    NBL = 64
    with ExitStack() as ctx:
        new_semaphore = ctx.enter_context(phase_semaphores(nc))

        def sb(n, shape, dt=F32):
            return ctx.enter_context(nc.sbuf_tensor(f"cmp_{n}", shape, dt))

        def sem(n):
            return new_semaphore(f"cmp_{n}")

        MP = SEQ // 2
        zrow = [sb(f"zrow{s}", [P, MP // P, N_KV, 2, DH]) for s in range(2)]
        zt = [sb(f"zt{s}", [P, N_KV, MP + 8]) for s in range(2)]
        posT = sb("posT", [P, 2, 16])
        w1s = [sb(f"w1s{s}", [P, 16, 2 * P]) for s in range(2)]
        w2s = sb("w2s", [P, 2, 2, DH])
        blk = [sb(f"blk{s}", [P, N_KV, NBL]) for s in range(2)]
        hidT = [sb(f"hidT{s}", [P, 2, N_KV, NBL]) for s in range(2)]
        kc = sb("kc", [NBL, N_KV, DH])
        sq = sb("sq", [NBL, N_KV, DH])
        ss = sb("ss", [NBL, N_KV])
        minus_half = sb("minus_half", [NBL, N_KV])
        kg = sb("kg", [NBL, DH])
        kst = sb("kst", [NBL, N_KV, 2, DH])
        t_ps = [ctx.enter_context(nc.psum_tensor(f"cmp_t{s}", [P, MP], F32)) for s in range(4)]
        h_ps = [ctx.enter_context(nc.psum_tensor(f"cmp_h{s}", [P, N_KV, NBL], F32)) for s in range(2)]
        o_ps = [ctx.enter_context(nc.psum_tensor(f"cmp_o{s}", [NBL, N_KV, DH], F32)) for s in range(2)]
        s_const, s_z, s_half, s_zero = sem("const"), sem("z"), sem("half"), sem("zero")
        s_tr, s_zt, s_blk, s_h, s_hid, s_o, s_fin = (sem(n) for n in ("tr", "zt", "blk", "h", "hid", "o", "fin"))
        s_chain, s_pool, s_ss, s_rs, s_norm, s_st, s_ktr = (
            sem(n) for n in ("chain", "pool", "ss", "rs", "norm", "st", "ktr"))
        s_h_step = sem("h_step")
        block = ctx.enter_context(nc.Block())

        @block.sync
        def _(sp):
            for z in range(2):
                src = qkv[:, z * 256:(z + 1) * 256].rearrange("(m p l) (g d) -> p m g l d", p=P, l=2, d=DH)
                for m in range(MP // P):
                    for l in range(2):
                        sp.dma_start(zrow[z][:, m, :, l, :], src[:, m, :, l, :]).then_inc(s_z, 16)
            sp.dma_start(posT[:, :, :], pos).then_inc(s_const, 16)
            for z in range(2):
                sp.dma_start(w2s[:, z, :, :], w2[z].rearrange("(k p) n -> p k n", p=P)).then_inc(s_const, 16)
            sp.dma_start(kg[:, :], kc_gain.to_broadcast([NBL, DH])).then_inc(s_const, 16)

        @block.gpsimd
        def _(pool):
            for z in range(2):
                pool.memset(zt[z][:, :, MP:MP + 8], 0.0).then_inc(s_zero, 1)
            pool.memset(minus_half[:, :], -0.5).then_inc(s_half, 1)
            pool.wait_ge(s_half, 1)
            pool.wait_ge(s_ss, 1)
            row_rstd(pool, Chain(pool, s_pool, 0), ss[:, :], ss[:, :], DH, minus_half[:, :]).then_inc(s_rs, 1)

        @block.scalar
        def _(act):
            for z in range(2):
                act.dma_start(w1s[z][:, :, :], w1[z].rearrange("(l p) n -> p l n", p=P)).then_inc(s_const, 16)
            for z in range(2):
                for g in range(N_KV):
                    act.wait_ge(s_tr, z * N_KV + g + 1)
                    act.copy(zt[z][:, g, 0:MP], t_ps[g][:, :]).then_inc(s_zt, 1)
            for z in range(2):
                for n in range(2):
                    act.wait_ge(s_h, z * 2 + n + 1)
                    act.activation(hidT[z][:, n, :, :], h_ps[n][:, :, :], ACT.Silu).then_inc(s_hid, 1)
            act.wait_ge(s_norm, 1)
            for a in range(2):
                act.copy(kst[:, :, a, :], kc[:, :, :]).then_inc(s_st, 1)
            act.wait_ge(s_ktr, 1)
            for g in range(N_KV):
                for copy in range(2):
                    act.copy(kct[:, g, copy * NBL:(copy + 1) * NBL], t_ps[g][:, 0:NBL]).then_inc(s_fin, 1)
            act.wait_ge(s_fin, 2 * N_KV)

        @block.vector
        def _(dve):
            dve.wait_ge(s_const, 16 * 6)
            dve.wait_ge(s_zero, 2)
            dve.wait_ge(s_zt, 2 * N_KV)
            for z in range(2):
                for l in range(16):
                    n = z * 16 + l
                    if n >= 2:
                        dve.wait_ge(s_h_step, n - 1)
                    dve.tensor_scalar(blk[l % 2][:, :, :], zt[z][:, :, l:l + 8 * (NBL - 1) + 1:8], posT[:, z, l:l + 1], None,
                                      ALU.add).then_inc(s_blk, 1)
            chain = Chain(dve, s_chain, 0)
            dve.wait_ge(s_o, 1)
            chain.step(dve.tensor_copy(kc[:, :, :], o_ps[0][:, :, :]))
            dve.wait_ge(s_o, 2)
            chain.step(dve.tensor_copy(vc[:, :, :], o_ps[1][:, :, :]))
            chain.step(dve.tensor_tensor(sq[:, :, :], kc[:, :, :], kc[:, :, :], ALU.mult))
            dve.tensor_reduce(ss[:, :], sq[:, :, :], AX.X, ALU.add).then_inc(s_ss, 1)
            dve.wait_ge(s_rs, 1)
            chain.step(dve.tensor_tensor(kc[:, :, :], kc[:, :, :],
                                         ss[:, :].rearrange("p (h a) -> p h a", a=1).to_broadcast([NBL, N_KV, DH]), ALU.mult))
            dve.tensor_tensor(kc[:, :, :], kc[:, :, :],
                              kg[:, :].rearrange("p (a d) -> p a d", a=1).to_broadcast([NBL, N_KV, DH]), ALU.mult).then_inc(s_norm, 1)

        @block.tensor
        def _(pe):
            pe.wait_ge(s_z, 16 * 2 * (MP // P) * 2)
            for z in range(2):
                for g in range(N_KV):
                    if z == 1:
                        pe.wait_ge(s_zt, g + 1)
                    for m in range(MP // P):
                        last = pe.transpose(t_ps[g][:, m * P:(m + 1) * P], zrow[z][:, m, g, :, :].rearrange("p l d -> p (l d)"), ident)
                    last.then_inc(s_tr, 1)
            for z in range(2):
                for l in range(16):
                    pe.wait_ge(s_blk, z * 16 + l + 1)
                    if z == 1 and l == 0:
                        pe.wait_ge(s_hid, 2)
                    for n in range(2):
                        last = pe.matmul(h_ps[n][:, :, :], w1s[z][:, l, n * P:(n + 1) * P], blk[l % 2][:, :, :],
                                         start=(l == 0), stop=(l == 15))
                        if l == 15:
                            last.then_inc(s_h, 1)
                    if l < 15:
                        last.then_inc(s_h_step, 1)
                    else:
                        pe.wait_ge(s_h, z * 2 + 2)
                        pe.sem_inc(s_h_step, 1)
            for z in range(2):
                pe.wait_ge(s_hid, z * 2 + 2)
                for g in range(N_KV):
                    for n in range(2):
                        last = pe.matmul(o_ps[z][:, g, :], hidT[z][:, n, g, :], w2s[:, z, n, :], start=(n == 0), stop=(n == 1))
                last.then_inc(s_o, 1)
            pe.wait_ge(s_st, 2)
            for g in range(N_KV):
                last = pe.transpose(t_ps[g][:, 0:NBL], kst[:, g, :, :].rearrange("p a d -> p (a d)"), ident[0:NBL, 0:NBL])
            last.then_inc(s_ktr, 1)


def bias_tables(eng, part, parts, bias_vec, win, win_mask, cmpb, done):
    rows = range(P * part // parts, P * (part + 1) // parts)
    for q in rows:
        eng.dma_start(win[q:q + 1, :, P:3 * P], bias_vec[:, 127 - q:127 - q + 2 * P].rearrange("(a h) n -> a h n", a=1)
                      ).then_inc(done, 16)
    if part + 1 < parts:
        return len(rows)
    eng.dma_start(win[:, :, 0:P], win_mask.rearrange("p (a n) -> p a n", a=1).to_broadcast([P, N_HEADS, P])).then_inc(done, 16)
    phases = bias_vec[:, NEAR:VEC].rearrange("h (r m) -> r h m", r=16)
    for a in range(8):
        eng.dma_start(cmpb[16 * a:16 * a + 16, :, :], phases[:, :, 7 - a:7 - a + CB]).then_inc(done, 16)
    return len(rows) + 9


def bias_vectors(nc, rel_bias, onehot, vec_dram):
    NB1 = N_BUCKETS + 1
    with ExitStack() as ctx:
        new_semaphore = ctx.enter_context(phase_semaphores(nc))

        tab = ctx.enter_context(nc.sbuf_tensor("bias_tab", [NB1, N_HEADS], F32))
        hot = ctx.enter_context(nc.sbuf_tensor("bias_hot", [NB1, VEC], F32))
        vec = ctx.enter_context(nc.sbuf_tensor("bias_vec", [N_HEADS, VEC], F32))
        ps = [ctx.enter_context(nc.psum_tensor(f"bias_ps{b}", [N_HEADS, 512], F32)) for b in range(5)]
        s_in, s_neg, s_mm, s_copy, s_vec = (new_semaphore(f"bias_{n}") for n in ("in", "neg", "mm", "copy", "vec"))
        block = ctx.enter_context(nc.Block())
        spans = [(a, min(a + 512, VEC)) for a in range(0, VEC, 512)]

        @block.sync
        def _(sp):
            sp.dma_start(tab[0:N_BUCKETS, :], rel_bias).then_inc(s_in, 16)
            sp.dma_start(hot[:, :], onehot).then_inc(s_in, 16)
            sp.wait_ge(s_copy, len(spans))
            sp.dma_start(vec_dram, vec[:, :]).then_inc(s_vec, 16)
            sp.wait_ge(s_vec, 16)

        @block.vector
        def _(dve):
            dve.memset(tab[N_BUCKETS:NB1, :], -NEG).then_inc(s_neg, 1)
            for n, (a, b) in enumerate(spans):
                dve.wait_ge(s_mm, n + 1)
                dve.tensor_copy(vec[:, a:b], ps[n][:, 0:b - a]).then_inc(s_copy, 1)

        @block.tensor
        def _(pe):
            pe.wait_ge(s_in, 32)
            pe.wait_ge(s_neg, 1)
            for n, (a, b) in enumerate(spans):
                pe.matmul(ps[n][:, 0:b - a], tab[:, :], hot[:, a:b], start=True, stop=True).then_inc(s_mm, 1)


def attend(nc, qkv, qt_dram, kt, kct, vc, gates, win, cmpb, sel_const, row_valid, ident, ot_dram, side_store):
    with ExitStack() as ctx:
        new_semaphore = ctx.enter_context(phase_semaphores(nc))

        def sb(n, shape, dt=F32):
            return ctx.enter_context(nc.sbuf_tensor(f"att_{n}", shape, dt))

        def sem(n):
            return new_semaphore(f"att_{n}")

        R = N_HEADS // N_KV
        NBL, NSB = 64, 16
        vs, vw = sb("vs", [P, TILES, N_KV * DH]), sb("vw", [P, TILES, N_KV * DH])
        qt = [sb(f"qt{s}", [P, N_HEADS, P], F32R) for s in range(2)]
        p_slc = [sb(f"p_slc{s}", [P, R, SEQ]) for s in range(2)]
        p_win = [sb(f"p_win{s}", [P, R, 3 * P]) for s in range(2)]
        p_cmp = [sb(f"p_cmp{s}", [P, N_HEADS, NBL]) for s in range(2)]
        shares = sb("shares", [P, N_HEADS, NBL])
        near = [sb(f"near{s}", [P, 2 * P]) for s in range(2)]
        pt = [sb(f"pt{s}", [P, R, P]) for s in range(4)]
        ot = [sb(f"ot{s}", [P, 2, P]) for s in range(2)]
        far_min, neg_max, sums, scale = sb("far_min", [P, 8]), sb("neg_max", [P, 8]), sb("sums", [P, 8]), sb("scale", [P, 8])
        c_min, c_rs = sb("c_min", [P, N_HEADS]), sb("c_rs", [P, N_HEADS])
        c_scale = [sb(f"c_scale{s}", [P, N_HEADS]) for s in range(2)]
        group_p = sb("group_p", [P, N_KV, NBL])
        imp, pick, top = sb("imp", [P, N_KV, NSB]), sb("pick", [P, N_KV, NSB]), sb("top", [P, N_KV])
        sel = [sb(f"sel{s}", [P, N_KV, NSB]) for s in range(2)]
        consts = sb("consts", [P, 2 * TILES + 1, NSB])
        valid, minus_one = sb("valid", [P, 1]), sb("minus_one", [P, 1])
        s_ps = [ctx.enter_context(nc.psum_tensor(f"att_s{s}", [P, SEQ], F32)) for s in range(2)]
        t_ps = [ctx.enter_context(nc.psum_tensor(f"att_t{s}", [P, R, P], F32)) for s in range(2)]
        o_ps = [ctx.enter_context(nc.psum_tensor(f"att_o{s}", [P, 512], F32)) for s in range(2)]
        s_const, s_qt = sem("const"), [sem(f"qt{s}") for s in range(2)]
        s_scores, s_sread, s_exp, s_scale, s_slc_scaled, s_win_scaled = (
            sem(n) for n in ("scores", "sread", "exp", "scale", "slc_scaled", "win_scaled"))
        s_cready, s_cexp, s_cscale, s_cscaled, s_sel, s_near = (
            sem(n) for n in ("cready", "cexp", "cscale", "cscaled", "sel", "near"))
        s_tr, s_pt_act, s_pt_dve, s_pv, s_oevac = (sem(n) for n in ("tr", "pt_act", "pt_dve", "pv", "oevac"))
        s_chain, s_inverse, s_ot_out = sem("chain"), sem("inverse"), [sem(f"ot_out{s}") for s in range(2)]
        block = ctx.enter_context(nc.Block())

        order = [("cmp", 0, g) for g in range(N_KV)]
        for u in range(4 * TILES):
            for b in range(8):
                order.append(("unit", u, b))
                if u % 4 == 1 and b % 2 and u // 4 + 1 < TILES:
                    order.append(("cmp", u // 4 + 1, b // 2))
        number = {step: n for n, step in enumerate(order)}

        def cmp_step(i, g):
            return number["cmp", i, g]

        def unit_step(u, b):
            return number["unit", u, b]

        def key_tiles(u):
            i = u // 4
            w0 = max(0, i - 2)
            return ([("cmp", 0, 0)] + [("win", (t - i + 2) * P, t) for t in range(w0, i + 1)]
                    + [("slc", t * P, t) for t in range(i + 1)])

        first_pt = [0]
        for u in range(4 * TILES):
            first_pt.append(first_pt[-1] + len(key_tiles(u)))

        def part(u, b0):
            n, b = len(key_tiles(u)), max(b0, 2)
            return range(first_pt[u] + n * (b - 2) // 6, first_pt[u] + n * (b - 1) // 6) if b0 >= 2 else range(0)

        @block.sync
        def _(sp):
            sp.dma_start(vs[:, :, :], qkv[:, 768:1024].rearrange("(i p) n -> p i n", p=P)).then_inc(s_const, 16)
            sp.dma_start(vw[:, :, :], qkv[:, 1280:1536].rearrange("(i p) n -> p i n", p=P)).then_inc(s_const, 16)
            sp.dma_start(consts[:, :, :], sel_const).then_inc(s_const, 16)
            sp.dma_start(valid[:, :], row_valid).then_inc(s_const, 16)

            def load_q(i):
                sp.dma_start(qt[i % 2][:, :, :].bitcast(F32), qt_dram[i * P:(i + 1) * P, :].rearrange("p (h t) -> p h t", t=P)
                             ).then_inc(s_qt[i % 2], 16)
            load_q(0)
            load_q(1)
            for u in range(4 * TILES):
                i, g = divmod(u, 4)
                if g == 2 and i + 2 < TILES:
                    sp.wait_ge(s_scores, unit_step(4 * i + 3, 7) + 1)
                    load_q(i + 2)
                sp.wait_ge(s_oevac, u + 1)
                sp.dma_start(ot_dram[:, 2 * g:2 * g + 2, i * P:(i + 1) * P], ot[u % 2][:, :, :]).then_inc(s_ot_out[u % 2], 16)
                side_store(sp, u)
            for s in range(2):
                sp.wait_ge(s_ot_out[s], 16 * 2 * TILES)

        @block.gpsimd
        def _(pool):
            inverses = Chain(pool, s_inverse, 1)
            pool.memset(minus_one[:, :], -1.0).then_inc(s_inverse, 1)
            pool.wait_ge(s_inverse, 1)

            def scale_cmp(i):
                pool.wait_ge(s_cscale, i + 1)
                pool.tensor_tensor(p_cmp[i % 2][:, :, :], p_cmp[i % 2][:, :, :],
                                   c_scale[i % 2][:, :].rearrange("p (h a) -> p h a", a=1).to_broadcast([P, N_HEADS, NBL]),
                                   ALU.mult).then_inc(s_cscaled, 1)

            def near_bias(u, r):
                i, g = divmod(u, 4)
                n = (u - 8) * R + r
                pool.wait_ge(s_sel, i - 1)
                if n >= 2:
                    v, q = divmod(n - 2, R)
                    pool.wait_ge(s_sread, unit_step(v + 8, 2 * q) + 1)
                pool.tensor_tensor(near[n % 2][:, :].rearrange("p (b c) -> p b c", c=DH),
                                   win[:, 4 * g + r, P:3 * P].rearrange("p (b c) -> p b c", c=DH),
                                   sel[i % 2][:, g, 2 * i - 2:2 * i + 2].rearrange("p (b a) -> p b a", a=1).to_broadcast([P, 4, DH]),
                                   ALU.add).then_inc(s_near, 1)

            def finish(k):
                u, b = divmod(k, 8)
                i, g = divmod(u, 4)
                pool.wait_ge(s_exp, k + 1)
                if k >= 8:
                    pool.wait_ge(s_win_scaled if b % 2 else s_slc_scaled, (k - 8) // 2 + 1)
                at, c = (4 * g + b // 2) * 3 + 1 + b % 2, slice(k % 8, k % 8 + 1)
                inverses.step(pool.tensor_tensor(sums[:, c], sums[:, c], minus_one[:, :], ALU.pow))
                pool.tensor_tensor(scale[:, c], gates[:, i, at:at + 1], sums[:, c], ALU.mult).then_inc(s_scale, 1)

            scale_cmp(0)
            for i in range(TILES):
                for g in range(N_KV):
                    u = 4 * i + g
                    for b in range(8):
                        if i >= 2 and b % 2 == 0:
                            near_bias(u, b // 2)
                        if b or u:
                            finish(8 * u + b - 1)
                        if g == 2 and b == 2 and i + 1 < TILES:
                            scale_cmp(i + 1)
            finish(8 * 4 * TILES - 1)

        @block.scalar
        def _(act):
            def copy_pt(m):
                act.wait_ge(s_tr, m + 1)
                if m >= 4:
                    act.wait_ge(s_pv, m - 3)
                rows = NBL if m in first_pt else P
                act.copy(pt[m % 4][0:rows, :, :], t_ps[m % 2][0:rows, :, :]).then_inc(s_pt_act, 1)

            def scale_slc(k):
                u, b = divmod(k, 8)
                p = p_slc[u % 2][:, b // 2, 0:(u // 4 + 1) * P]
                act.wait_ge(s_scale, k + 1)
                act.mul(p, p, scale[:, k % 8:k % 8 + 1]).then_inc(s_slc_scaled, 1)

            def copy_out(u):
                act.wait_ge(s_pv, first_pt[u + 1])
                if u >= 2:
                    act.wait_ge(s_ot_out[u % 2], 16 * (u // 2))
                act.copy(ot[u % 2][:, :, :], o_ps[u % 2][:, 0:2 * P].rearrange("p (a q) -> p a q", a=2)).then_inc(s_oevac, 1)

            def values_part(u, b):
                for m in part(u, b):
                    if m == first_pt[u] + 1 and u >= 1:
                        copy_out(u - 1)
                    if m % 2 == 0:
                        copy_pt(m)

            def exp_cmp(i):
                act.wait_ge(s_cready, i + 1)
                act.activation(p_cmp[i % 2][:, :, :], p_cmp[i % 2][:, :, :], ACT.Exp, scale=-1.0).then_inc(s_cexp, 1)

            exp_cmp(0)
            for i in range(TILES):
                for g in range(N_KV):
                    u = 4 * i + g
                    if g == 2 and i + 1 < TILES:
                        exp_cmp(i + 1)
                    for b in range(8):
                        k = 8 * u + b
                        if b % 2 == 0:
                            p = p_slc[u % 2][:, b // 2, 0:(i + 1) * P]
                        else:
                            p = p_win[u % 2][:, b // 2, max(0, 2 - i) * P:3 * P]
                        act.wait_ge(s_sread, unit_step(u, b) + 1)
                        if k >= 8:
                            act.wait_ge(s_scale, k - 7)
                        act.activation(p, p, ACT.Exp, scale=-1.0, bias=neg_max[:, k % 8:k % 8 + 1],
                                       accum_out=sums[:, k % 8:k % 8 + 1]).then_inc(s_exp, 1)
                        if b % 2 and k >= 3:
                            scale_slc(k - 3)
                        if u:
                            values_part(u - 1, b)
            scale_slc(8 * 4 * TILES - 2)
            for b in range(8):
                values_part(4 * TILES - 1, b)
            copy_out(4 * TILES - 1)

        @block.vector
        def _(dve):
            dve.wait_ge(s_const, 64)
            chain = Chain(dve, s_chain, 0)

            def bc(ap, n):
                return ap.rearrange("p (h a) -> p h a", a=1).to_broadcast([P, ap.shape[1], n])

            def copy_pt(m):
                dve.wait_ge(s_tr, m + 1)
                if m >= 4:
                    dve.wait_ge(s_pv, m - 3)
                rows = NBL if m in first_pt else P
                dve.tensor_copy(pt[m % 4][0:rows, :, :], t_ps[m % 2][0:rows, :, :]).then_inc(s_pt_dve, 1)

            def scale_win(k):
                u, b = divmod(k, 8)
                p = p_win[u % 2][:, b // 2, max(0, 2 - u // 4) * P:3 * P]
                dve.wait_ge(s_scale, k + 1)
                dve.tensor_scalar(p, p, scale[:, k % 8:k % 8 + 1], None, ALU.mult).then_inc(s_win_scaled, 1)

            def cmp_bias(i, g):
                n = cmp_step(i, g)
                dve.wait_ge(s_scores, n + 1)
                if i >= 2 and g == 0:
                    dve.wait_ge(s_tr, first_pt[4 * (i - 1)])
                hs = slice(4 * g, 4 * g + 4)
                dve.tensor_tensor(p_cmp[i % 2][:, hs, :], s_ps[n % 2][:, 0:4 * P].rearrange("p (r c) -> p r c", c=P)[:, :, 0:NBL],
                                  cmpb[:, hs, 56 - 8 * i:56 - 8 * i + NBL], ALU.add).then_inc(s_sread, 1)

            def cmp_max(i):
                pc = p_cmp[i % 2]
                dve.wait_ge(s_sread, cmp_step(i, 3) + 1)
                chain.step(dve.tensor_reduce(c_min[:, :], pc[:, :, :], AX.X, ALU.min))
                dve.tensor_tensor(pc[:, :, :], pc[:, :, :], bc(c_min[:, :], NBL), ALU.subtract).then_inc(s_cready, 1)

            def cmp_scale(i):
                pc = p_cmp[i % 2]
                dve.wait_ge(s_cexp, i + 1)
                chain.step(dve.tensor_reduce(c_rs[:, :], pc[:, :, :], AX.X, ALU.add))
                chain.step(dve.reciprocal(c_rs[:, :], c_rs[:, :]))
                if i == 0:
                    chain.step(dve.tensor_scalar(c_rs[:, :], c_rs[:, :], valid[:, 0:1], None, ALU.mult))
                if i >= 2:
                    chain.step(dve.tensor_tensor(shares[:, :, :], pc[:, :, :], bc(c_rs[:, :], NBL), ALU.mult))
                    dve.wait_ge(s_cscaled, i - 1)
                dve.tensor_tensor(c_scale[i % 2][:, :], c_rs[:, :],
                                  gates[:, i, :].rearrange("p (h b) -> p h b", b=3)[:, :, 0], ALU.mult).then_inc(s_cscale, 1)

            def select_blocks(i):
                chain.step(dve.tensor_reduce(group_p[:, :, :], shares[:, :, :].rearrange("p (g r) c -> p g c r", r=R), AX.X, ALU.add))
                fours = group_p[:, :, :].rearrange("p g (j c) -> p g j c", c=4)
                chain.step(dve.tensor_reduce(imp[:, :, :], fours[:, :, :, 0:3], AX.X, ALU.add))
                chain.step(dve.scalar_tensor_tensor(out=imp[:, :, :], in0=fours[:, :, :, 3], scalar=0.5, in1=imp[:, :, :],
                                                    op0=ALU.mult, op1=ALU.add))
                chain.step(dve.scalar_tensor_tensor(out=imp[:, :, 1:NSB], in0=fours[:, :, 0:NSB - 1, 3], scalar=0.5,
                                                    in1=imp[:, :, 1:NSB], op0=ALU.mult, op1=ALU.add))

                def per_group(row):
                    return consts[:, row:row + 1, :].to_broadcast([P, N_KV, NSB])

                chain.step(dve.tensor_tensor(imp[:, :, :], imp[:, :, :], per_group(i), ALU.add))
                chain.step(dve.tensor_reduce(top[:, :], imp[:, :, :], AX.X, ALU.max))
                chain.step(dve.tensor_tensor(pick[:, :, :], imp[:, :, :], bc(top[:, :], NSB), ALU.is_equal))
                chain.step(dve.tensor_tensor(pick[:, :, :], pick[:, :, :], per_group(2 * TILES), ALU.mult))
                chain.step(dve.tensor_reduce(top[:, :], pick[:, :, :], AX.X, ALU.max))
                chain.step(dve.tensor_tensor(pick[:, :, :], pick[:, :, :], bc(top[:, :], NSB), ALU.is_equal))
                chain.step(dve.tensor_tensor(pick[:, :, :], pick[:, :, :], per_group(TILES + i), ALU.add))
                dve.tensor_scalar(sel[i % 2][:, :, :], pick[:, :, :], 1.0, NEG, ALU.subtract, ALU.mult).then_inc(s_sel, 1)
                dve.wait_ge(s_sel, i - 1)

            def add_bias(u, b):
                i, g = divmod(u, 4)
                r, k, n = b // 2, 8 * u + b, unit_step(u, b)
                c = k % 8
                ps = s_ps[n % 2]
                dve.wait_ge(s_scores, n + 1)
                if u >= 2 and b == 0:
                    dve.wait_ge(s_tr, first_pt[u - 1])
                if k >= 8:
                    dve.wait_ge(s_exp, k - 7)
                h = 4 * g + r
                if b % 2 or i < 2:
                    if b % 2:
                        lo = max(0, 2 - i) * P
                        out, keys = p_win[u % 2][:, r, lo:3 * P], 3 * P - lo
                    else:
                        keys = (i + 1) * P
                        out = p_slc[u % 2][:, r, 0:keys]
                    dve.tensor_tensor_reduce(out, win[:, h, 3 * P - keys:3 * P], ps[:, 0:keys], 1.0, -LOWEST,
                                             ALU.add, ALU.min, neg_max[:, c:c + 1]).then_inc(s_sread, 1)
                else:
                    far = (i - 1) * P
                    out = p_slc[u % 2][:, r, :]
                    chain.step(dve.tensor_tensor_reduce(
                        out[:, 0:far].rearrange("p (b c) -> p b c", c=DH), bc(sel[i % 2][:, g, 0:2 * i - 2], DH),
                        ps[:, 0:far].rearrange("p (b c) -> p b c", c=DH), 1.0, -LOWEST, ALU.add, ALU.min, far_min[:, c:c + 1]))
                    m = (u - 8) * R + r
                    dve.wait_ge(s_near, m + 1)
                    dve.tensor_tensor_reduce(out[:, far:far + 2 * P], near[m % 2][:, :], ps[:, far:far + 2 * P], 1.0,
                                             far_min[:, c:c + 1], ALU.add, ALU.min, neg_max[:, c:c + 1]).then_inc(s_sread, 1)

            for g in range(N_KV):
                cmp_bias(0, g)
            cmp_max(0)
            cmp_scale(0)
            for i in range(TILES):
                for g in range(N_KV):
                    u = 4 * i + g
                    for b in range(8):
                        add_bias(u, b)
                        if b % 2 and 8 * u + b >= 3:
                            scale_win(8 * u + b - 2)
                        if i + 1 < TILES:
                            if g == 1 and b % 2:
                                cmp_bias(i + 1, b // 2)
                            if g == 1 and b == 7:
                                cmp_max(i + 1)
                            if g == 2 and b == 1:
                                cmp_scale(i + 1)
                            if g == 2 and b == 4 and i + 1 >= 2:
                                select_blocks(i + 1)
                        if u:
                            for m in part(u - 1, b):
                                if m % 2:
                                    copy_pt(m)
            scale_win(8 * 4 * TILES - 1)
            for b in range(8):
                for m in part(4 * TILES - 1, b):
                    if m % 2:
                        copy_pt(m)

        @block.tensor
        def _(pe):
            pe.wait_ge(s_const, 64)

            def free_scores(n):
                if n >= 2:
                    pe.wait_ge(s_sread, n - 1)

            def cmp_scores(i, g):
                n = cmp_step(i, g)
                free_scores(n)
                for r in range(R):
                    last = pe.matmul(s_ps[n % 2][:, r * P:(r + 1) * P], qt[i % 2][:, 4 * g + r, :].bitcast(F32), kct[:, g, :],
                                     start=True, stop=True)
                last.then_inc(s_scores, 1)

            def scores(u, b):
                i, g = divmod(u, 4)
                n = unit_step(u, b)
                free_scores(n)
                q = qt[i % 2][:, 4 * g + b // 2, :]
                t0 = max(0, i - 2) * P if b % 2 else 0
                for c0 in range(t0, (i + 1) * P, 512):
                    c1 = min(c0 + 512, (i + 1) * P)
                    for hl in range(2):
                        last = pe.matmul(s_ps[n % 2][:, c0 - t0:c1 - t0], q, kt[:, 4 * (b % 2) + g, hl, c0:c1],
                                         start=(hl == 0), stop=(hl == 1))
                last.then_inc(s_scores, 1)

            def of(m):
                u = max(x for x in range(4 * TILES) if first_pt[x] <= m)
                return u, key_tiles(u)[m - first_pt[u]]

            def transpose_p(m):
                u, (branch, col, t) = of(m)
                i, g = divmod(u, 4)
                if branch == "cmp":
                    pe.wait_ge(s_cscaled, i + 1)
                    pe.wait_ge(s_slc_scaled, 4 * u + 4)
                    pe.wait_ge(s_win_scaled, 4 * u + 4)
                if m >= 2:
                    pe.wait_ge(s_pt_dve if m % 2 else s_pt_act, m // 2)
                for r in range(R):
                    if branch == "cmp":
                        last = pe.transpose(t_ps[m % 2][0:NBL, r, :], p_cmp[i % 2][:, 4 * g + r, :], ident)
                    else:
                        p = (p_win if branch == "win" else p_slc)[u % 2]
                        last = pe.transpose(t_ps[m % 2][:, r, :], p[:, r, col:col + P], ident)
                last.then_inc(s_tr, 1)

            def values(m):
                u, (branch, col, t) = of(m)
                g = u % 4
                pe.wait_ge(s_pt_dve if m % 2 else s_pt_act, m // 2 + 1)
                start, stop = m == first_pt[u], m + 1 == first_pt[u + 1]
                if start and u >= 2:
                    pe.wait_ge(s_oevac, u - 1)
                rows = NBL if branch == "cmp" else P
                v = vc[:, g, :] if branch == "cmp" else (vw if branch == "win" else vs)[:, t, g * DH:(g + 1) * DH]
                for parity in range(2):
                    last = pe.matmul(o_ps[u % 2][parity * DH:(parity + 1) * DH, 0:2 * P].rearrange("p (a q) -> p a q", a=2), v,
                                     pt[m % 4][0:rows, parity:R:2, :], start=start, stop=stop)
                last.then_inc(s_pv, 1)

            def values_part(u, b):
                for m in part(u, b):
                    transpose_p(m)
                    if m >= 2:
                        values(m - 2)

            waiting = None
            for kind, x, y in order:
                if kind == "cmp":
                    if y == 0:
                        pe.wait_ge(s_qt[x % 2], 16 * (x // 2 + 1))
                    cmp_scores(x, y)
                else:
                    scores(x, y)
                if waiting:
                    values_part(*waiting)
                waiting = (x - 1, y) if kind == "unit" and x else None
            values_part(*waiting)
            for b in range(8):
                values_part(4 * TILES - 1, b)
            values(first_pt[-1] - 2)
            values(first_pt[-1] - 1)


def split_rows(nc, src, xt_hi, xt_lo):
    with ExitStack() as ctx:
        new_semaphore = ctx.enter_context(phase_semaphores(nc))

        raw = [ctx.enter_context(nc.sbuf_tensor(f"split_raw{s}", [P, SEQ], F32)) for s in range(4)]
        s_in = [new_semaphore(f"split_in{s}") for s in range(4)]
        s_hi, s_lo = (new_semaphore(f"split_{n}") for n in ("hi", "lo"))
        block = ctx.enter_context(nc.Block())

        @block.sync
        def _(sp):
            for k in range(KT):
                if k >= 4:
                    sp.wait_ge(s_lo, k - 3)
                sp.dma_start(raw[k % 4][:, :], src[:, k, :]).then_inc(s_in[k % 4], 16)

        @block.scalar
        def _(act):
            for k in range(KT):
                act.wait_ge(s_in[k % 4], 16 * (k // 4 + 1))
                act.copy(xt_hi[:, k, :], raw[k % 4][:, :]).then_inc(s_hi, 1)

        @block.vector
        def _(dve):
            for k in range(KT):
                dve.wait_ge(s_hi, k + 1)
                dve.tensor_tensor(xt_lo[:, k, :], raw[k % 4][:, :], xt_hi[:, k, :], ALU.subtract).then_inc(s_lo, 1)


def route(nc, logits, consts, before, token_ids, slots, weights, jobs, slot_tokens):
    E2 = 2 * N_EXP
    NR = MAX_JOBS + 1
    with ExitStack() as ctx:
        new_semaphore = ctx.enter_context(phase_semaphores(nc))

        def sb(n, shape, dt=F32):
            return ctx.enter_context(nc.sbuf_tensor(f"route_{n}", shape, dt))

        def sem(n):
            return new_semaphore(f"route_{n}")

        te = [P, TILES, N_EXP]
        con = sb("con", [P, ROUTE_CONSTS])
        lower, ones = sb("lower", [P, P]), sb("ones", [P, P])
        ids, zero = sb("ids", [P, TILES], I32), sb("zero", [P, SLOT_TILES], I32)
        rest, hit, tmp = sb("rest", te), sb("hit", te), sb("tmp", te)
        first, second, both = sb("first", te), sb("second", te), sb("both", te)
        top = [sb(f"top{s}", [P, TILES]) for s in range(2)]
        low, ratio = sb("low", [P, TILES]), sb("ratio", [P, TILES])
        ahead = sb("ahead", te)
        counts = sb("counts", te)
        total = sb("total", [P, N_EXP])
        cube = sb("cube", [P, N_EXP, N_EXP])
        tiles, base, odd = sb("tiles", [P, N_EXP]), sb("base", [P, N_EXP]), sb("odd", [P, N_EXP])
        slot_f = sb("slot_f", [P, 2, TILES])
        have, left, field = sb("have", [P, N_EXP, 2]), sb("left", [P, N_EXP, 2]), sb("field", [P, 3, N_EXP, 2])
        order, square = sb("order", [P, E2]), sb("square", [P, E2, E2])
        at, pick = sb("at", [P, NR, E2]), sb("pick", [P, NR, E2])
        records = sb("records", [P, 64])
        c_ps = ctx.enter_context(nc.psum_tensor("route_c", te, F32))
        r_ps = ctx.enter_context(nc.psum_tensor("route_r", te, F32))
        s_in, s_one, s_both, s_mm, s_chain, s_low, s_exp, s_slots, s_zero, s_zeroed, s_scatter, s_jobs = (
            sem(n) for n in ("in", "one", "both", "mm", "chain", "low", "exp", "slots", "zero", "zeroed", "scatter", "jobs"))
        block = ctx.enter_context(nc.Block())

        def const(name):
            a, n = ROUTE_AT[name]
            return con[:, a:a + n]

        @block.sync
        def _(sp):
            sp.dma_start(con[:, :], consts).then_inc(s_in, 16)
            sp.dma_start(lower[:, :], before).then_inc(s_in, 16)
            sp.dma_start(ids[:, :], token_ids).then_inc(s_in, 16)
            sp.wait_ge(s_zero, 1)
            sp.dma_start(slot_tokens.rearrange("(p s) a -> p (s a)", p=P), zero[:, :]).then_inc(s_zeroed, 16)

        @block.gpsimd
        def _(pool):
            pool.memset(zero[:, :], 0).then_inc(s_zero, 1)
            pool.memset(ones[:, :], 1.0).then_inc(s_one, 1)
            pool.wait_ge(s_zeroed, 16)
            pool.wait_ge(s_in, 48)
            pool.wait_ge(s_slots, 1)
            for i in range(TILES):
                for choice in range(2):
                    pool.indirect_dma_start(out=slot_tokens, out_offset=bass.IndirectOffsetOnAxis(ap=slots[:, choice, i:i + 1], axis=0),
                                            in_=ids[:, i:i + 1], in_offset=None).then_inc(s_scatter, 16)
            pool.wait_ge(s_scatter, 16 * 2 * TILES)

        @block.scalar
        def _(act):
            act.wait_ge(s_low, 1)
            act.activation(ratio[:, :], low[:, :], ACT.Exp).then_inc(s_exp, 1)

        @block.tensor
        def _(pe):
            pe.wait_ge(s_in, 48)
            pe.wait_ge(s_one, 1)
            pe.wait_ge(s_both, 1)
            pe.matmul(c_ps[:, :, :], ones[:, :], both[:, :, :], start=True, stop=True).then_inc(s_mm, 1)
            pe.matmul(r_ps[:, :, :], lower[:, :], both[:, :, :], start=True, stop=True).then_inc(s_mm, 1)

        @block.vector
        def _(dve):
            chain = Chain(dve, s_chain, 0)

            def do(out, a, b, op):
                chain.step(dve.tensor_tensor(out, a, b, op))

            def last(ap, n):
                return ap.rearrange("p (m a) -> p m a", a=1).to_broadcast([P, ap.shape[1], n])

            def mid(ap, n):
                return ap.rearrange("p (a m) -> p a m", a=1).to_broadcast([P, n, ap.shape[1]])

            def reduce(out, a, op=ALU.add):
                chain.step(dve.tensor_reduce(out, a, AX.X, op))

            def best(out, values, top):
                reduce(top, values, ALU.max)
                do(hit[:, :, :], values, last(top, N_EXP), ALU.is_equal)
                do(hit[:, :, :], hit[:, :, :], mid(const("down"), TILES), ALU.mult)
                reduce(low[:, :], hit[:, :, :], ALU.max)
                do(out, hit[:, :, :], last(low[:, :], N_EXP), ALU.is_equal)

            dve.wait_ge(s_in, 48)
            best(first[:, :, :], logits[:, :, :], top[0][:, :])
            chain.step(dve.scalar_tensor_tensor(out=rest[:, :, :], in0=first[:, :, :], scalar=LOWEST, in1=logits[:, :, :],
                                                op0=ALU.mult, op1=ALU.add))
            best(second[:, :, :], rest[:, :, :], top[1][:, :])
            dve.tensor_tensor(both[:, :, :], first[:, :, :], second[:, :, :], ALU.add).then_inc(s_both, 1)
            dve.tensor_tensor(low[:, :], top[1][:, :], top[0][:, :], ALU.subtract).then_inc(s_low, 1)
            dve.wait_ge(s_exp, 1)
            chain.step(dve.tensor_scalar(low[:, :], ratio[:, :], 1.0, None, ALU.add))
            chain.step(dve.reciprocal(weights[:, 0, :], low[:, :]))
            do(weights[:, 1, :], weights[:, 0, :], ratio[:, :], ALU.mult)

            dve.wait_ge(s_mm, 2)
            chain.step(dve.tensor_copy(counts[:, :, :], c_ps[:, :, :]))
            chain.step(dve.memset(ahead[:, 0, :], 0.0))
            for i in range(1, TILES):
                do(ahead[:, i, :], ahead[:, i - 1, :], counts[:, i - 1, :], ALU.add)
            do(total[:, :], ahead[:, TILES - 1, :], counts[:, TILES - 1, :], ALU.add)
            do(ahead[:, :, :], r_ps[:, :, :], ahead[:, :, :], ALU.add)

            do(cube[:, :, :], last(total[:, :], TILES), mid(const("starts"), N_EXP), ALU.is_gt)
            reduce(tiles[:, :], cube[:, :, :])
            chain.step(dve.tensor_scalar(odd[:, :], tiles[:, :], 1.0, None, ALU.is_equal))
            chain.step(dve.scalar_tensor_tensor(out=odd[:, :], in0=tiles[:, :], scalar=CAP + 1.0, in1=odd[:, :],
                                                op0=ALU.is_equal, op1=ALU.add))
            do(tiles[:, :], tiles[:, :], odd[:, :], ALU.add)
            prior = const("prior").rearrange("p (a b) -> p a b", b=E2)
            do(cube[:, :, :], mid(tiles[:, :], N_EXP), prior[:, 0:N_EXP, 0:N_EXP], ALU.mult)
            reduce(base[:, :], cube[:, :, :])

            chain.step(dve.scalar_tensor_tensor(out=ahead[:, :, :], in0=mid(base[:, :], TILES), scalar=float(P), in1=ahead[:, :, :],
                                                op0=ALU.mult, op1=ALU.add))
            for choice, hot in enumerate((first, second)):
                do(tmp[:, :, :], hot[:, :, :], ahead[:, :, :], ALU.mult)
                reduce(slot_f[:, choice, :], tmp[:, :, :])
            dve.tensor_copy(slots[:, :, :], slot_f[:, :, :]).then_inc(s_slots, 1)

            do(left[:, :, :], last(tiles[:, :], 2), const("skip").rearrange("p (e c) -> p e c", c=2), ALU.subtract)
            chain.step(dve.tensor_scalar(have[:, :, :], left[:, :, :], 0.0, None, ALU.is_gt))
            do(square[:, :, :], mid(have[:, :, :].rearrange("p e c -> p (e c)"), E2), prior, ALU.mult)
            reduce(order[:, :], square[:, :, :])
            do(at[:, :, :], mid(order[:, :], NR), last(const("record"), E2), ALU.is_equal)
            do(at[:, :, :], at[:, :, :], mid(have[:, :, :].rearrange("p e c -> p (e c)"), NR), ALU.mult)
            chain.step(dve.tensor_copy(field[:, 0, :, :], const("expert").rearrange("p (e c) -> p e c", c=2)))
            do(field[:, 1, :, :], last(base[:, :], 2), const("skip").rearrange("p (e c) -> p e c", c=2), ALU.add)
            chain.step(dve.tensor_scalar(field[:, 2, :, :], left[:, :, :], float(CAP), None, ALU.min))
            chain.step(dve.memset(records[:, :], 0.0))
            for f in range(3):
                do(pick[:, :, :], at[:, :, :], mid(field[:, f, :, :].rearrange("p e c -> p (e c)"), NR), ALU.mult)
                reduce(records[:, f:f + E_REC * (NR - 1) + 1:E_REC], pick[:, :, :])
            reduce(records[:, JOB_COUNT_AT:JOB_COUNT_AT + 1], have[:, :, :].rearrange("p e c -> p (e c)"))
            dve.tensor_copy(jobs[0:1, :], records[0:1, :]).then_inc(s_jobs, 1)


def combine(nc, x, y, slots, weights, out):
    with ExitStack() as ctx:
        new_semaphore = ctx.enter_context(phase_semaphores(nc))

        S = 3
        xt, y1, y2 = ([ctx.enter_context(nc.sbuf_tensor(f"comb_{n}{s}", [P, D], F32)) for s in range(S)] for n in ("x", "y1", "y2"))
        s_x = [new_semaphore(f"comb_x{s}") for s in range(S)]
        s_y = [new_semaphore(f"comb_y{s}") for s in range(S)]
        s_out = [new_semaphore(f"comb_out{s}") for s in range(S)]
        s_sum = new_semaphore("comb_sum")
        block = ctx.enter_context(nc.Block())

        @block.sync
        def _(sp):
            for i in range(TILES):
                s = i % S
                if i >= S:
                    sp.wait_ge(s_out[s], 16 * (i // S))
                sp.dma_start(xt[s][:, :], x[i * P:(i + 1) * P, :]).then_inc(s_x[s], 16)

        @block.gpsimd
        def _(pool):
            for i in range(TILES):
                s = i % S
                if i >= S:
                    pool.wait_ge(s_sum, 2 * (i - S) + 2)
                for choice, yt in enumerate((y1, y2)):
                    pool.indirect_dma_start(out=yt[s][:, :], out_offset=None, in_=y,
                                            in_offset=bass.IndirectOffsetOnAxis(ap=slots[:, choice, i:i + 1], axis=0)
                                            ).then_inc(s_y[s], 16)

        @block.vector
        def _(dve):
            for i in range(TILES):
                s = i % S
                dve.wait_ge(s_x[s], 16 * (i // S + 1))
                dve.wait_ge(s_y[s], 32 * (i // S + 1))
                for choice, yt in enumerate((y1, y2)):
                    dve.scalar_tensor_tensor(out=xt[s][:, :], in0=yt[s][:, :], scalar=weights[:, choice, i:i + 1], in1=xt[s][:, :],
                                             op0=ALU.mult, op1=ALU.add).then_inc(s_sum, 1)
                    dve.wait_ge(s_sum, 2 * i + choice + 1)

        @block.scalar
        def _(act):
            for i in range(TILES):
                s = i % S
                act.wait_ge(s_sum, 2 * i + 2)
                act.dma_start(out[i * P:(i + 1) * P, :], xt[s][:, :]).then_inc(s_out[s], 16)
            for s in range(S):
                act.wait_ge(s_out[s], 16 * len(range(s, TILES, S)))


def trunk(nc, x, onehot, rel_bias, gain_mix0, gain_ffn0, gain_ffn1, pool_w, pool_scale, chunk_gains, w_kvq, k_gains,
          cmp_pos, cmp_w1, cmp_w2, w_o, ffn_wgu, ffn_wd, router, moe_wgu, moe_wd, bands, identity, win_mask,
          sel_const, row_valid, route_const, before, token_ids, ffn_jobs, out):
    def dram(name, shape, dt=F32):
        return nc.dram_tensor(name, shape, dt, kind="Internal").ap()

    x_mid, h_ffn, y_ffn, x1 = (dram(n, [SEQ, D]) for n in ("x_mid", "h_ffn", "y_ffn", "x1"))
    qkv = dram("qkv", [SEQ, 6 * 512])
    qt_dram = dram("qt", [SEQ, N_HEADS * P])
    bias_vec = dram("bias_vec_rows", [N_HEADS, VEC])
    ot_dram = dram("ot_rows", [P, KT, SEQ])
    att_out, x2, h_moe = (dram(n, [SEQ, D]) for n in ("att_out", "x2", "h_moe"))
    slot_tokens = dram("slot_tokens", [SLOT_TILES * P, 1], I32)
    y_moe = dram("y_moe", [SLOT_TILES * P, D])

    with ExitStack() as whole:
        def sb(stack, name, shape, dt=F32):
            return stack.enter_context(nc.sbuf_tensor(name, shape, dt))

        ident_t = sb(whole, "ident", [P, P])
        ident = ident_t[:, :]
        dense_jobs = sb(whole, "dense_jobs", [1, 64], I32)
        zeros = sb(whole, "zeros", [P, D // 4])
        s_zeros, s_y_zeroed = nc.alloc_semaphore("zeros"), nc.alloc_semaphore("y_zeroed")
        k_gain_dram = dram("k_gain_dram", [1, (2 * N_KV + 1) * DH])
        with ExitStack() as first:
            gk, gq = (sb(first, n, [1, (2 * N_KV + 1) * DH]) for n in ("gk", "gq"))
            s_ident, s_gains, s_product = (nc.alloc_semaphore(n) for n in ("ident_loaded", "gains_loaded", "gains_product"))
            with nc.Block() as block:
                @block.sync
                def _(sp):
                    sp.dma_start(gk[:, :], k_gains[0:1, :]).then_inc(s_gains, 16)
                    sp.dma_start(gq[:, :], k_gains[1:2, :]).then_inc(s_gains, 16)
                    sp.dma_start(ident, identity).then_inc(s_ident, 16)
                    sp.dma_start(dense_jobs[:, :], ffn_jobs).then_inc(s_ident, 16)
                    sp.wait_ge(s_product, 1)
                    sp.dma_start(k_gain_dram, gk[:, :]).then_inc(s_ident, 16)
                    sp.wait_ge(s_ident, 48)

                @block.gpsimd
                def _(pool):
                    pool.memset(zeros[:, :], 0.0).then_inc(s_zeros, 1)
                    pool.wait_ge(s_zeros, 1)

                @block.vector
                def _(dve):
                    dve.wait_ge(s_gains, 32)
                    dve.scalar_tensor_tensor(out=gk[:, :], in0=gk[:, :], scalar=-(DH ** -0.5), in1=gq[:, :],
                                             op0=ALU.mult, op1=ALU.mult).then_inc(s_product, 1)

        def zero_rows(sp, u):
            sp.dma_start(y_moe.rearrange("(p s) (a d) -> p s a d", p=P, a=4)[:, u, :, :],
                         zeros[:, :].rearrange("p (a d) -> p a d", a=1).to_broadcast([P, 4, D // 4])).then_inc(s_y_zeroed, 16)

        bias_vectors(nc, rel_bias, onehot, bias_vec)

        pool_mixer(nc, x, gain_mix0, gain_ffn0, pool_scale, pool_w, bands, x_mid, h_ffn)

        def dense_rows(pool, j, base, stage, ids, s_ids, s_rows):
            for t in range(CAP):
                pool.dma_start(stage[:, t, :], h_ffn[bass.ds((base + t) * P, P), :]).then_inc(s_rows, 16)
        swiglu_jobs(nc, "ffn", ffn_wgu, ffn_wd, dense_jobs, SEQ // (CAP * P), dense_rows,
                    y_ffn.rearrange("(s p) d -> p s d", p=P), ident, (CAP,))

        with ExitStack() as att:
            win = sb(att, "win", [P, N_HEADS, 3 * P])
            cmpb = sb(att, "cmpb", [P, N_HEADS, CB])
            with ExitStack() as proj:
                xt_hi, xt_lo = (sb(proj, f"xt_{n}", [P, KT, SEQ], F32R) for n in ("hi", "lo"))
                add_norm(nc, "kvn", x_mid, y_ffn, None, x1, None, ident, xt_hi, xt_lo)
                project(nc, "kvq", xt_hi, xt_lo, w_kvq, chunk_gains, 6, qkv, last_cols=256,
                        side_loads=lambda sp, c, done: bias_tables(sp, c, 6, bias_vec, win, win_mask, cmpb, done))
            kt = sb(att, "kt", [P, 2 * N_KV, 2, SEQ], F32R)
            gates = sb(att, "gates", [P, TILES, 3 * N_HEADS])
            kct = sb(att, "kct", [P, N_KV, P])
            vc = sb(att, "vc", [P // 2, N_KV, DH])
            split_heads(nc, qkv, k_gain_dram[:, 0:2 * N_KV * DH], ident, kt, qt_dram, gates)
            compress_keys(nc, qkv, cmp_pos, cmp_w1, cmp_w2, k_gain_dram[:, 2 * N_KV * DH:(2 * N_KV + 1) * DH], ident, kct, vc)
            attend(nc, qkv, qt_dram, kt, kct, vc, gates, win, cmpb, sel_const, row_valid, ident, ot_dram, zero_rows)

        with ExitStack() as proj:
            xt_hi, xt_lo = (sb(proj, f"ot_{n}", [P, KT, SEQ], F32R) for n in ("hi", "lo"))
            split_rows(nc, ot_dram, xt_hi, xt_lo)
            project(nc, "wo", xt_hi, xt_lo, w_o, None, 2, att_out)

        logits = sb(whole, "logits", [P, TILES, N_EXP])
        slots = sb(whole, "slots", [P, 2, TILES], U32)
        weights = sb(whole, "weights", [P, 2, TILES])
        jobs = sb(whole, "jobs", [1, 64], I32)
        add_norm(nc, "moen", x1, att_out, gain_ffn1, x2, h_moe, ident, router=router, logits=logits)
        route(nc, logits, route_const, before, token_ids, slots, weights, jobs, slot_tokens)

        def expert_rows(pool, j, base, stage, ids, s_ids, s_rows):
            with nc.allow_non_contiguous_dma(reason="one token number a partition and tile"):
                pool.dma_start(ids[:, :], slot_tokens.rearrange("(s p) a -> p (s a)", p=P)[:, bass.ds(base, CAP)].bitcast(U32)
                               ).then_inc(s_ids, 16)
            pool.wait_ge(s_ids, j * 16 + 16)
            pool.sem_inc(s_ids_seen, 1)
            for t in range(CAP):
                pool.indirect_dma_start(out=stage[:, t, :], out_offset=None, in_=h_moe,
                                        in_offset=bass.IndirectOffsetOnAxis(ap=ids[:, t:t + 1], axis=0)).then_inc(s_rows, 16)
        s_ids_seen = nc.alloc_semaphore("ids_seen")
        with nc.Block() as block:
            @block.sync
            def _(sp):
                sp.wait_ge(s_y_zeroed, 16 * SLOT_TILES)
        swiglu_jobs(nc, "moe", moe_wgu, moe_wd, jobs, jobs[0:1, JOB_COUNT_AT:JOB_COUNT_AT + 1], expert_rows,
                    y_moe.rearrange("(s p) d -> p s d", p=P), ident, (2, 3, CAP))
        combine(nc, x2, y_moe, slots, weights, out)


_INS = ["x", "onehot", "rel_bias", "gain_mix0", "gain_ffn0", "gain_ffn1", "pool_w", "pool_scale", "chunk_gains", "w_kvq",
        "k_gains", "cmp_pos", "cmp_w1", "cmp_w2", "w_o", "ffn_wgu", "ffn_wd", "router", "moe_wgu", "moe_wd", "bands",
        "identity", "win_mask", "sel_const", "row_valid", "route_const", "before", "token_ids", "ffn_jobs"]


def rel_bucket(dist):
    import math
    import numpy as np
    n = np.maximum(dist, 0)
    exact = N_BUCKETS // 2
    nf = np.maximum(n, 1).astype(np.float32)
    large = exact + (np.log(nf / np.float32(exact)) / np.float32(math.log(128 / exact)) * np.float32(N_BUCKETS - exact)).astype(np.int32)
    return np.where(n < exact, n, np.minimum(large, N_BUCKETS - 1))


def shape_constants():
    import numpy as np
    f = np.float32
    hot = np.zeros((N_BUCKETS + 1, VEC), f)

    def put(first, dist):
        last = N_BUCKETS - 1
        for c, (d, b) in enumerate(zip(dist, rel_bucket(dist))):
            if d < 0:
                hot[N_BUCKETS, first + c] = 1
            elif b != last:
                hot[b, first + c], hot[last, first + c] = -1, 1
    put(0, 255 - np.arange(3 * P - 1))
    for r in range(16):
        put(NEAR + r * P, r - 16 * (np.arange(P - 1) - 63) - 31)
    s, t = np.arange(P)[:, None], np.arange(P)[None, :]
    bands = np.zeros((P, 3, N_GRP, P), f)
    for g, w in enumerate((2, 4, 8, 16)):
        inside = (t - s >= 0) & (t - s < w)
        bands[:, 0, g] = inside / np.minimum(t + 1, w).astype(f) - (s == t)
        bands[:, 1, g] = inside / f(w) - (s == t)
        bands[:, 2, g] = (t + P - s < w) / f(w)
    nsb = SEQ // 64
    sel = np.zeros((P, 2 * TILES + 1, nsb), f)
    blk = np.arange(nsb)[None, :]
    for i in range(TILES):
        own = 2 * i + np.arange(P)[:, None] // 64
        sel[:, i] = np.where((blk >= 1) & (blk <= own - 2), 0, -8)
        sel[:, TILES + i] = (blk == 0) | (blk == own) | (blk == own - 1)
    sel[:, 2 * TILES] = nsb - np.arange(nsb)
    e2 = 2 * N_EXP
    route = {
        "down": N_EXP - np.arange(N_EXP), "starts": P * np.arange(TILES),
        "prior": (np.arange(e2)[None, :] < np.arange(e2)[:, None]).ravel(),
        "record": np.arange(MAX_JOBS + 1), "expert": np.repeat(np.arange(N_EXP), 2), "skip": np.tile([0, CAP], N_EXP),
    }
    rc = np.zeros((P, ROUTE_CONSTS), f)
    for name, (a, n) in ROUTE_AT.items():
        rc[:, a:a + n] = route[name]
    jobs = np.zeros((1, 64), np.int32)
    for j in range(SEQ // (CAP * P)):
        jobs[0, E_REC * j:E_REC * j + 3] = (0, j * CAP, CAP)
    return {
        "onehot": hot, "bands": bands, "identity": np.eye(P, dtype=f), "win_mask": np.where(t > s, 0, -NEG).astype(f),
        "sel_const": sel, "row_valid": (np.arange(P) >= 31).astype(f).reshape(P, 1), "route_const": rc,
        "before": (s < t).astype(f), "token_ids": (np.arange(TILES)[None, :] * P + np.arange(P)[:, None]).astype(np.int32),
        "ffn_jobs": jobs,
    }


def kernel(x, rel_bias, norm_mix, norm_ffn, pool_w, pool_scale, norm_kv, w_kv, g_k, cmp_pos, cmp_w1, cmp_w2, w_qg, g_q,
           w_o, ffn_wg, ffn_wu, ffn_wd, router, moe_wg, moe_wu, moe_wd):
    import numpy as np
    import concourse.bacc as bacc
    from concourse.bass_utils import run_bass_kernel_spmd

    def chunked(w):
        n = w.shape[1] // 512
        return w.reshape(KT, P, n, 512).transpose(2, 1, 0, 3).reshape(n * P, KT * 512)

    def gate_up(wg, wu):
        w = np.stack([wg, wu], 1).reshape(-1, 2, KT, P, MT, P)
        return w.transpose(0, 4, 3, 1, 2, 5).reshape(-1, 2 * D)

    a = {k: np.asarray(v) for k, v in dict(
        x=x, rel_bias=rel_bias, norm_mix=norm_mix, norm_ffn=norm_ffn, pool_w=pool_w, pool_scale=pool_scale, norm_kv=norm_kv,
        w_kv=w_kv, g_k=g_k, cmp_pos=cmp_pos, cmp_w1=cmp_w1, cmp_w2=cmp_w2, w_qg=w_qg, g_q=g_q, w_o=w_o, ffn_wg=ffn_wg,
        ffn_wu=ffn_wu, ffn_wd=ffn_wd, router=router, moe_wg=moe_wg, moe_wu=moe_wu, moe_wd=moe_wd).items()}
    w_all = np.concatenate([a["w_kv"], a["w_qg"][0], np.zeros((D, 6 * 512 - 1536 - 1072), np.float32)], 1)
    gains = np.stack([a["norm_kv"]] * 3 + [a["norm_mix"][1]] * 3)
    arrays = {
        "x": a["x"].reshape(SEQ, D), "rel_bias": a["rel_bias"], "gain_mix0": a["norm_mix"][0:1], "gain_ffn0": a["norm_ffn"][0:1],
        "gain_ffn1": a["norm_ffn"][1:2], "pool_w": a["pool_w"][0], "pool_scale": a["pool_scale"][0:1],
        "chunk_gains": gains.reshape(6, KT, P).transpose(2, 0, 1), "w_kvq": chunked(w_all),
        "k_gains": np.stack([np.concatenate([a["g_k"][1]] * N_KV + [a["g_k"][2]] * N_KV + [a["g_k"][0]]),
                             np.concatenate([a["g_q"][0]] * (2 * N_KV + 1))]),
        "cmp_pos": a["cmp_pos"].reshape(2, 16, P).transpose(2, 0, 1), "cmp_w1": a["cmp_w1"], "cmp_w2": a["cmp_w2"],
        "w_o": chunked(a["w_o"][0]), "ffn_wgu": gate_up(a["ffn_wg"], a["ffn_wu"]), "ffn_wd": a["ffn_wd"].reshape(-1, D),
        "router": a["router"][0], "moe_wgu": gate_up(a["moe_wg"][0], a["moe_wu"][0]), "moe_wd": a["moe_wd"].reshape(-1, D),
        **shape_constants(),
    }
    nc = bacc.Bacc("TRN2", target_bir_lowering=False, num_devices=1)
    ins, args = {}, []
    for name in _INS:
        v = np.ascontiguousarray(arrays[name])
        ins[f"in_{name}"] = v
        args.append(nc.dram_tensor(f"in_{name}", v.shape, mybir.dt.from_np(v.dtype), kind="ExternalInput").ap())
    out = nc.dram_tensor("out_x", [SEQ, D], F32, kind="ExternalOutput").ap()
    trunk(nc, *args, out)
    r = run_bass_kernel_spmd(nc, [ins], core_ids=[0])
    return r.results[0]["out_x"].reshape(1, SEQ, D)
```
